# Optimizing a Trainium2 kernel written in Bass

```python
import jax, jax.numpy as jnp
from jax import lax
import numpy as np
import math
import jax
import jax.numpy as jnp

D_MODEL = 1024
BATCH = 1
SEQ = 512
DEPTH = 2

HEAD_DIM = 64
ATTN_HEADS = 8
ATTN_KV_HEADS = 2
ATTN_GROUP = ATTN_HEADS // ATTN_KV_HEADS
WINDOW = 128
ATTN_BLOCK = 128
ROPE_THETA = 10000.0

RET_HEADS = 4
RET_DK = 64
RET_DV = 64
RET_CHUNK = 128

GLA_HEADS = 4
GLA_DK = 32
GLA_DV = 64
GLA_CHUNK = 64
GLA_GATE_RANK = 16
GLA_GATE_NORMALIZER = 16.0

EPS = 1e-6

ATTN_W = ATTN_HEADS * HEAD_DIM
RET_W = RET_HEADS * RET_DV
GLA_W = GLA_HEADS * GLA_DV
D_MIX = ATTN_W + RET_W + GLA_W

IN_SIZES = (
    ATTN_HEADS * HEAD_DIM, ATTN_KV_HEADS * HEAD_DIM, ATTN_KV_HEADS * HEAD_DIM, ATTN_W,
    RET_HEADS * RET_DK, RET_HEADS * RET_DK, RET_HEADS * RET_DV, RET_W,
    GLA_HEADS * GLA_DK, GLA_HEADS * GLA_DK, GLA_HEADS * GLA_DV, GLA_W,
    GLA_GATE_RANK,
)
D_IN = sum(IN_SIZES)
IN_SPLITS = [int(s) for s in np.cumsum(IN_SIZES)[:-1]]


def rms_norm(x, gain=None):
    xf = x.astype(jnp.float32)
    y = xf * lax.rsqrt(jnp.mean(xf * xf, axis=-1, keepdims=True) + EPS)
    if gain is not None:
        y = y * gain.astype(jnp.float32)
    return y.astype(x.dtype)

def apply_rotary(x, positions, inv_freq):
    ang = positions.astype(jnp.float32)[..., None] * inv_freq
    cos = jnp.cos(ang)[:, :, None, :]
    sin = jnp.sin(ang)[:, :, None, :]
    x1, x2 = jnp.split(x.astype(jnp.float32), 2, axis=-1)
    out = jnp.concatenate([x1 * cos - x2 * sin, x2 * cos + x1 * sin], axis=-1)
    return out.astype(x.dtype)

def sliding_window_attention(q, k, v, sinks):
    B, S, H, D = q.shape
    nb = S // ATTN_BLOCK
    qb = q.reshape(B, nb, ATTN_BLOCK, ATTN_KV_HEADS, ATTN_GROUP, D)
    kb = k.reshape(B, nb, ATTN_BLOCK, ATTN_KV_HEADS, D)
    vb = v.reshape(B, nb, ATTN_BLOCK, ATTN_KV_HEADS, D)

    def with_prev(t):
        prev = jnp.pad(t, ((0, 0), (1, 0), (0, 0), (0, 0), (0, 0)))[:, :-1]
        return jnp.concatenate([prev, t], axis=2)

    kk, vv = with_prev(kb), with_prev(vb)
    s = jnp.einsum('bnqhgd,bnkhd->bnhgqk', qb, kk).astype(jnp.float32) * (D ** -0.5)
    i = jnp.arange(ATTN_BLOCK)[:, None]
    j = jnp.arange(2 * ATTN_BLOCK)[None, :]
    rel = i + ATTN_BLOCK - j
    kpos = (jnp.arange(nb)[:, None] - 1) * ATTN_BLOCK + jnp.arange(2 * ATTN_BLOCK)[None, :]
    valid = ((rel >= 0) & (rel < WINDOW))[None] & (kpos >= 0)[:, None, :]
    s = jnp.where(valid[None, :, None, None], s, -1e30)
    sink = sinks.astype(jnp.float32).reshape(ATTN_KV_HEADS, ATTN_GROUP)[None, None, :, :, None, None]
    sink = jnp.broadcast_to(sink, s.shape[:-1] + (1,))
    p = jax.nn.softmax(jnp.concatenate([s, sink], axis=-1), axis=-1)[..., :-1]
    o = jnp.einsum('bnhgqk,bnkhd->bnqhgd', p.astype(v.dtype), vv)
    return o.reshape(B, S, H * D)

def retention(q, k, v):
    B, S, H, Dk = q.shape
    Dv = v.shape[-1]
    C = RET_CHUNK
    nc = S // C
    f32 = jnp.float32
    log_g = jnp.log(1.0 - 2.0 ** (-5.0 - jnp.arange(H, dtype=f32)))
    idx = jnp.arange(C, dtype=f32)
    diff = idx[:, None] - idx[None, :]
    dmask = jnp.where(diff >= 0, jnp.exp(log_g[:, None, None] * jnp.maximum(diff, 0.0)), 0.0)
    q_decay = jnp.exp(log_g[:, None] * (idx + 1.0))[..., None]
    k_decay = jnp.exp(log_g[:, None] * (C - 1.0 - idx))[..., None]
    chunk_decay = jnp.exp(log_g * C)[:, None, None]

    def to_chunks(t):
        return t.astype(f32).reshape(B, nc, C, H, t.shape[-1]).transpose(1, 0, 3, 2, 4)

    qc, kc, vc = to_chunks(q), to_chunks(k * (Dk ** -0.5)), to_chunks(v)

    def step(state, inp):
        qi, ki, vi = inp
        sc = jnp.einsum('bhid,bhjd->bhij', qi, ki) * dmask
        intra = jnp.einsum('bhij,bhjv->bhiv', sc, vi)
        inter = jnp.einsum('bhid,bhdv->bhiv', qi * q_decay, state)
        new_state = chunk_decay * state + jnp.einsum('bhjd,bhjv->bhdv', ki * k_decay, vi)
        return new_state, intra + inter

    state0 = jnp.zeros((B, H, Dk, Dv), f32)
    _, out = lax.scan(step, state0, (qc, kc, vc))
    return out.transpose(1, 0, 3, 2, 4).reshape(B, S, H, Dv).astype(v.dtype)

def gated_linear_attention(q, k, v, log_a):
    B, S, H, Dk = q.shape
    Dv = v.shape[-1]
    C = GLA_CHUNK
    nc = S // C
    f32 = jnp.float32

    def to_chunks(t):
        return t.astype(f32).reshape(B, nc, C, H, t.shape[-1]).transpose(1, 0, 3, 2, 4)

    qc, kc, vc, gc = to_chunks(q * (Dk ** -0.5)), to_chunks(k), to_chunks(v), to_chunks(log_a)
    causal = jnp.tril(jnp.ones((C, C), dtype=bool))[..., None]

    def step(state, inp):
        qi, ki, vi, gi = inp
        b = jnp.cumsum(gi, axis=2)
        rel = b[:, :, :, None, :] - b[:, :, None, :, :]
        decay = jnp.where(causal, jnp.exp(jnp.minimum(rel, 0.0)), 0.0)
        sc = jnp.einsum('bhid,bhijd,bhjd->bhij', qi, decay, ki)
        intra = jnp.einsum('bhij,bhjv->bhiv', sc, vi)
        inter = jnp.einsum('bhid,bhdv->bhiv', qi * jnp.exp(b), state)
        b_last = b[:, :, -1:, :]
        new_state = (jnp.exp(b_last)[:, :, 0, :, None] * state
                     + jnp.einsum('bhjd,bhjv->bhdv', ki * jnp.exp(b_last - b), vi))
        return new_state, intra + inter

    state0 = jnp.zeros((B, H, Dk, Dv), f32)
    _, out = lax.scan(step, state0, (qc, kc, vc, gc))
    return out.transpose(1, 0, 3, 2, 4).reshape(B, S, H, Dv).astype(v.dtype)

def hybrid_layer(x, c_act, positions, w_mod, b_mod, pre_gain, post_gain, w_in, sinks,
                 gla_gate_w, gla_gate_b, gla_norm_gain, w_out):
    B, S, _ = x.shape
    mod = c_act @ w_mod + b_mod
    shift, scale, gate = jnp.split(mod[:, None, :], 3, axis=-1)
    h = rms_norm(x, pre_gain) * (1.0 + scale) + shift
    proj = h @ w_in
    (aq, ak, av, ag, rq, rk, rv, rg, gq, gk, gv, gg, ga) = jnp.split(proj, IN_SPLITS, axis=-1)

    rope_freq = ROPE_THETA ** (-jnp.arange(0, HEAD_DIM, 2, dtype=jnp.float32) / HEAD_DIM)
    aq = apply_rotary(aq.reshape(B, S, ATTN_HEADS, HEAD_DIM), positions, rope_freq)
    ak = apply_rotary(ak.reshape(B, S, ATTN_KV_HEADS, HEAD_DIM), positions, rope_freq)
    av = av.reshape(B, S, ATTN_KV_HEADS, HEAD_DIM)
    a_out = sliding_window_attention(aq, ak, av, sinks) * jax.nn.silu(ag)

    ret_freq = 1.0 / (10000.0 ** jnp.linspace(0.0, 1.0, RET_DK // 2, dtype=jnp.float32))
    rq = apply_rotary(rq.reshape(B, S, RET_HEADS, RET_DK), positions, ret_freq)
    rk = apply_rotary(rk.reshape(B, S, RET_HEADS, RET_DK), positions, ret_freq)
    r = retention(rq, rk, rv.reshape(B, S, RET_HEADS, RET_DV))
    r_out = rms_norm(r).reshape(B, S, RET_W) * jax.nn.silu(rg)

    gate_logits = (ga @ gla_gate_w + gla_gate_b).astype(jnp.float32)
    log_a = (jax.nn.log_sigmoid(gate_logits) / GLA_GATE_NORMALIZER).reshape(B, S, GLA_HEADS, GLA_DK)
    g = gated_linear_attention(gq.reshape(B, S, GLA_HEADS, GLA_DK), gk.reshape(B, S, GLA_HEADS, GLA_DK),
                               gv.reshape(B, S, GLA_HEADS, GLA_DV), log_a)
    g_out = rms_norm(g, gla_norm_gain).reshape(B, S, GLA_W) * jax.nn.silu(gg)

    y = jnp.concatenate([a_out, r_out, g_out], axis=-1) @ w_out
    return x + gate * rms_norm(y, post_gain)

def first_inputs(seed: int = 0) -> dict:
    key = jax.random.key(seed)
    ks = jax.random.split(key, 16)
    f32 = jnp.float32
    x = jax.random.normal(ks[0], (BATCH, SEQ, D_MODEL), f32)
    c = jax.random.normal(ks[1], (BATCH, D_MODEL), f32)
    positions = jnp.broadcast_to(jnp.arange(SEQ, dtype=jnp.int32)[None, :], (BATCH, SEQ))
    w_mod = jax.random.normal(ks[2], (DEPTH, D_MODEL, 3 * D_MODEL), f32) * (0.5 * D_MODEL ** -0.5)
    b_mod = jax.random.normal(ks[3], (DEPTH, 3 * D_MODEL), f32) * 0.01
    pre_norm_gain = 1.0 + 0.02 * jax.random.normal(ks[4], (DEPTH, D_MODEL), f32)
    post_norm_gain = 1.0 + 0.02 * jax.random.normal(ks[5], (DEPTH, D_MODEL), f32)
    w_in = jax.random.normal(ks[6], (DEPTH, D_MODEL, D_IN), f32) * (D_MODEL ** -0.5)
    attn_sinks = 0.5 * jax.random.normal(ks[7], (DEPTH, ATTN_HEADS), f32)
    gla_gate_w = jax.random.normal(ks[8], (DEPTH, GLA_GATE_RANK, GLA_HEADS * GLA_DK), f32) * (GLA_GATE_RANK ** -0.5)
    gla_gate_b = 0.01 * jax.random.normal(ks[9], (DEPTH, GLA_HEADS * GLA_DK), f32)
    gla_norm_gain = 1.0 + 0.02 * jax.random.normal(ks[10], (DEPTH, GLA_DV), f32)
    w_out = jax.random.normal(ks[11], (DEPTH, D_MIX, D_MODEL), f32) * (D_MIX ** -0.5)
    return {"x": x, "c": c, "positions": positions, "w_mod": w_mod, "b_mod": b_mod,
            "pre_norm_gain": pre_norm_gain, "post_norm_gain": post_norm_gain, "w_in": w_in,
            "attn_sinks": attn_sinks, "gla_gate_w": gla_gate_w, "gla_gate_b": gla_gate_b,
            "gla_norm_gain": gla_norm_gain, "w_out": w_out}

def first_block(x, c, positions, w_mod, b_mod, pre_norm_gain, post_norm_gain, w_in,
              attn_sinks, gla_gate_w, gla_gate_b, gla_norm_gain, w_out):
    c_act = jax.nn.silu(c)
    for l in range(DEPTH):
        x = hybrid_layer(x, c_act, positions, w_mod[l], b_mod[l], pre_norm_gain[l], post_norm_gain[l],
                         w_in[l], attn_sinks[l], gla_gate_w[l], gla_gate_b[l], gla_norm_gain[l], w_out[l])
    return x


Q_BLOCK = 128
LN_EPS = 1e-5
RMS_EPS = 1e-5
N_BUCKETS = 32
MAX_DISTANCE = 2048
N_BIAS_COLS = 16
A_HEADS = 4
A_QK = 64
A_V = 128
B_PAIRS = ((128, 1), (512, 4), (2048, 16))
B_HEADS = 4
B_DIM = 64
C_HEADS = 8
C_KV_GROUPS = 2
C_DIM = 64
CMP_LEN = 32
CMP_STRIDE = 16
CMP_HIDDEN = 256
SLC_BLOCK = 64
SLC_TOP_N = 16
SLC_Q_CHUNK = 32
WIN_SIZE = 512
D_HEADS = 8
D_Q_LORA = 384
D_KV_LORA = 256
D_NOPE = 64
D_ROPE = 32
D_V = 64
D_FF = 2816
CONV_W = 3

EVEN_SPLITS = (2 * A_HEADS * A_QK, 2 * A_HEADS * A_QK, A_HEADS * A_V, len(B_PAIRS) * 3 * B_HEADS * B_DIM)
EVEN_IN = sum(EVEN_SPLITS)
EVEN_OUT = A_HEADS * A_V + B_HEADS * B_DIM
ODD_SPLITS = (C_HEADS * C_DIM, 3 * 2 * C_KV_GROUPS * C_DIM, 3 * C_HEADS, D_Q_LORA, D_KV_LORA, D_ROPE)
ODD_IN = sum(ODD_SPLITS)
ODD_OUT = C_HEADS * C_DIM + D_HEADS * D_V


def split_cols(h, sizes):
    outs, off = [], 0
    for s in sizes:
        outs.append(h[..., off:off + s])
        off += s
    return outs

def layer_norm(x, g, b):
    xf = x.astype(jnp.float32)
    mu = jnp.mean(xf, -1, keepdims=True)
    var = jnp.mean(jnp.square(xf - mu), -1, keepdims=True)
    return ((xf - mu) * lax.rsqrt(var + LN_EPS) * g + b).astype(x.dtype)

def rms_norm_2(x, g):
    xf = x.astype(jnp.float32)
    return (xf * lax.rsqrt(jnp.mean(xf * xf, -1, keepdims=True) + RMS_EPS) * g).astype(x.dtype)

def t5_bucket(dist):
    max_exact = N_BUCKETS // 2
    n = jnp.maximum(dist, 0)
    nf = jnp.maximum(n, 1).astype(jnp.float32)
    large = max_exact + (jnp.log(nf / max_exact) / math.log(MAX_DISTANCE / max_exact) * (N_BUCKETS - max_exact)).astype(jnp.int32)
    return jnp.where(n < max_exact, n, jnp.minimum(large, N_BUCKETS - 1))

def rope(x, pos):
    half = x.shape[-1] // 2
    inv = ROPE_THETA ** (-jnp.arange(half, dtype=jnp.float32) / half)
    ang = pos.astype(jnp.float32)[:, None] * inv
    ang = ang.reshape(ang.shape[:1] + (1,) * (x.ndim - 3) + (half,))
    cos, sin = jnp.cos(ang), jnp.sin(ang)
    xf = x.astype(jnp.float32)
    x1, x2 = xf[..., :half], xf[..., half:]
    return jnp.concatenate([x1 * cos - x2 * sin, x1 * sin + x2 * cos], -1).astype(x.dtype)

def banded_attention(q, k, v, max_dist, bias_tbl, dist_scale):
    N, L, G, Hg, D = q.shape
    blk = Q_BLOCK
    n_prev = -(-max_dist // blk)
    nb = -(-L // blk)
    pad = nb * blk - L
    qb = jnp.pad(q, ((0, 0), (0, pad), (0, 0), (0, 0), (0, 0))).reshape(N, nb, blk, G, Hg, D)
    kv_pad = ((0, 0), (n_prev * blk, pad), (0, 0), (0, 0))
    kb = jnp.pad(k, kv_pad).reshape(N, nb + n_prev, blk, G, D)
    vb = jnp.pad(v, kv_pad).reshape(N, nb + n_prev, blk, G, v.shape[-1])
    kw = jnp.concatenate([kb[:, j:j + nb] for j in range(n_prev + 1)], axis=2)
    vw = jnp.concatenate([vb[:, j:j + nb] for j in range(n_prev + 1)], axis=2)
    n_keys = (n_prev + 1) * blk
    kj = jnp.arange(n_keys)
    dist = jnp.arange(blk)[:, None] + n_prev * blk - kj[None, :]
    kpos = (jnp.arange(nb) * blk)[:, None, None] - n_prev * blk + kj[None, None, :]
    valid = (dist >= 0) & (dist <= max_dist) & (kpos >= 0)
    bias = bias_tbl[t5_bucket(dist * dist_scale)].transpose(2, 3, 0, 1)
    s = jnp.einsum('nbqghd,nbkgd->nbghqk', qb, kw).astype(jnp.float32) * (D ** -0.5) + bias
    s = jnp.where(valid[:, None, None], s, -jnp.inf)
    m = jnp.max(s, -1, keepdims=True)
    p = jnp.exp(s - m)
    den = jnp.sum(p, -1, keepdims=True)
    o = jnp.einsum('nbghqk,nbkgd->nbqghd', (p / den).astype(v.dtype), vw)
    lse = (m + jnp.log(den))[..., 0].transpose(0, 1, 4, 2, 3)
    o = o.reshape(N, nb * blk, G, Hg, v.shape[-1])[:, :L]
    lse = lse.reshape(N, nb * blk, G, Hg)[:, :L]
    return o, lse

def diff_attention(q, k, v, lam, bias_tbl):
    B, S, _, H, Dk = q.shape
    nb = S // Q_BLOCK
    kpos = jnp.arange(S)
    qb = q.reshape(B, nb, Q_BLOCK, 2, H, Dk).swapaxes(0, 1)

    def step(args):
        qi, start = args
        dist = (start + jnp.arange(Q_BLOCK))[:, None] - kpos[None, :]
        bias = bias_tbl[t5_bucket(dist)].transpose(2, 0, 1)
        s = jnp.einsum('bqmhd,bkmhd->bmhqk', qi, k).astype(jnp.float32) * (Dk ** -0.5) + bias
        s = jnp.where(dist >= 0, s, -jnp.inf)
        p = jax.nn.softmax(s, axis=-1)
        w = p[:, 0] - lam * p[:, 1]
        return jnp.einsum('bhqk,bkhd->bqhd', w.astype(v.dtype), v)

    o = lax.map(step, (qb, jnp.arange(nb) * Q_BLOCK))
    return o.swapaxes(0, 1).reshape(B, S, H, v.shape[-1])

def to_residue(t, d):
    B, S, H, D = t.shape
    return t.reshape(B, S // d, d, H, D).transpose(0, 2, 1, 3, 4).reshape(B * d, S // d, H, D)

def dilated_mixture(hb, bias_table):
    B, S = hb.shape[:2]
    outs, lses = [], []
    for i, (window, d) in enumerate(B_PAIRS):
        M = S // d
        col = A_HEADS + i * B_HEADS
        tbl = bias_table[:, col:col + B_HEADS][:, :, None]
        o, lse = banded_attention(to_residue(hb[:, :, i, 0], d)[:, :, :, None], to_residue(hb[:, :, i, 1], d),
                                  to_residue(hb[:, :, i, 2], d), window // d, tbl, d)
        outs.append(o.reshape(B, d, M, B_HEADS, B_DIM).transpose(0, 2, 1, 3, 4).reshape(B, S, B_HEADS, B_DIM))
        lses.append(lse.reshape(B, d, M, B_HEADS).transpose(0, 2, 1, 3).reshape(B, S, B_HEADS))
    wts = jax.nn.softmax(jnp.stack(lses), axis=0)
    return jnp.einsum('pbsh,pbshd->bshd', wts.astype(outs[0].dtype), jnp.stack(outs))

def nsa_compress(t, pe, w1, w2):
    B, S, G, D = t.shape
    ch = t.reshape(B, S // CMP_STRIDE, CMP_STRIDE, G, D)
    blocks = jnp.concatenate([ch[:, :-1], ch[:, 1:]], axis=2)
    blocks = blocks + pe[:, None, :]
    flat = blocks.transpose(0, 1, 3, 2, 4).reshape(B, blocks.shape[1], G, CMP_LEN * D)
    return jax.nn.gelu(flat @ w1) @ w2

def nsa_compressed(q, k, v, pe, w1, w2, tbl):
    B, S, G, Hg, D = q.shape
    kc = nsa_compress(k, pe[0], w1[0], w2[0])
    vc = nsa_compress(v, pe[1], w1[1], w2[1])
    ncb = kc.shape[1]
    kend = jnp.arange(ncb) * CMP_STRIDE + CMP_LEN - 1
    dist = jnp.arange(S)[:, None] - kend[None, :]
    bias = tbl[t5_bucket(dist)].transpose(2, 3, 0, 1)
    s = jnp.einsum('bqghd,bcgd->bghqc', q, kc).astype(jnp.float32) * (D ** -0.5) + bias
    s = jnp.where(dist >= 0, s, -jnp.inf)
    m = jnp.max(s, -1, keepdims=True)
    p = jnp.exp(s - jnp.where(jnp.isfinite(m), m, 0.0))
    den = jnp.sum(p, -1, keepdims=True)
    p = p / jnp.where(den > 0, den, 1.0)
    o = jnp.einsum('bghqc,bcgd->bqghd', p.astype(v.dtype), vc)
    n_sel = S // SLC_BLOCK
    r = SLC_BLOCK // CMP_STRIDE
    pg = jnp.sum(p, axis=2)
    pp = jnp.pad(pg, ((0, 0), (0, 0), (0, 0), (1, r * (n_sel + 1) - 1 - ncb))).reshape(B, G, S, n_sel + 1, r)
    score = 0.5 * pp[..., :-1, 0] + jnp.sum(pp[..., :-1, 1:], -1) + 0.5 * pp[..., 1:, 0]
    return o, score

def nsa_selected(q, k, v, slc_score, tbl):
    B, S, G, Hg, D = q.shape
    n_sel = S // SLC_BLOCK
    top_n = min(SLC_TOP_N, n_sel)
    qblk = jnp.arange(S) // SLC_BLOCK
    jb = jnp.arange(n_sel)[None, :]
    allowed = jb <= qblk[:, None]
    forced = (jb == 0) | (jb == qblk[:, None]) | (jb == qblk[:, None] - 1)
    score = jnp.where(forced, jnp.inf, jnp.where(allowed, slc_score.astype(jnp.float32), -jnp.inf))
    _, idx = lax.top_k(score, top_n)
    kb = k.reshape(B, n_sel, SLC_BLOCK, G, D).transpose(0, 3, 1, 2, 4)
    vb = v.reshape(B, n_sel, SLC_BLOCK, G, v.shape[-1]).transpose(0, 3, 1, 2, 4)
    nq = S // SLC_Q_CHUNK
    idx_c = idx.transpose(0, 2, 1, 3).reshape(B, nq, SLC_Q_CHUNK, G, top_n).swapaxes(0, 1)
    q_c = q.reshape(B, nq, SLC_Q_CHUNK, G, Hg, D).swapaxes(0, 1)
    bi = jnp.arange(B)[:, None, None, None]
    gi = jnp.arange(G)[None, None, :, None]
    tok = jnp.arange(SLC_BLOCK)

    def step(args):
        qi, ii, start = args
        kg = kb[bi, gi, ii]
        vg = vb[bi, gi, ii]
        qp = start + jnp.arange(SLC_Q_CHUNK)
        dist = qp[None, :, None, None, None] - (ii[..., None] * SLC_BLOCK + tok)
        bias = tbl[t5_bucket(dist), gi[..., None]]
        s = jnp.einsum('bqghd,bqgnkd->bqghnk', qi, kg).astype(jnp.float32) * (D ** -0.5) + jnp.moveaxis(bias, -1, 3)
        s = jnp.where((dist >= 0)[:, :, :, None], s, -jnp.inf)
        p = jax.nn.softmax(s.reshape(s.shape[:4] + (-1,)), axis=-1).astype(v.dtype)
        return jnp.einsum('bqghk,bqgkd->bqghd', p, vg.reshape(vg.shape[:3] + (-1, vg.shape[-1])))

    o = lax.map(step, (q_c, idx_c, jnp.arange(nq) * SLC_Q_CHUNK))
    return o.swapaxes(0, 1).reshape(B, S, G, Hg, v.shape[-1])

def mla_attention(q_nope, q_rope, k_nope, k_rope, v):
    B, S, H, _ = q_nope.shape
    nb = S // Q_BLOCK
    kpos = jnp.arange(S)
    scale = (D_NOPE + D_ROPE) ** -0.5

    def blocks(t):
        return t.reshape((B, nb, Q_BLOCK) + t.shape[2:]).swapaxes(0, 1)

    def step(args):
        qn, qr, start = args
        s = (jnp.einsum('bqhd,bkhd->bhqk', qn, k_nope) + jnp.einsum('bqhr,bkr->bhqk', qr, k_rope)).astype(jnp.float32) * scale
        s = jnp.where((start + jnp.arange(Q_BLOCK))[:, None] >= kpos[None, :], s, -jnp.inf)
        p = jax.nn.softmax(s, axis=-1).astype(v.dtype)
        return jnp.einsum('bhqk,bkhd->bqhd', p, v)

    o = lax.map(step, (blocks(q_nope), blocks(q_rope), jnp.arange(nb) * Q_BLOCK))
    return o.swapaxes(0, 1).reshape(B, S, H, v.shape[-1])

def even_mixer(x, w_in, w_out, lam_p, subln_g, bias_table, layer_idx):
    B, S, _ = x.shape
    qa, ka, va, hb = split_cols(x @ w_in, EVEN_SPLITS)
    qa = qa.reshape(B, S, 2, A_HEADS, A_QK)
    ka = ka.reshape(B, S, 2, A_HEADS, A_QK)
    va = va.reshape(B, S, A_HEADS, A_V)
    lam_init = 0.8 - 0.6 * math.exp(-0.3 * layer_idx)
    lp = lam_p.astype(jnp.float32)
    lam = jnp.exp(jnp.sum(lp[0] * lp[1])) - jnp.exp(jnp.sum(lp[2] * lp[3])) + lam_init
    o_a = diff_attention(qa, ka, va, lam, bias_table[:, :A_HEADS])
    o_a = rms_norm_2(o_a, subln_g) * (1.0 - lam_init)
    o_b = dilated_mixture(hb.reshape(B, S, len(B_PAIRS), 3, B_HEADS, B_DIM), bias_table)
    y = jnp.concatenate([o_a.reshape(B, S, -1), o_b.reshape(B, S, -1)], axis=-1)
    return y @ w_out

def odd_mixer(x, w_in, w_out, cmp_pe, cmp_w1, cmp_w2, q_norm_g, kv_norm_g, w_uq, w_uk, w_uv, bias_table):
    B, S, _ = x.shape
    G, Hg = C_KV_GROUPS, C_HEADS // C_KV_GROUPS
    q_c, kv_c, gate_c, cq, ckv, k_rope = split_cols(x @ w_in, ODD_SPLITS)
    q = q_c.reshape(B, S, G, Hg, C_DIM)
    kv = kv_c.reshape(B, S, 3, 2, G, C_DIM)
    gates = jax.nn.sigmoid(gate_c.astype(jnp.float32)).reshape(B, S, 3, G, Hg, 1).astype(x.dtype)
    tbl_c = bias_table[:, :C_HEADS].reshape(N_BUCKETS, G, Hg)
    o_cmp, slc_score = nsa_compressed(q, kv[:, :, 0, 0], kv[:, :, 0, 1], cmp_pe, cmp_w1, cmp_w2, tbl_c)
    o_slc = nsa_selected(q, kv[:, :, 1, 0], kv[:, :, 1, 1], slc_score, tbl_c)
    o_win, _ = banded_attention(q, kv[:, :, 2, 0], kv[:, :, 2, 1], WIN_SIZE - 1, tbl_c, 1)
    o_c = gates[:, :, 0] * o_cmp + gates[:, :, 1] * o_slc + gates[:, :, 2] * o_win
    pos = jnp.arange(S)
    qd = (rms_norm_2(cq, q_norm_g) @ w_uq).reshape(B, S, D_HEADS, D_NOPE + D_ROPE)
    c = rms_norm_2(ckv, kv_norm_g)
    k_nope = (c @ w_uk).reshape(B, S, D_HEADS, D_NOPE)
    v = (c @ w_uv).reshape(B, S, D_HEADS, D_V)
    o_d = mla_attention(qd[..., :D_NOPE], rope(qd[..., D_NOPE:], pos), k_nope, rope(k_rope, pos), v)
    y = jnp.concatenate([o_c.reshape(B, S, -1), o_d.reshape(B, S, -1)], axis=-1)
    return y @ w_out

def conv_ffn(x, w_up, conv_w, conv_b, w_down):
    a, g = jnp.split(x @ w_up, 2, axis=-1)
    g = lax.conv_general_dilated(g, conv_w[:, None, :].astype(g.dtype), window_strides=(1,),
                                 padding=((CONV_W - 1, 0),), dimension_numbers=('NWC', 'WIO', 'NWC'),
                                 feature_group_count=D_FF) + conv_b
    return (jax.nn.gelu(g) * a) @ w_down

def second_inputs(seed: int = 0) -> dict:
    key = jax.random.key(seed)
    ks = jax.random.split(key, 22)
    f32 = jnp.float32
    n_ev, n_od = (DEPTH + 1) // 2, DEPTH // 2
    beta = (8 * DEPTH) ** -0.25

    def w(k, shape, fan_in, gain=1.0):
        return jax.random.normal(k, shape, f32) * (gain * fan_in ** -0.5)

    def near_one(k, shape):
        return 1.0 + 0.02 * jax.random.normal(k, shape, f32)

    def small(k, shape, std):
        return std * jax.random.normal(k, shape, f32)

    return {
        'x': jax.random.normal(ks[0], (BATCH, SEQ, D_MODEL), f32),
        'rel_bias': small(ks[1], (N_BUCKETS, N_BIAS_COLS), 0.2),
        'ev_w_in': w(ks[2], (n_ev, D_MODEL, EVEN_IN), D_MODEL),
        'ev_w_out': w(ks[3], (n_ev, EVEN_OUT, D_MODEL), EVEN_OUT, beta),
        'ev_lambda': small(ks[4], (n_ev, 4, A_QK), 0.1),
        'ev_subln': near_one(ks[5], (n_ev, A_V)),
        'od_w_in': w(ks[6], (n_od, D_MODEL, ODD_IN), D_MODEL),
        'od_w_out': w(ks[7], (n_od, ODD_OUT, D_MODEL), ODD_OUT, beta),
        'od_cmp_pe': small(ks[8], (n_od, 2, CMP_LEN, C_DIM), 0.1),
        'od_cmp_w1': w(ks[9], (n_od, 2, CMP_LEN * C_DIM, CMP_HIDDEN), CMP_LEN * C_DIM),
        'od_cmp_w2': w(ks[10], (n_od, 2, CMP_HIDDEN, C_DIM), CMP_HIDDEN),
        'od_q_norm': near_one(ks[11], (n_od, D_Q_LORA)),
        'od_kv_norm': near_one(ks[12], (n_od, D_KV_LORA)),
        'od_w_uq': w(ks[13], (n_od, D_Q_LORA, D_HEADS * (D_NOPE + D_ROPE)), D_Q_LORA),
        'od_w_uk': w(ks[14], (n_od, D_KV_LORA, D_HEADS * D_NOPE), D_KV_LORA),
        'od_w_uv': w(ks[15], (n_od, D_KV_LORA, D_HEADS * D_V), D_KV_LORA),
        'ffn_w_up': w(ks[16], (DEPTH, D_MODEL, 2 * D_FF), D_MODEL),
        'ffn_conv_w': w(ks[17], (DEPTH, CONV_W, D_FF), CONV_W),
        'ffn_conv_b': small(ks[18], (DEPTH, D_FF), 0.02),
        'ffn_w_down': w(ks[19], (DEPTH, D_FF, D_MODEL), D_FF, beta),
        'ln_g': near_one(ks[20], (DEPTH, 2, D_MODEL)),
        'ln_b': small(ks[21], (DEPTH, 2, D_MODEL), 0.02),
    }

def second_block(x, rel_bias, ev_w_in, ev_w_out, ev_lambda, ev_subln, od_w_in, od_w_out, od_cmp_pe, od_cmp_w1,
              od_cmp_w2, od_q_norm, od_kv_norm, od_w_uq, od_w_uk, od_w_uv, ffn_w_up, ffn_conv_w, ffn_conv_b,
              ffn_w_down, ln_g, ln_b):
    alpha = (2 * DEPTH) ** 0.25
    for l in range(DEPTH):
        i = l // 2
        if l % 2 == 0:
            y = even_mixer(x, ev_w_in[i], ev_w_out[i], ev_lambda[i], ev_subln[i], rel_bias, l)
        else:
            y = odd_mixer(x, od_w_in[i], od_w_out[i], od_cmp_pe[i], od_cmp_w1[i], od_cmp_w2[i], od_q_norm[i],
                          od_kv_norm[i], od_w_uq[i], od_w_uk[i], od_w_uv[i], rel_bias)
        x = layer_norm(alpha * x + y, ln_g[l, 0], ln_b[l, 0])
        y = conv_ffn(x, ffn_w_up[l], ffn_conv_w[l], ffn_conv_b[l], ffn_w_down[l])
        x = layer_norm(alpha * x + y, ln_g[l, 1], ln_b[l, 1])
    return x


def setup_inputs(seed=0):
    out = dict(first_inputs(seed))
    for name, value in second_inputs(seed + 1).items():
        if name != "x":
            out[name + "_2"] = value
    return out


def reference(
    x, c, positions, w_mod, b_mod, pre_norm_gain, post_norm_gain, w_in, attn_sinks, gla_gate_w,
    gla_gate_b, gla_norm_gain, w_out, rel_bias_2, ev_w_in_2, ev_w_out_2, ev_lambda_2,
    ev_subln_2, od_w_in_2, od_w_out_2, od_cmp_pe_2, od_cmp_w1_2, od_cmp_w2_2, od_q_norm_2,
    od_kv_norm_2, od_w_uq_2, od_w_uk_2, od_w_uv_2, ffn_w_up_2, ffn_conv_w_2, ffn_conv_b_2,
    ffn_w_down_2, ln_g_2, ln_b_2,
):
    x = first_block(
        x, c, positions, w_mod, b_mod, pre_norm_gain, post_norm_gain, w_in, attn_sinks,
        gla_gate_w, gla_gate_b, gla_norm_gain, w_out,
    )
    return second_block(
        x, rel_bias_2, ev_w_in_2, ev_w_out_2, ev_lambda_2, ev_subln_2, od_w_in_2, od_w_out_2,
        od_cmp_pe_2, od_cmp_w1_2, od_cmp_w2_2, od_q_norm_2, od_kv_norm_2, od_w_uq_2, od_w_uk_2,
        od_w_uv_2, ffn_w_up_2, ffn_conv_w_2, ffn_conv_b_2, ffn_w_down_2, ln_g_2, ln_b_2,
    )


_drawn_inputs = setup_inputs


def setup_inputs(seed=0):
    import zlib

    import numpy as np

    out = dict(_drawn_inputs(seed))
    spreads = {}
    factors = {'pre_norm_gain': 3.238,
     'post_norm_gain': 5.763,
     'attn_sinks': 8.0,
     'gla_gate_b': 8.0,
     'gla_norm_gain': 7.901,
     'ev_lambda_2': 3.077,
     'ev_subln_2': 8.0,
     'od_cmp_pe_2': 7.821,
     'od_q_norm_2': 8.0,
     'od_kv_norm_2': 8.0,
     'ffn_conv_b_2': 8.0}
    for name, (base, spread) in spreads.items():
        noise = np.random.default_rng([zlib.crc32(name.encode()), seed]).standard_normal(out[name].shape)
        drawn = base * np.exp(spread * noise) if base else spread * noise
        out[name] = jnp.asarray(drawn.astype(out[name].dtype))
    for name, factor in factors.items():
        out[name] = (out[name] * factor).astype(out[name].dtype)
    return out
```

```python
from contextlib import ExitStack

import numpy as np

import concourse.bass as bass
from concourse import mybir

F32 = mybir.dt.float32
I32 = mybir.dt.int32
ACT = mybir.ActivationFunctionType
ALU = mybir.AluOpType
AX = mybir.AxisListType

P = 128
T = 512
B = 128
NB = T // B
D = 1024
KD = D // P
NEG = -1e30
LAYERS = 2
D_IN = 3088
DFF = 2816
NF = DFF // P
ALPHA = (2 * LAYERS) ** 0.25
LAM_INIT = 0.8 - 0.6
SLOTS = 8
HSPAN = 896
BUCKETS = 32
WIDEST = 1280

NTILES = 34


def t5_bucket(dist):
    n = np.maximum(dist, 0)
    nf = np.maximum(n, 1).astype(np.float32)
    large = 16 + (np.log(nf / np.float32(16)) / np.float32(np.log(2048 / 16)) * np.float32(16)).astype(np.int32)
    return np.where(n < 16, n, np.minimum(large, 31))


VECS = [(-511, 511, lambda d: d >= 0), (-127, 255, lambda d: (d >= 0) & (d <= 128)),
        (-127, 511, lambda d: (d >= 0) & (d % 4 == 0)), (-127, 511, lambda d: (d >= 0) & (d % 16 == 0))]
VEC_AT = np.cumsum([0] + [b - a + 1 for a, b, _ in VECS])
VEC_LEN = int(VEC_AT[-1])


def constants():
    f = np.float32
    out = {}
    eye = np.eye(P)
    rot = np.zeros((2, P, P))
    for n, half in enumerate((32, 16)):
        for m in range(P):
            if m % (2 * half) < half:
                rot[n, m + half, m] = -1
            else:
                rot[n, m - half, m] = 1
    ones = np.ones((P, P))
    pair = np.kron(np.eye(2), np.ones((64, 64))) / 64
    out["mats"] = np.stack([eye, rot[0], rot[1], ones / 1024, pair, ones / 128, ones / 384, ones / 256], 1)
    p = np.arange(P)
    freq = np.stack([10000.0 ** (-(p % 32) * 2 / 64), 1 / 10000.0 ** ((p % 32) / 31), np.zeros(P) + (p >= 31)], 1)
    out["freq"] = freq
    inv = (f(10000.0) ** (-np.arange(16, dtype=f) / f(16))).astype(f)[p % 16]
    ang = (np.arange(T, dtype=f)[None] * inv[:, None]).astype(f).astype(np.float64)
    out["mla_rope"] = np.stack([np.cos(ang), np.sin(ang)], 1)
    j, i = np.arange(P)[:, None], np.arange(T)[None]
    gam = 1 - 2.0 ** (-5 - np.arange(4))
    out["decay"] = np.stack([np.where(i >= j, g ** np.maximum(i - j, 0), 0) / 8 for g in gam], 1)
    out["upper"] = (i >= j) / 16.0
    q, c = np.arange(P)[:, None], np.arange(2 * B)[None]
    rel = q + B - c
    out["window"] = np.where((rel >= 0) & (rel < 128), 0, NEG)
    out["causal"] = np.where(q + np.arange(T)[None] - 127 >= 0, 0, NEG)
    j, i = np.arange(P)[:, None], np.arange(P)[None]
    out["sub"] = np.stack([(j // 16 < i // 16), (j // 16 == i // 16) & (i >= j)], 1)
    out["heads"] = (p[:, None] // 32 == np.arange(4)[None])
    hot = []
    for a, b, ok in VECS:
        d = np.arange(a, b + 1)
        h = np.zeros((BUCKETS + 1, len(d)))
        h[np.where(ok(d), t5_bucket(d), BUCKETS), np.arange(len(d))] = 1
        hot.append(h)
    out["onehot"] = np.concatenate(hot, 1)
    return {k: np.ascontiguousarray(v, dtype=f) for k, v in out.items()}


class Side:

    def __init__(self):
        self.given, self.taken, self.last = {}, {}, None
        self.job = self.seg = self.turn = self.group = self.sq = self.step = 0
        self.emptied = {"act": 0, "dve": 0}

    def signals(self, sem):
        self.given[id(sem)] = self.given.get(id(sem), 0) + 1
        self.last = (sem, self.given[id(sem)])
        return sem

    def after(self, sem, n=1):
        self.taken[id(sem)] = self.taken.get(id(sem), 0) + n
        return self.taken[id(sem)]

    def emptied_by(self, by):
        self.emptied[by] += 1
        self.job += 1


def build(nc, io, cst, out, stop=None):
    ctx = ExitStack()
    with ctx:
        def sb(name, shape):
            return ctx.enter_context(nc.sbuf_tensor(name, [P] + shape, F32))

        X = sb("X", [KD, T])
        H = sb("H", [KD, T])
        Z = sb("Z", [NTILES, T])
        RING = sb("RING", [SLOTS, 8, P])
        BIAS = sb("BIAS", [8 * HSPAN])
        S = sb("S", [2, WIDEST])
        E = sb("E", [2, WIDEST])
        ET = sb("ET", [2, WIDEST // B, B])
        MATS = sb("MATS", [8, P])
        SMALL = sb("SMALL", [1000])
        GAIN = sb("GAIN", [2, LAYERS, KD])
        LNG = sb("LNG", [2, 4, KD])
        CONV = sb("CONV", [LAYERS, 4, NF])
        BMOD = sb("BMOD", [LAYERS, 24])
        TINY = sb("TINY", [128])
        PS = ctx.enter_context(nc.psum_tensor("PS", [P, 8, T], F32))
        SCR = nc.dram_tensor("bias_vectors", [16, VEC_LEN], F32, kind="Internal").ap()

        IDN, ROT64, ROT32, ONES_D, ONES_64, ONES_128, ONES_384, ONES_256 = (MATS[:, i, :] for i in range(8))
        EPS6, EPS5, ONE = TINY[:, 0:1], TINY[:, 1:2], TINY[:, 2:3]
        FREQ, LATE = TINY[:, 4:6], TINY[:, 6:7]
        NMAX, DEN, RDEN = TINY[:, 8:10], TINY[:, 10:12], TINY[:, 12:14]
        GLAG, SUBG, LAM, LTMP = TINY[:, 14:16], TINY[:, 16:17], TINY[:, 17:18], TINY[:, 20:24]
        QG, KVG = TINY[:, 24:27], TINY[:, 28:30]
        SINKS = TINY[:, 32:48]
        CT, CACT = TINY[:, 48:56], TINY[:, 56:64]
        MOD = TINY[:, 64:88]
        GA, GB = TINY[:, 88:96], TINY[:, 96:104]

        DECAY = BIAS[:, 0:2048].rearrange("p (h i) -> p h i", h=4)
        UPPER = BIAS[:, 2048:2560]
        WINDOW = BIAS[:, 2560:2816]
        SUBM = BIAS[:, 2816:3072].rearrange("p (a i) -> p a i", a=2)
        HEADS = BIAS[:, 3072:3076]
        BREF = BIAS[:, 3076:3108]
        ROPE = BIAS[:, 3584:5632].rearrange("p (a t) -> p a t", a=4)
        GK1 = BIAS[:, 5632:6400]
        BFULL4 = BIAS[:, 0:2048].rearrange("p (h x) -> p h x", h=4)
        BD4 = BIAS[:, 3072:5120].rearrange("p (h x) -> p h x", h=4)
        BWIN = BIAS[:, 2048:3072].rearrange("p (h x) -> p h x", h=4)
        BD16 = BIAS[:, 5120:7168].rearrange("p (h x) -> p h x", h=4)
        BFULL8 = BIAS[:, :].rearrange("p (h x) -> p h x", h=8)
        TABLE = SMALL[0:33, 0:16]
        GWB = [SMALL[0:17, 32 + 128 * l:160 + 128 * l] for l in range(LAYERS)]
        LAMP = SMALL[:, 600:856]
        CAUSAL = SMALL[:, 0:512]
        KCT = SMALL[:, 512:574]
        VC = SMALL[0:31, 576:704].rearrange("p (g d) -> p g d", g=2)
        H1 = SMALL[:, 704:828].rearrange("p (h c) -> p h c", h=2)
        PLACE = SMALL[:, 828:860].rearrange("p (a l) -> p a l", a=2)
        GATES = SMALL[:, 860:956]
        SQ = S[:, 0, 0:1024].rearrange("p (a t) -> p a t", a=2)
        RS = S[:, 1, 0:512]
        RT = S[:, 1, 512:1024]
        GPAD = E[:, 0, 0:1032].rearrange("p (a t) -> p a t", a=2)
        CONVED = E[:, 1, 0:1024].rearrange("p (a t) -> p a t", a=2)
        GELUED = ET[:, 0, 0:8, :].rearrange("p (a b) q -> p a (b q)", a=2)
        MROPE = ET[:, 1, 0:8, :].rearrange("p (a b) q -> p a (b q)", a=2)
        CMPIN = E[:, :, :].rearrange("p a t -> p (a t)")[:, 0:1984].rearrange("p (a l c) -> p a l c", a=2, l=16)

        def z(i, n=1):
            return Z[:, i, :] if n == 1 else Z[:, i:i + n, :].rearrange("p a t -> p (a t)")

        def ztok(i, tt, c0, n):
            return Z[:, i, tt * P + c0:tt * P + c0 + n]

        XIN = Z[:, 0:8, :].rearrange("p (b a) t -> p b (a t)", b=NB)
        HOT, VECS_SB = z(10, 6)[0:33, 0:VEC_LEN], z(16, 6)[0:16, 0:VEC_LEN]
        HOT_CUTS = [(c, min(T, VEC_LEN - c)) for c in range(0, VEC_LEN, T)]
        GK2 = z(0, 2).rearrange("p (s j) -> p s j", s=8)
        GPROD = z(2, 4).rearrange("p (c j) -> p c j", c=16)
        GQ1, GQ2 = z(10), z(11)
        GS, GTMP = Z[:, 6:10, :], z(33)

        def sem(name):
            return ctx.enter_context(nc.semaphore(name))

        pe_step, act_step, dve_step = sem("pe_step"), sem("act_step"), sem("dve_step")
        pe_met, act_met, dve_met = sem("pe_met"), sem("act_met"), sem("dve_met")
        const_in, x_in, table_out, bias_in, stored = (sem(n) for n in ("const_in", "x_in", "table_out", "bias_in", "stored"))
        loaded = [sem(f"loaded{i}") for i in range(SLOTS)]
        acc_ready, acc_free_act, acc_free_dve = sem("acc_ready"), sem("acc_free_act"), sem("acc_free_dve")
        scores_ready, scores_free, max_ready = sem("scores_ready"), sem("scores_free"), sem("max_ready")
        exp_ready, probs_ready, turned, turn_free = sem("exp_ready"), sem("probs_ready"), sem("turned"), sem("turn_free")
        values_done, mix_free = sem("values_done"), sem("mix_free")
        sq_ready, sq_used, rstd_ready, normed = sem("sq_ready"), sem("sq_used"), sem("rstd_ready"), sem("normed")
        gla_to_act, gla_to_pe, gla_act = sem("gla_to_act"), sem("gla_to_pe"), sem("gla_act")
        conv_ready, gelu_ready, cmp_ready = sem("conv_ready"), sem("gelu_ready"), sem("cmp_ready")
        side_dve, side_act = sem("side_dve"), sem("side_act")

        def cols(w, c0, n, k0=0, nk=KD):
            return (0, n, nk, w[k0 * P:(k0 + nk) * P, c0:c0 + n].rearrange("(k p) n -> p k n", p=P))

        def at(part, d0):
            return (d0,) + part[1:]

        def job(kind, chunks, src, dst, how="copy", by="act", m=P, **more):
            return dict(kind=kind, chunks=chunks, src=src, dst=dst, how=how, by=by, m=m, **more)

        def feat(w, c0, src, dst, m=P, nk=KD, **more):
            chunks = [[cols(w, c0, m, k0, min(8, nk - k0))] for k0 in range(0, nk, 8)]
            return job("F", chunks, src, dst, m=m, **more)

        def tok(w, c0, src, dst, m=P, nk=KD, **more):
            return job("T", [[cols(w, c0, m, 0, nk)]], src, dst, m=m, **more)

        def twice(w, c0, src, dst, **more):
            part = cols(w, c0, 64)
            return job("F", [[part, at(part, 64)]], src, dst, **more)

        def with_rope(jobs, rot, cos, sin):
            got = []
            for n, j in enumerate(jobs):
                got.append(j)
                if n:
                    got.append(dict(kind="R", chunks=[], of=jobs[n - 1], rot=rot, cos=cos, sin=sin, by="dve"))
            got.append(dict(kind="R", chunks=[], of=jobs[-1], rot=rot, cos=cos, sin=sin, by="dve"))
            for n, g in enumerate(got):
                if g["kind"] == "R":
                    g["back"] = n - max(k for k in range(n) if got[k] is g["of"])
            return got

        def hsrc(k):
            return H[:, k, :]

        def xsrc(k):
            return X[:, k, :]

        def mod_jobs(l):
            w = io["w_mod"][l]
            return [dict(kind="M", by="dve", layer=l, n0=4 * g,
                         chunks=[[cols(w, (4 * g + i) * P, P)] for i in range(4)]) for g in range(6)]

        AQ, AK, RQ, RK, AG, RG, GG, GQ, GK, AV, RV, GV, GAT, BT, Q1, Q2, LA, TMP = (
            0, 4, 6, 8, 10, 14, 16, 18, 19, 20, 21, 23, 25, 26, 27, 28, 31, 32)

        def first_jobs(l):
            w = io["w_in"][l]
            jobs = with_rope([feat(w, 128 * i, hsrc, z(AQ + i)) for i in range(4)]
                             + [twice(w, 512 + 64 * g, hsrc, z(AK + g)) for g in range(2)],
                             ROT64, ROPE[:, 0, :], ROPE[:, 1, :])
            jobs += with_rope([feat(w, 1280 + 128 * i, hsrc, z(RQ + i)) for i in range(4)],
                              ROT64, ROPE[:, 2, :], ROPE[:, 3, :])
            jobs += [tok(w, 640, hsrc, z(AV))]
            jobs += [tok(w, 1792 + 128 * i, hsrc, z(RV + i)) for i in range(2)]
            jobs += [tok(w, 2560 + 128 * i, hsrc, z(GV + i)) for i in range(2)]
            jobs += [feat(w, 2304, hsrc, z(GQ), scale=32 ** -0.5), feat(w, 2432, hsrc, z(GK))]
            jobs += [feat(w, 3072, hsrc, Z[0:16, GAT, :], m=16)]
            jobs += [feat(w, 768 + 128 * i, hsrc, z(AG + i), how="silu") for i in range(4)]
            jobs += [feat(w, 2048 + 128 * i, hsrc, z(RG + i), how="silu") for i in range(2)]
            jobs += [feat(w, 2816 + 128 * i, hsrc, z(GG + i), how="silu") for i in range(2)]
            return jobs

        def out_jobs(w, nk, how):
            if how == "copy":
                return [feat(w, 128 * n, hsrc, z(n), nk=nk) for n in range(KD)]
            return [feat(w, 128 * n, hsrc, X[:, n, :], nk=nk, how="res", by="dve") for n in range(KD)]

        QA, KA, VA, BQ, BK, BV = 0, 4, 8, 12, 18, 24

        def even_jobs():
            w = io["ev_w_in_2"][0]
            jobs = [feat(w, 128 * i, xsrc, z(QA + i)) for i in range(4)]
            jobs += [feat(w, 512 + 128 * i, xsrc, z(KA + i)) for i in range(4)]
            jobs += [tok(w, 1024 + 128 * i, xsrc, z(VA + i)) for i in range(4)]
            for br in range(3):
                jobs += [feat(w, 1536 + 768 * br + 128 * i, xsrc, z(BQ + 2 * br + i)) for i in range(2)]
                jobs += [feat(w, 1792 + 768 * br + 128 * i, xsrc, z(BK + 2 * br + i)) for i in range(2)]
                jobs += [tok(w, 2048 + 768 * br + 128 * i, xsrc, z(BV + 2 * br + i)) for i in range(2)]
            return jobs

        CQT, SK, WK, SV, WV, CQ, CKV, KR, QN, QR, KN, MV, CK, CV = 0, 4, 6, 8, 9, 10, 13, 15, 16, 20, 22, 26, 30, 32

        def odd_jobs():
            w = io["od_w_in_2"][0]
            jobs = []
            for kv, d in ((0, CK), (1, CV)):
                jobs += [twice(w, 512 + kv * 128 + g * 64, xsrc, z(d + g), how="shift") for g in range(2)]
            jobs += [feat(w, 128 * i, xsrc, z(CQT + i)) for i in range(4)]
            for br, d in ((1, SK), (2, WK)):
                jobs += [twice(w, 512 + br * 256 + g * 64, xsrc, z(d + g)) for g in range(2)]
            jobs += [tok(w, 512 + 256 + 128, xsrc, z(SV)), tok(w, 512 + 512 + 128, xsrc, z(WV))]
            jobs += [tok(w, 1280, xsrc, GATES, m=24, how="sigmoid")]
            jobs += [feat(w, 1304 + 128 * i, xsrc, z(CQ + i)) for i in range(3)]
            jobs += [feat(w, 1688 + 128 * i, xsrc, z(CKV + i)) for i in range(2)]
            part = cols(w, 1944, 32)
            return jobs + with_rope([job("F", [[at(part, 32 * i) for i in range(4)]], xsrc, z(KR))], ROT32,
                                    MROPE[:, 0, :], MROPE[:, 1, :])

        def cmp_jobs():
            got = []
            for kv in range(2):
                w1 = io["od_cmp_w1_2"][0, kv]
                for h in range(2):
                    got.append(dict(kind="C", by="act", how="gelu", kv=kv, h=h,
                                    chunks=[[cols(w1, 128 * h, P, 0, 8)], [cols(w1, 128 * h, P, 8, 8)]]))
                part = cols(io["od_cmp_w2_2"][0, kv], 0, 64, 0, 2)
                got.append(dict(kind="C2", by="act", how="kct" if kv == 0 else "vc", kv=kv, back=1,
                                chunks=[[part, at(part, 64)] if kv == 0 else [part]]))
            return got

        def mla_jobs():
            wq, wk, wv = io["od_w_uq_2"][0], io["od_w_uk_2"][0], io["od_w_uv_2"][0]

            def csrc(k):
                return z(CQ + k)

            def ksrc(k):
                return z(CKV + k)
            jobs = with_rope([job("F", [[at(cols(wq, (4 * t + i) * 96 + 64, 32, 0, 3), 32 * i) for i in range(4)]],
                                  csrc, z(QR + t)) for t in range(2)], ROT32, MROPE[:, 0, :], MROPE[:, 1, :])
            jobs += [job("F", [[at(cols(wq, (2 * t + i) * 96, 64, 0, 3), 64 * i) for i in range(2)]], csrc, z(QN + t))
                     for t in range(4)]
            jobs += [feat(wk, 128 * t, ksrc, z(KN + t), nk=2) for t in range(4)]
            jobs += [tok(wv, 128 * t, ksrc, z(MV + t), nk=2) for t in range(4)]
            return jobs

        def up_jobs(l):
            w = io["ffn_w_up_2"][l]
            jobs = []
            for j in range(NF):
                jobs.append(feat(w, DFF + 128 * j, xsrc, None, how="conv", j=j))
                jobs.append(feat(w, 128 * j, xsrc, z(j), how="gate", by="dve", j=j))
            return jobs

        def down_jobs(l):
            w = io["ffn_w_down_2"][l]
            return [feat(w, 128 * n, z, X[:, n, :], nk=NF, how="res", by="dve") for n in range(KD)]

        def half(tile, h, t0, n):
            return Z[64 * (h % 2):64 * (h % 2) + 64, tile, t0:t0 + n]

        def hout(tile, h, b):
            return H[64 * (h % 2):64 * (h % 2) + 64, tile, b * B:b * B + B]

        def step(segs, values, dst, first, last, scale, sink=None, factor=None, late=False):
            return dict(segs=segs, values=values, dst=dst, first=first, last=last, scale=scale, sink=sink,
                        factor=factor, late=late, keys=sum(n for _, n, _ in segs))

        def back(view, x, n, stride=1):
            end = x - stride * n
            return view[:, x:(end if end >= 0 else None):-stride]

        def swa_steps(l):
            got = []
            for h in range(8):
                for b in range(NB):
                    k0 = max(0, b - 1)
                    n = (b + 1 - k0) * B
                    p0 = 64 * (h % 2)
                    seg = ([(half(AQ + h // 2, h, b * B, B), Z[p0:p0 + 64, AK + h // 4, k0 * B:k0 * B + n])], n,
                           WINDOW[:, 2 * B - n:2 * B])
                    vals = [ztok(AV, kb, 64 * (h // 4), 64) for kb in range(k0, b + 1)]
                    got.append(step([seg], vals, hout(h // 2, h, b), True, True, 64 ** -0.5,
                                    sink=SINKS[:, 8 * l + h:8 * l + h + 1]))
            return got

        def even_steps():
            got = []
            for h in range(4):
                for b in range(NB):
                    n = (b + 1) * B
                    for m in range(2):
                        t = 2 * m + h // 2
                        seg = ([(half(QA + t, h, b * B, B), half(KA + t, h, 0, n))], n, back(BFULL4[:, h, :], b * B + 127, n))
                        vals = [ztok(VA + h, kb, 0, P) for kb in range(b + 1)]
                        got.append(step([seg], vals, H[:, h, b * B:b * B + B], m == 0, m == 1, 64 ** -0.5,
                                        factor=LAM if m else None))
            for h in range(4):
                for b in range(NB):
                    segs, vals = [], []
                    for br, view in ((0, BWIN), (1, BD4), (2, BD16)):
                        k0 = max(0, b - 1) if br == 0 else 0
                        n = (b + 1 - k0) * B
                        segs.append(([(half(BQ + 2 * br + h // 2, h, b * B, B), half(BK + 2 * br + h // 2, h, k0 * B, n))],
                                     n, back(view[:, h, :], (b - k0) * B + 127, n)))
                        vals += [ztok(BV + 2 * br + h // 2, kb, 64 * (h % 2), 64) for kb in range(k0, b + 1)]
                    got.append(step(segs, vals, hout(4 + h // 2, h, b), True, True, 64 ** -0.5))
            return got

        def odd_steps():
            got = []
            for h in range(8):
                g, p0 = h // 4, 64 * (h % 2)
                for b in range(NB):
                    n = (b + 1) * B
                    q = half(CQT + h // 2, h, b * B, B)

                    def gate(br):
                        return GATES[:, b * 24 + br * 8 + h:b * 24 + br * 8 + h + 1]
                    seg = ([(q, KCT[p0:p0 + 64, 31 * g:31 * g + 31])], 31, back(BFULL8[:, h, :], B * b + 480, 31, 16))
                    got.append(step([seg], [VC[:, g, :]], None, True, False, 64 ** -0.5, factor=gate(0), late=b == 0))
                    for br, kt, vt in ((1, SK, SV), (2, WK, WV)):
                        seg = ([(q, Z[p0:p0 + 64, kt + g, 0:n])], n, back(BFULL8[:, h, :], B * b + 511, n))
                        vals = [ztok(vt, kb, 64 * g, 64) for kb in range(b + 1)]
                        got.append(step([seg], vals, hout(h // 2, h, b), False, br == 2, 64 ** -0.5, factor=gate(br)))
            for h in range(8):
                r0 = 32 * (h % 4)
                for b in range(NB):
                    n = (b + 1) * B
                    seg = ([(half(QN + h // 2, h, b * B, B), half(KN + h // 2, h, 0, n)),
                            (Z[r0:r0 + 32, QR + h // 4, b * B:b * B + B], Z[r0:r0 + 32, KR, 0:n])],
                           n, back(CAUSAL, b * B + 127, n))
                    vals = [ztok(MV + h // 2, kb, 64 * (h % 2), 64) for kb in range(b + 1)]
                    got.append(step([seg], vals, hout(4 + h // 2, h, b), True, True, 96 ** -0.5))
            return got

        stages = [("setup", 0)]
        for l in range(LAYERS):
            stages += [(s, l) for s in ("mod", "prenorm", "proj", "swa", "ret", "gla", "out", "postnorm")]
        stages += [("even_in", 0), ("even_mix", 0), ("even_sub", 0), ("even_out", 0), ("ln", 0), ("up", 0), ("down", 0),
                   ("ln", 1), ("odd_in", 0), ("odd_norms", 0), ("odd_up", 0), ("odd_mix", 0), ("odd_out", 0), ("ln", 2),
                   ("up", 1), ("down", 1), ("ln", 3)]
        if stop:
            stages = stages[:stages.index(stop) + 1]
        else:
            stages += [("store", 0)]

        def jobs_of(s, l):
            plans = {"mod": lambda: mod_jobs(l), "proj": lambda: first_jobs(l),
                     "out": lambda: out_jobs(io["w_out"][l], 8, "copy"), "even_in": even_jobs,
                     "even_out": lambda: out_jobs(io["ev_w_out_2"][0], 6, "res"),
                     "odd_in": lambda: odd_jobs() + cmp_jobs(), "odd_up": mla_jobs,
                     "odd_out": lambda: out_jobs(io["od_w_out_2"][0], 8, "res"),
                     "up": lambda: up_jobs(l), "down": lambda: down_jobs(l)}
            return plans[s]() if s in plans else []

        def steps_of(s, l):
            return {"swa": lambda: swa_steps(l), "even_mix": even_steps, "odd_mix": odd_steps}[s]()

        BANKS = {"setup": KD + len(HOT_CUTS), "prenorm": 1, "postnorm": 1, "ret": 2, "gla": 4, "even_sub": 4, "ln": 2,
                 "odd_norms": 2, "store": 8}
        N_CONST, BIAS_IN = [0], []

        block = ctx.enter_context(nc.Block())

        @block.gpsimd
        def _(pool):
            n_const, n_bias = [0], [0]

            def load(dst, src):
                n_const[0] += 1
                pool.dma_start(dst, src).then_inc(const_in, 16)

            def load_later(dst, src):
                n_bias[0] += 1
                pool.dma_start(dst, src).then_inc(bias_in, 16)

            def all_met(stage):
                pool.wait_ge(act_met, stages.index(stage))
                pool.wait_ge(dve_met, stages.index(stage))
                pool.wait_ge(pe_met, stages.index(stage))

            def hankel(view, vec, c0, start):
                load_later(view, bass.AP(tensor=SCR.tensor, offset=c0 * VEC_LEN + int(VEC_AT[vec]) + start,
                                         ap=[[1, P], [VEC_LEN, view.shape[1]], [1, view.shape[2]]]))

            with nc.allow_non_contiguous_dma(reason="small operands, a feature to a partition"):
                load(MATS[:, :, :], cst["mats"])
                load(TINY[:, 4:7], cst["freq"])
                load(CT, io["c"][0].rearrange("(k p) -> p k", p=P))
                load(HOT, cst["onehot"])
                load(TABLE[0:32, :], io["rel_bias_2"])
                load(z(22).bitcast(I32), io["positions"][0].partition_broadcast(P))
                for l in range(LAYERS):
                    load(BMOD[:, l, :], io["b_mod"][l].rearrange("(k p) -> p k", p=P))
                    load(GAIN[:, 0, l, :], io["pre_norm_gain"][l].rearrange("(k p) -> p k", p=P))
                    load(GAIN[:, 1, l, :], io["post_norm_gain"][l].rearrange("(k p) -> p k", p=P))
                    load(SINKS[:, 8 * l:8 * l + 8], io["attn_sinks"][l].partition_broadcast(P))
                    load(GWB[l][0:16, :], io["gla_gate_w"][l])
                    load(GWB[l][16:17, :], io["gla_gate_b"][l:l + 1])
                    for a in range(2):
                        load(GLAG[64 * a:64 * a + 64, l:l + 1], io["gla_norm_gain"][l].rearrange("(p o) -> p o", o=1))
                        load(LNG[:, 0, 2 * l + a, :], io["ln_g_2"][l, a].rearrange("(k p) -> p k", p=P))
                        load(LNG[:, 1, 2 * l + a, :], io["ln_b_2"][l, a].rearrange("(k p) -> p k", p=P))
                    for a in range(3):
                        load(CONV[:, l, a, :], io["ffn_conv_w_2"][l, a].rearrange("(k p) -> p k", p=P))
                    load(CONV[:, l, 3, :], io["ffn_conv_b_2"][l].rearrange("(k p) -> p k", p=P))
                load(DECAY, cst["decay"])
                load(UPPER, cst["upper"])
                load(WINDOW, cst["window"])
                load(SUBM, cst["sub"])
                load(HEADS, cst["heads"])
                load(SUBG, io["ev_subln_2"][0].rearrange("(p o) -> p o", o=1))
                load(QG, io["od_q_norm_2"][0].rearrange("(k p) -> p k", p=P))
                load(KVG, io["od_kv_norm_2"][0].rearrange("(k p) -> p k", p=P))
                load(LAMP, io["ev_lambda_2"][0].rearrange("a b -> (a b)").partition_broadcast(P))
                N_CONST[0] = 16 * n_const[0]
                if ("even_in", 0) in stages:
                    all_met(("even_in", 0))
                    hankel(BFULL4, 0, 0, 511 - 127)
                    hankel(BWIN, 1, 4, 0)
                    hankel(BD4, 2, 8, 0)
                    hankel(BD16, 3, 12, 0)
                BIAS_IN.append(16 * n_bias[0])
                if ("even_sub", 0) in stages:
                    all_met(("even_sub", 0))
                    load_later(MROPE, cst["mla_rope"])
                    load_later(CAUSAL, cst["causal"])
                    for kv in range(2):
                        load_later(PLACE[:, kv, :], io["od_cmp_pe_2"][0, kv].rearrange("(l two) d -> (two d) l", two=2))
                    hankel(BFULL8, 0, 0, 0)
                BIAS_IN.append(16 * n_bias[0])

        @block.sync
        def _(sp):
            sp.dma_start(XIN, io["x"][0].rearrange("(b p) n -> p b n", p=P)).then_inc(x_in, 16)
            job_of = []
            n_jobs = 0
            for s, l in stages:
                js = jobs_of(s, l)
                for j in js:
                    for parts in j["chunks"]:
                        c = len(job_of)
                        if c >= SLOTS:
                            sp.wait_ge(acc_ready, job_of[c - SLOTS] + 1)
                        for d0, n, nk, src in parts:
                            sp.dma_start(RING[:, c % SLOTS, 0:nk, d0:d0 + n], src).then_inc(loaded[c % SLOTS], 16)
                        job_of.append(n_jobs)
                    n_jobs += 1
                n_jobs += BANKS.get(s, 0)
            if not stop:
                sp.wait_ge(act_met, len(stages))
                sp.dma_start(out.rearrange("(b p) n -> p b n", p=P), XIN).then_inc(stored, 16)
                sp.wait_ge(stored, 16)


        @block.tensor
        def _(pe):
            me = Side()
            mm = nc.tensor.matmul
            frees = {"act": acc_free_act, "dve": acc_free_dve}
            freed = []
            at_chunk = [0]
            landed = [0] * SLOTS

            def begin(by):
                if me.job >= 2:
                    pe.wait_ge(*freed[me.job - 2])
                me.emptied_by(by)
                freed.append((frees[by], me.emptied[by]))
                return PS[:, (me.job - 1) % 2, :]

            def done(ins):
                ins.then_inc(me.signals(acc_ready), 1)

            def slot(parts):
                c = at_chunk[0] % SLOTS
                landed[c] += 16 * len(parts)
                pe.wait_ge(loaded[c], landed[c])
                at_chunk[0] += 1
                return RING[:, c], parts[0][2]

            def linear(jobs):
                for j in jobs:
                    bank = begin(j["by"])
                    m = j.get("m", P)
                    if "back" in j:
                        pe.wait_ge(*freed[me.job - 1 - j["back"]])
                    if j["kind"] == "R":
                        ins = mm(bank, j["rot"], j["of"]["dst"], start=True, stop=True)
                    elif j["kind"] == "F":
                        k, total = 0, sum(parts[0][2] for parts in j["chunks"])
                        for parts in j["chunks"]:
                            w, nk = slot(parts)
                            for i in range(nk):
                                ins = mm(bank[0:m, :], w[:, i, 0:m], j["src"](k), start=(k == 0), stop=(k == total - 1))
                                k += 1
                    elif j["kind"] == "T":
                        w, nk = slot(j["chunks"][0])
                        for tt in range(NB):
                            for i in range(nk):
                                ins = mm(bank[:, tt * m:tt * m + m], j["src"](i)[:, tt * B:tt * B + B], w[:, i, 0:m],
                                         start=(i == 0), stop=(i == nk - 1))
                    elif j["kind"] == "M":
                        for n, parts in enumerate(j["chunks"]):
                            w, nk = slot(parts)
                            for i in range(nk):
                                ins = mm(bank[:, n:n + 1], w[:, i, :], CACT[:, i:i + 1], start=(i == 0), stop=(i == nk - 1))
                    elif j["kind"] == "C":
                        if j["kv"] == 0 and j["h"] == 0:
                            pe.wait_ge(cmp_ready, me.after(cmp_ready))
                        for a, parts in enumerate(j["chunks"]):
                            w, nk = slot(parts)
                            for i in range(nk):
                                k = 8 * a + i
                                ins = mm(bank[:, 0:62], w[:, i, :], CMPIN[:, j["kv"], k, :], start=(k == 0), stop=(k == 15))
                    elif j["kv"] == 0:
                        w, nk = slot(j["chunks"][0])
                        for i in range(2):
                            ins = mm(bank[:, 0:62], w[:, i, :], H1[:, i, :], start=(i == 0), stop=(i == 1))
                    else:
                        w, nk = slot(j["chunks"][0])
                        for g in range(2):
                            for i in range(2):
                                ins = mm(bank[0:31, g * 64:g * 64 + 64], H1[:, i, 31 * g:31 * g + 31], w[:, i, 0:64],
                                         start=(i == 0), stop=(i == 1))
                    done(ins)

            def sums(ones, n):
                bank = begin("act")
                for k in range(n):
                    pe.wait_ge(sq_ready, me.sq + 1)
                    ins = mm(bank, ones, SQ[:, me.sq % 2, :], start=(k == 0), stop=(k == n - 1))
                    me.sq += 1
                    if k < n - 1:
                        ins.then_inc(me.signals(sq_used), 1)
                done(ins)

            def score_bank():
                if me.seg - 1 > 0:
                    pe.wait_ge(scores_free, me.seg - 1)
                me.seg += 1
                return PS[:, 2 + (me.seg - 1) % 2, :]

            def mix_bank():
                if me.group - 1 > 0:
                    pe.wait_ge(mix_free, me.group - 1)
                return PS[:, 6 + me.group % 2, :]

            def attention(steps):
                n, base, turns = len(steps), me.step, {}

                def scores(i):
                    for pairs, keys, _ in steps[i]["segs"]:
                        bank = score_bank()
                        for a, (q, k) in enumerate(pairs):
                            ins = mm(bank[:, 0:keys], q, k, start=(a == 0), stop=(a == len(pairs) - 1))
                        ins.then_inc(me.signals(scores_ready), 1)

                def turn(i):
                    pe.wait_ge(probs_ready, base + i + 1)
                    keys = steps[i]["keys"]
                    for c0 in range(0, keys, 4 * B):
                        if me.turn - 1 > 0:
                            pe.wait_ge(turn_free, me.turn - 1)
                        bank = PS[:, 4 + me.turn % 2, :]
                        for c in range(c0, min(keys, c0 + 4 * B), B):
                            w = min(B, keys - c)
                            ins = nc.tensor.transpose(bank[0:w, c - c0:c - c0 + B], E[:, (base + i) % 2, c:c + w], IDN)
                        ins.then_inc(me.signals(turned), 1)
                        me.turn += 1
                    turns[i] = me.turn

                def values(i):
                    s = steps[i]
                    pe.wait_ge(turn_free, turns[i])
                    bank = mix_bank()
                    for a, v in enumerate(s["values"]):
                        w = min(B, s["keys"] - a * B)
                        ins = mm(bank[0:v.shape[1], 0:B], v, ET[0:w, (base + i) % 2, a, :], start=(s["first"] and a == 0),
                                 stop=(s["last"] and a == len(s["values"]) - 1))
                    ins.then_inc(me.signals(values_done), 1)
                    me.group += s["last"]
                for i in range(n + 2):
                    if i < n:
                        scores(i)
                    if 1 <= i <= n:
                        turn(i - 1)
                    if i >= 2:
                        values(i - 2)
                me.step += n

            def retention():
                for h in range(4):
                    t, p0 = h // 2, 64 * (h % 2)
                    o = mix_bank()[0:64, :]

                    def value(jb):
                        pe.wait_ge(scores_free, me.seg - (jb < NB - 1))
                        mm(o[:, jb * B:T], ztok(RV + t, jb, p0, 64), E[:, jb % 2, 0:T - jb * B], start=(jb == 0),
                            stop=(jb == NB - 1), skip_group_check=True) \
                            .then_inc(me.signals(values_done), 1)
                    for jb in range(NB):
                        mm(score_bank()[:, 0:T - jb * B], Z[p0:p0 + 64, RK + t, jb * B:jb * B + B],
                            Z[p0:p0 + 64, RQ + t, jb * B:T], start=True, stop=True) \
                            .then_inc(me.signals(scores_ready), 1)
                        if jb:
                            value(jb - 1)
                    value(NB - 1)
                    me.group += 1

            def gla(l):
                pe.wait_ge(gla_to_pe, me.after(gla_to_pe))
                bank = begin("dve")
                for tt in range(NB):
                    ins = mm(bank[:, tt * B:tt * B + B], Z[0:17, GAT, tt * B:tt * B + B], GWB[l], start=True, stop=True)
                done(ins)
                pe.wait_ge(gla_to_pe, me.after(gla_to_pe))
                bank = begin("act")
                for a in range(NB):
                    ins = mm(bank[:, a * B:T], z(LA)[:, a * B:a * B + B], UPPER[:, 0:T - a * B], start=(a == 0),
                             stop=(a == NB - 1), skip_group_check=True)
                done(ins)
                for qb in range(NB):
                    pe.wait_ge(gla_to_pe, me.after(gla_to_pe))
                    for jb in range(qb):
                        bank = score_bank()
                        k0 = (0, 0, 128, 384)[qb] + jb * B
                        mm(bank, GK1[:, k0:k0 + B], GQ1, start=True, stop=True).then_inc(me.signals(scores_ready), 1)
                    bank = score_bank()
                    for a in range(8):
                        c = slice(16 * a, 16 * a + 16)
                        ins = mm(bank.rearrange("p (h i) -> p h i", h=4)[:, :, c], GK2[:, a, :],
                                 GQ2.rearrange("p (h i) -> p h i", h=4)[:, :, c], start=True, stop=True)
                    ins.then_inc(me.signals(scores_ready), 1)
                    bank = score_bank()
                    for c in range(16):
                        ins = mm(bank[:, 4 * c:4 * c + 4], GPROD[:, c, :], HEADS, start=True, stop=True)
                    ins.then_inc(me.signals(scores_ready), 1)
                    o = mix_bank()[0:64, :]
                    pe.wait_ge(gla_to_pe, me.after(gla_to_pe))
                    for h in range(4):
                        for jb in range(qb + 1):
                            ins = mm(o[:, h * B:h * B + B], ztok(GV + h // 2, jb, 64 * (h % 2), 64),
                                     GS[:, jb, h * B:h * B + B], start=(jb == 0), stop=(jb == qb))
                    ins.then_inc(me.signals(values_done), 1)
                    me.group += 1

            for n_met, (s, l) in enumerate(stages, 1):
                if s == "setup":
                    pe.wait_ge(const_in, N_CONST[0])
                    pe.wait_ge(x_in, 16)
                    for k in range(KD):
                        bank = begin("act")
                        for b in range(NB):
                            ins = nc.tensor.transpose(bank[:, b * B:b * B + B], XIN[:, b, k * P:k * P + P], IDN)
                        done(ins)
                    pe.wait_ge(side_dve, me.after(side_dve))
                    for c, w in HOT_CUTS:
                        bank = begin("dve")
                        done(mm(bank[0:16, 0:w], TABLE, HOT[:, c:c + w], start=True, stop=True))
                elif s in ("prenorm", "postnorm"):
                    sums(ONES_D, KD)
                elif s == "ln":
                    bank = begin("dve")
                    for k in range(KD):
                        ins = mm(bank, ONES_D, X[:, k, :], start=(k == 0), stop=(k == KD - 1))
                    done(ins)
                    sums(ONES_D, KD)
                elif s in ("swa", "even_mix", "odd_mix"):
                    attention(steps_of(s, l))
                elif s == "ret":
                    retention()
                    for t in range(2):
                        sums(ONES_64, 1)
                elif s == "gla":
                    gla(l)
                    for t in range(2):
                        sums(ONES_64, 1)
                elif s == "even_sub":
                    for t in range(4):
                        sums(ONES_128, 1)
                elif s == "odd_norms":
                    sums(ONES_384, 3)
                    sums(ONES_256, 2)
                elif s == "store":
                    for n in range(8):
                        bank = begin("act")
                        b, c = n // 2, n % 2
                        for i in range(4):
                            ins = nc.tensor.transpose(bank[:, i * P:i * P + P], X[:, 4 * c + i, b * B:b * B + B], IDN)
                        done(ins)
                else:
                    linear(jobs_of(s, l))
                pe.wait_ge(*me.last)
                pe.sem_inc(pe_met, 1)
                pe.wait_ge(act_met, n_met)
                pe.wait_ge(dve_met, n_met)

        @block.scalar
        def _(act):
            me = Side()
            fn = nc.scalar.activation
            vals = [0]
            squared = []
            inner = [0]

            def take():
                me.emptied_by("act")
                act.wait_ge(acc_ready, me.job)
                return PS[:, (me.job - 1) % 2, :]

            def stat(tiles, eps):
                for k, t in enumerate(tiles):
                    if me.sq >= 2:
                        act.wait_ge(*squared[me.sq - 2])
                    fn(SQ[:, me.sq % 2, :], t, ACT.Square).then_inc(me.signals(sq_ready), 1)
                    me.sq += 1
                    if k < len(tiles) - 1:
                        inner[0] += 1
                        squared.append((sq_used, inner[0]))
                    else:
                        squared.append((acc_ready, me.job + 1))
                bank = take()
                act.wait_ge(*me.last)
                fn(RS, bank, ACT.Ln, bias=eps).then_inc(me.signals(acc_free_act), 1)
                act.wait_ge(*me.last)
                fn(RS, RS, ACT.Exp, scale=-0.5).then_inc(me.signals(rstd_ready), 1)

            def linear(jobs, l):
                n = 0
                for j in jobs:
                    if j["by"] != "act":
                        me.emptied_by(j["by"])
                        continue
                    bank = take()
                    how, m = j["how"], j.get("m", P)
                    if how == "copy" and "scale" in j:
                        fn(j["dst"], bank[0:m, :], ACT.Copy, scale=j["scale"]).then_inc(me.signals(acc_free_act), 1)
                    elif how == "copy":
                        fn(j["dst"], bank[0:m, :], ACT.Copy).then_inc(me.signals(acc_free_act), 1)
                    elif how == "silu":
                        fn(j["dst"], bank, ACT.Silu).then_inc(me.signals(acc_free_act), 1)
                    elif how == "shift":
                        fn(j["dst"][0:64, :], bank[0:64, :], ACT.Copy).then_inc(me.signals(act_step), 1)
                        fn(j["dst"][64:128, 0:T - 1], bank[64:128, 1:T], ACT.Copy).then_inc(me.signals(acc_free_act), 1)
                    elif how == "sigmoid":
                        fn(j["dst"], bank[:, 0:96], ACT.Sigmoid).then_inc(me.signals(acc_free_act), 1)
                    elif how == "gelu":
                        act.wait_ge(*me.last)
                        fn(H1[:, j["h"], :], bank[:, 0:62], ACT.Gelu_apprx_tanh).then_inc(me.signals(acc_free_act), 1)
                    elif how == "kct":
                        fn(KCT, bank[:, 0:62], ACT.Copy).then_inc(me.signals(acc_free_act), 1)
                    elif how == "vc":
                        fn(VC, bank[0:31, 0:128].rearrange("p (g d) -> p g d", g=2), ACT.Copy) \
                            .then_inc(me.signals(acc_free_act), 1)
                    elif how == "conv":
                        if l * NF + n - 1 > 0:
                            act.wait_ge(conv_ready, l * NF + n - 1)
                        act.wait_ge(*me.last)
                        fn(GPAD[:, n % 2, 2:T + 2], bank, ACT.Copy).then_inc(me.signals(acc_free_act), 1)
                        act.wait_ge(conv_ready, l * NF + n + 1)
                        act.wait_ge(*me.last)
                        fn(GELUED[:, n % 2, :], CONVED[:, n % 2, :], ACT.Gelu_apprx_tanh) \
                            .then_inc(me.signals(gelu_ready), 1)
                        n += 1

            def attention(steps):
                n, base, turns, t = len(steps), me.step, [], me.turn
                for s in steps:
                    t += -(-s["keys"] // (4 * B))
                    turns.append(t)

                def exps(i):
                    s, r = steps[i], (base + i) % 2
                    act.wait_ge(max_ready, base + i + 1)
                    if i >= 2:
                        act.wait_ge(turned, turns[i - 2])
                    keys = s["keys"] + (s["sink"] is not None)
                    fn(E[:, r, 0:keys], S[:, r, 0:keys], ACT.Exp, bias=NMAX[:, r:r + 1], scale=1.0,
                        accum_out=DEN[:, r:r + 1]) \
                        .then_inc(me.signals(exp_ready), 1)

                def collect(i):
                    s, r = steps[i], (base + i) % 2
                    if i >= 2:
                        if vals[0] + i - 1 > 0:
                            act.wait_ge(values_done, vals[0] + i - 1)
                    w = min(B, s["keys"])
                    for c0 in range(0, s["keys"], 4 * B):
                        me.turn += 1
                        act.wait_ge(turned, me.turn)
                        nb = -(-min(4 * B, s["keys"] - c0) // B)
                        fn(ET[0:w, r, c0 // B:c0 // B + nb, :],
                            PS[0:w, 4 + (me.turn - 1) % 2, 0:nb * B].rearrange("p (a q) -> p a q", a=nb), ACT.Copy) \
                            .then_inc(me.signals(turn_free), 1)

                def mixed(i):
                    s = steps[i]
                    if s["last"]:
                        act.wait_ge(values_done, vals[0] + i + 1)
                        fn(s["dst"], PS[0:s["values"][0].shape[1], 6 + me.group % 2, 0:B], ACT.Copy) \
                            .then_inc(me.signals(mix_free), 1)
                        me.group += 1
                for i in range(n + 2):
                    if i < n:
                        exps(i)
                    if 1 <= i <= n:
                        collect(i - 1)
                    if i >= 2:
                        mixed(i - 2)
                me.step += n
                vals[0] += n

            def retention():
                for h in range(4):
                    vals[0] += NB
                    act.wait_ge(values_done, vals[0])
                    fn(H[64 * (h % 2):64 * (h % 2) + 64, 4 + h // 2, :], PS[0:64, 6 + me.group % 2, :], ACT.Copy) \
                        .then_inc(me.signals(mix_free), 1)
                    me.group += 1

            def gla():
                me.emptied_by("dve")
                act.wait_ge(gla_to_act, me.after(gla_to_act))
                act.wait_ge(*me.last)
                fn(z(TMP), z(TMP), ACT.Exp, scale=-1.0).then_inc(me.signals(act_step), 1)
                act.wait_ge(*me.last)
                fn(z(TMP), z(TMP), ACT.Ln, bias=ONE).then_inc(me.signals(gla_act), 1)
                bank = take()
                act.wait_ge(*me.last)
                fn(z(BT), bank, ACT.Copy).then_inc(me.signals(acc_free_act), 1)
                act.wait_ge(gla_to_act, me.after(gla_to_act))
                fn(z(Q1)[:, B:T], z(Q1)[:, B:T], ACT.Exp).then_inc(me.signals(act_step), 1)
                fn(z(Q2), z(Q2), ACT.Exp).then_inc(me.signals(act_step), 1)
                fn(GK1, GK1, ACT.Exp).then_inc(me.signals(gla_act), 1)
                for qb in range(NB):
                    act.wait_ge(gla_to_act, me.after(gla_to_act))
                    fn(z(0, 2), z(0, 2), ACT.Exp).then_inc(me.signals(act_step), 1)
                    fn(z(2, 4), z(2, 4), ACT.Exp).then_inc(me.signals(gla_act), 1)
                    vals[0] += 1
                    act.wait_ge(values_done, vals[0])
                    o = PS[0:64, 6 + me.group % 2, :].rearrange("p (a b i) -> p a b i", a=2, b=2)
                    fn(H[0:64, 6:8, qb * B:qb * B + B], o[:, :, 0, :], ACT.Copy).then_inc(me.signals(act_step), 1)
                    fn(H[64:128, 6:8, qb * B:qb * B + B], o[:, :, 1, :], ACT.Copy).then_inc(me.signals(mix_free), 1)
                    me.group += 1

            def stats(groups, eps):
                act.wait_ge(*me.last)
                for tiles in groups:
                    stat(tiles, eps)
                    act.wait_ge(normed, me.after(normed, len(tiles)))

            for n_met, (s, l) in enumerate(stages, 1):
                if s == "setup":
                    act.wait_ge(const_in, N_CONST[0])
                    for k in range(KD):
                        bank = take()
                        fn(X[:, k, :], bank, ACT.Copy).then_inc(me.signals(acc_free_act), 1)
                    for _ in HOT_CUTS:
                        me.emptied_by("dve")
                    fn(CACT, CT, ACT.Silu).then_inc(me.signals(act_step), 1)
                    act.wait_ge(acc_free_dve, me.emptied["dve"])
                    act.dma_start(SCR, VECS_SB).then_inc(table_out, 16)
                    act.wait_ge(side_dve, me.after(side_dve, 2))
                    for n in range(2):
                        fn(ROPE[:, 2 * n, :], z(24 + 3 * n), ACT.Sin).then_inc(me.signals(act_step), 1)
                        fn(ROPE[:, 2 * n + 1, :], z(23 + 3 * n), ACT.Sin).then_inc(me.signals(act_step), 1)
                elif s == "prenorm":
                    stat([X[:, k, :] for k in range(KD)], EPS6)
                    for k in range(KD):
                        act.wait_ge(normed, me.after(normed))
                        fn(H[:, k, :], H[:, k, :], ACT.Identity, bias=MOD[:, k:k + 1], scale=1.0) \
                            .then_inc(me.signals(act_step), 1)
                elif s == "postnorm":
                    stat([z(k) for k in range(KD)], EPS6)
                    act.wait_ge(normed, me.after(normed, KD))
                elif s == "ln":
                    me.emptied_by("dve")
                    act.wait_ge(normed, me.after(normed, KD))
                    stat([X[:, k, :] for k in range(KD)], EPS5)
                    for k in range(KD):
                        act.wait_ge(normed, me.after(normed))
                        fn(X[:, k, :], X[:, k, :], ACT.Identity, bias=LNG[:, 1, l, k:k + 1], scale=1.0) \
                            .then_inc(me.signals(act_step), 1)
                elif s in ("swa", "even_mix", "odd_mix"):
                    attention(steps_of(s, l))
                elif s == "ret":
                    retention()
                    stats([[H[:, 4 + t, :]] for t in range(2)], EPS6)
                elif s == "gla":
                    gla()
                    stats([[H[:, 6 + t, :]] for t in range(2)], EPS6)
                elif s == "even_sub":
                    stats([[H[:, t, :]] for t in range(4)], EPS5)
                elif s == "odd_norms":
                    stats([[z(CQ + i) for i in range(3)], [z(CKV + i) for i in range(2)]], EPS5)
                elif s == "store":
                    for n in range(8):
                        bank = take()
                        fn(z(n), bank, ACT.Copy).then_inc(me.signals(acc_free_act), 1)
                else:
                    linear(jobs_of(s, l), l)
                if s == "even_in":
                    act.wait_ge(side_dve, me.after(side_dve))
                    act.wait_ge(*me.last)
                    fn(LTMP[:, 2:4], LTMP[:, 0:2], ACT.Exp).then_inc(me.signals(side_act), 1)
                act.wait_ge(*me.last)
                act.sem_inc(act_met, 1)
                act.wait_ge(pe_met, n_met)
                act.wait_ge(dve_met, n_met)

        @block.vector
        def _(dve):
            me = Side()
            tt, ts, stt = nc.vector.tensor_tensor, nc.vector.tensor_scalar, nc.vector.scalar_tensor_tensor
            vals = [0]

            def take():
                me.emptied_by("dve")
                dve.wait_ge(acc_ready, me.job)
                return PS[:, (me.job - 1) % 2, :]

            def rope(j):
                bank, d = take(), j["of"]["dst"]
                dve.wait_ge(*me.last)
                tt(RT, bank, j["sin"], ALU.mult).then_inc(me.signals(acc_free_dve), 1)
                dve.wait_ge(*me.last)
                tt(d, d, j["cos"], ALU.mult).then_inc(me.signals(dve_step), 1)
                dve.wait_ge(*me.last)
                tt(d, d, RT, ALU.add).then_inc(me.signals(dve_step), 1)

            def linear(jobs, l):
                n = 0
                for j in jobs:
                    if j["kind"] == "C" and j["kv"] == 0 and j["h"] == 0:
                        dve.wait_ge(acc_free_act, me.emptied["act"])
                        dve.wait_ge(bias_in, BIAS_IN[1])
                        for kv in range(2):
                            for g in range(2):
                                src = z((CK, CV)[kv] + g)
                                win = bass.AP(tensor=src.tensor, offset=src.offset, ap=[list(src.ap[0]), [2, 16], [16, 31]])
                                dve.wait_ge(*me.last)
                                tt(CMPIN[:, kv, :, 31 * g:31 * g + 31], win,
                                    PLACE[:, kv, :].unsqueeze(2).broadcast_to([P, 16, 31]), ALU.add) \
                                    .then_inc(me.signals(cmp_ready if kv + g == 2 else dve_step), 1)
                    if j["by"] != "dve":
                        me.emptied_by(j["by"])
                        if j["how"] == "conv":
                            dve.wait_ge(acc_free_act, me.emptied["act"])
                            g, c, a = GPAD[:, n % 2, :], CONVED[:, n % 2, :], j["j"]
                            tap = [CONV[:, l, i, a:a + 1] for i in range(4)]
                            dve.wait_ge(*me.last)
                            ts(c, g[:, 2:T + 2], tap[2], tap[3], ALU.mult, ALU.add).then_inc(me.signals(dve_step), 1)
                            dve.wait_ge(*me.last)
                            stt(c, g[:, 1:T + 1], tap[1], c, ALU.mult, ALU.add).then_inc(me.signals(dve_step), 1)
                            dve.wait_ge(*me.last)
                            stt(c, g[:, 0:T], tap[0], c, ALU.mult, ALU.add).then_inc(me.signals(conv_ready), 1)
                        continue
                    if j["kind"] == "R":
                        rope(j)
                    elif j["kind"] == "M":
                        bank = take()
                        dve.wait_ge(*me.last)
                        tt(MOD[:, j["n0"]:j["n0"] + 4], bank[:, 0:4], BMOD[:, l, j["n0"]:j["n0"] + 4], ALU.add) \
                            .then_inc(me.signals(acc_free_dve), 1)
                    elif j["how"] == "gate":
                        bank = take()
                        dve.wait_ge(gelu_ready, me.after(gelu_ready))
                        dve.wait_ge(*me.last)
                        tt(j["dst"], bank, GELUED[:, n % 2, :], ALU.mult).then_inc(me.signals(acc_free_dve), 1)
                        n += 1
                    elif j["how"] == "res":
                        bank = take()
                        dve.wait_ge(*me.last)
                        stt(j["dst"], j["dst"], ALPHA, bank, ALU.mult, ALU.add).then_inc(me.signals(acc_free_dve), 1)

            def attention(steps):
                n, base = len(steps), me.step

                def soften(i):
                    s, r = steps[i], (base + i) % 2
                    c = 0
                    for _, keys, bias in s["segs"]:
                        me.seg += 1
                        dve.wait_ge(scores_ready, me.seg)
                        dve.wait_ge(*me.last)
                        stt(S[:, r, c:c + keys], PS[:, 2 + (me.seg - 1) % 2, 0:keys], s["scale"], bias, ALU.mult,
                            ALU.add) \
                            .then_inc(me.signals(scores_free), 1)
                        c += keys
                    if s["sink"] is not None:
                        dve.wait_ge(*me.last)
                        nc.vector.tensor_copy(S[:, r, c:c + 1], s["sink"]).then_inc(me.signals(dve_step), 1)
                        c += 1
                    dve.wait_ge(*me.last)
                    nc.vector.tensor_reduce(NMAX[:, r:r + 1], S[:, r, 0:c], AX.X, ALU.max, negate=True) \
                        .then_inc(me.signals(max_ready), 1)

                def normalise(i):
                    s, r = steps[i], (base + i) % 2
                    dve.wait_ge(exp_ready, base + i + 1)
                    dve.wait_ge(*me.last)
                    nc.vector.reciprocal(RDEN[:, r:r + 1], DEN[:, r:r + 1]).then_inc(me.signals(dve_step), 1)
                    if s["late"]:
                        dve.wait_ge(*me.last)
                        tt(RDEN[:, r:r + 1], RDEN[:, r:r + 1], LATE, ALU.mult).then_inc(me.signals(dve_step), 1)
                    e = E[:, r, 0:s["keys"]]
                    if s["factor"] is None:
                        dve.wait_ge(*me.last)
                        ts(e, e, RDEN[:, r:r + 1], None, ALU.mult).then_inc(me.signals(probs_ready), 1)
                    else:
                        dve.wait_ge(*me.last)
                        ts(e, e, RDEN[:, r:r + 1], s["factor"], ALU.mult, ALU.mult).then_inc(me.signals(probs_ready), 1)
                for i in range(n + 1):
                    if i < n:
                        soften(i)
                    if i:
                        normalise(i - 1)
                me.step += n
                vals[0] += n

            def retention():
                for h in range(4):
                    for jb in range(NB):
                        me.seg += 1
                        dve.wait_ge(scores_ready, me.seg)
                        if jb >= 2 or h:
                            if vals[0] - 1 > 0:
                                dve.wait_ge(values_done, vals[0] - 1)
                        vals[0] += 1
                        w = T - jb * B
                        dve.wait_ge(*me.last)
                        tt(E[:, jb % 2, 0:w], PS[:, 2 + (me.seg - 1) % 2, 0:w], DECAY[:, h, 0:w], ALU.mult) \
                            .then_inc(me.signals(scores_free), 1)

            def gla():
                dve.wait_ge(*me.last)
                nc.vector.tensor_copy(GTMP[0:16, :], z(GAT)[0:16, :]).then_inc(me.signals(dve_step), 1)
                dve.wait_ge(*me.last)
                nc.vector.memset(z(GAT)[0:32, :], 1.0).then_inc(me.signals(dve_step), 1)
                dve.wait_ge(*me.last)
                nc.vector.tensor_copy(z(GAT)[0:16, :], GTMP[0:16, :]).then_inc(me.signals(gla_to_pe), 1)
                bank = take()
                dve.wait_ge(*me.last)
                nc.vector.tensor_copy(z(LA), bank).then_inc(me.signals(acc_free_dve), 1)
                dve.wait_ge(*me.last)
                stt(z(TMP), z(LA), -1.0, z(LA), ALU.mult, ALU.max).then_inc(me.signals(gla_to_act), 1)
                dve.wait_ge(*me.last)
                ts(z(LA), z(LA), 0.0, None, ALU.min).then_inc(me.signals(dve_step), 1)
                dve.wait_ge(gla_act, me.after(gla_act))
                dve.wait_ge(*me.last)
                tt(z(LA), z(LA), z(TMP), ALU.subtract).then_inc(me.signals(gla_to_pe), 1)
                me.emptied_by("act")
                dve.wait_ge(acc_free_act, me.emptied["act"])
                b = z(BT)
                dve.wait_ge(*me.last)
                nc.vector.memset(BREF[:, 0:1], 0.0).then_inc(me.signals(dve_step), 1)
                dve.wait_ge(*me.last)
                nc.vector.tensor_copy(BREF[:, 1:32], b[:, 15:511:16]).then_inc(me.signals(dve_step), 1)
                dve.wait_ge(*me.last)
                tt(z(Q2).rearrange("p (a i) -> p a i", a=32), b.rearrange("p (a i) -> p a i", a=32),
                    BREF.unsqueeze(2).broadcast_to([P, 32, 16]), ALU.subtract) \
                    .then_inc(me.signals(dve_step), 1)
                k0 = 0
                for qb in range(1, NB):
                    end = b[:, qb * B - 1:qb * B]
                    dve.wait_ge(*me.last)
                    ts(z(Q1)[:, qb * B:qb * B + B], b[:, qb * B:qb * B + B], end, None, ALU.subtract) \
                        .then_inc(me.signals(dve_step), 1)
                    dve.wait_ge(*me.last)
                    ts(GK1[:, k0:k0 + qb * B], b[:, 0:qb * B], end, -1.0, ALU.subtract, ALU.mult) \
                        .then_inc(me.signals(gla_to_act if qb == NB - 1 else dve_step), 1)
                    k0 += qb * B
                dve.wait_ge(gla_act, me.after(gla_act))
                dve.wait_ge(*me.last)
                tt(z(Q1)[:, B:T], z(Q1)[:, B:T], z(GQ)[:, B:T], ALU.mult).then_inc(me.signals(dve_step), 1)
                dve.wait_ge(*me.last)
                tt(z(Q2), z(Q2), z(GQ), ALU.mult).then_inc(me.signals(dve_step), 1)
                k0 = 0
                for qb in range(1, NB):
                    dve.wait_ge(*me.last)
                    tt(GK1[:, k0:k0 + qb * B], GK1[:, k0:k0 + qb * B], z(GK)[:, 0:qb * B], ALU.mult) \
                        .then_inc(me.signals(dve_step), 1)
                    k0 += qb * B
                for qb in range(NB):
                    bb, qq, kk = (z(t)[:, qb * B:qb * B + B] for t in (BT, GQ, GK))

                    def within(x):
                        return x.rearrange("p (a c) -> p c a", a=8).unsqueeze(3).broadcast_to([P, 16, 8, 16])

                    def over(x, n):
                        return x.unsqueeze(1).broadcast_to([P, n, B])
                    prod4 = GPROD.rearrange("p c (a j) -> p c a j", a=8)
                    dve.wait_ge(*me.last)
                    tt(GK2, BREF[:, 8 * qb:8 * qb + 8].unsqueeze(2).broadcast_to([P, 8, B]), over(bb, 8),
                        ALU.subtract) \
                        .then_inc(me.signals(dve_step), 1)
                    dve.wait_ge(*me.last)
                    ts(GK2, GK2, 0.0, None, ALU.min).then_inc(me.signals(dve_step), 1)
                    dve.wait_ge(*me.last)
                    nc.vector.tensor_copy(prod4, within(bb)).then_inc(me.signals(dve_step), 1)
                    dve.wait_ge(*me.last)
                    tt(GPROD, GPROD, over(bb, 16), ALU.subtract).then_inc(me.signals(dve_step), 1)
                    dve.wait_ge(*me.last)
                    ts(GPROD, GPROD, 0.0, None, ALU.min).then_inc(me.signals(gla_to_act), 1)
                    dve.wait_ge(gla_act, me.after(gla_act))
                    dve.wait_ge(*me.last)
                    tt(GK2, GK2, over(kk, 8), ALU.mult).then_inc(me.signals(dve_step), 1)
                    dve.wait_ge(*me.last)
                    tt(GPROD, GPROD, over(kk, 16), ALU.mult).then_inc(me.signals(dve_step), 1)
                    for t, q in ((GQ1, Q1), (GQ2, Q2)):
                        if qb or q == Q2:
                            dve.wait_ge(*me.last)
                            tt(t.rearrange("p (h i) -> p h i", h=4), over(z(q)[:, qb * B:qb * B + B], 4),
                                HEADS.unsqueeze(2).broadcast_to([P, 4, B]), ALU.mult) \
                                .then_inc(me.signals(dve_step), 1)
                    dve.wait_ge(*me.last)
                    tt(prod4, prod4, within(qq), ALU.mult).then_inc(me.signals(gla_to_pe), 1)
                    for jb in range(qb):
                        me.seg += 1
                        dve.wait_ge(scores_ready, me.seg)
                        dve.wait_ge(*me.last)
                        nc.vector.tensor_copy(GS[:, jb, :], PS[:, 2 + (me.seg - 1) % 2, :]) \
                            .then_inc(me.signals(scores_free), 1)
                    own = GS[:, qb, :].rearrange("p (h i) -> p h i", h=4)
                    me.seg += 1
                    dve.wait_ge(scores_ready, me.seg)
                    dve.wait_ge(*me.last)
                    tt(own, PS[:, 2 + (me.seg - 1) % 2, :].rearrange("p (h i) -> p h i", h=4),
                        SUBM[:, 0, :].unsqueeze(1).broadcast_to([P, 4, B]), ALU.mult) \
                        .then_inc(me.signals(scores_free), 1)
                    me.seg += 1
                    dve.wait_ge(scores_ready, me.seg)
                    near = PS[:, 2 + (me.seg - 1) % 2, 0:64].rearrange("p (c h) -> p h c", h=4)
                    for h in range(4):
                        dve.wait_ge(*me.last)
                        tt(GTMP[:, h * B:h * B + B].rearrange("p (a c) -> p a c", a=8),
                            SUBM[:, 1, :].rearrange("p (a c) -> p a c", a=8), near[:, h, :].unsqueeze(1).broadcast_to([P, 8, 16]), ALU.mult) \
                            .then_inc(me.signals(scores_free if h == 3 else dve_step), 1)
                    dve.wait_ge(*me.last)
                    tt(GS[:, qb, :], GS[:, qb, :], GTMP, ALU.add).then_inc(me.signals(gla_to_pe), 1)
                    vals[0] += 1
                    dve.wait_ge(values_done, vals[0])

            def scaled(tiles, gains, gates=None):
                dve.wait_ge(rstd_ready, me.after(rstd_ready))
                for n, t in enumerate(tiles):
                    if gates:
                        if gains is None:
                            dve.wait_ge(*me.last)
                            tt(t, t, RS, ALU.mult).then_inc(me.signals(dve_step), 1)
                        else:
                            dve.wait_ge(*me.last)
                            stt(t, t, gains[n], RS, ALU.mult, ALU.mult).then_inc(me.signals(dve_step), 1)
                        dve.wait_ge(*me.last)
                        tt(t, t, gates[n], ALU.mult).then_inc(me.signals(normed), 1)
                    else:
                        dve.wait_ge(*me.last)
                        stt(t, t, gains[n], RS, ALU.mult, ALU.mult).then_inc(me.signals(normed), 1)

            def angles():
                whole, parts = 12582912.0, (6.28125, 0.0019350051879882812, 3.01991605e-7)
                dve.wait_ge(*me.last)
                nc.vector.tensor_copy(z(29), z(22).bitcast(I32)).then_inc(me.signals(dve_step), 1)
                for n in range(2):
                    r, c, turns = z(23 + 3 * n), z(24 + 3 * n), z(25 + 3 * n)
                    dve.wait_ge(*me.last)
                    ts(r, z(29), FREQ[:, n:n + 1], None, ALU.mult).then_inc(me.signals(dve_step), 1)
                    dve.wait_ge(*me.last)
                    ts(turns, r, float(1 / (2 * np.pi)), whole, ALU.mult, ALU.add).then_inc(me.signals(dve_step), 1)
                    dve.wait_ge(*me.last)
                    ts(turns, turns, whole, None, ALU.subtract).then_inc(me.signals(dve_step), 1)
                    for part in parts:
                        dve.wait_ge(*me.last)
                        stt(r, turns, -part, r, ALU.mult, ALU.add).then_inc(me.signals(dve_step), 1)
                    dve.wait_ge(*me.last)
                    ts(r, r, 3.1415925, -3.1415925, ALU.min, ALU.max).then_inc(me.signals(dve_step), 1)
                    dve.wait_ge(*me.last)
                    stt(c, r, -1.0, r, ALU.mult, ALU.min) \
                        .then_inc(me.signals(dve_step), 1)
                    dve.wait_ge(*me.last)
                    ts(c, c, float(np.pi / 2), None, ALU.add).then_inc(me.signals(side_dve if n else dve_step), 1)

            for n_met, (s, l) in enumerate(stages, 1):
                if s == "setup":
                    dve.wait_ge(const_in, N_CONST[0])
                    nc.vector.memset(EPS6, 1e-6).then_inc(me.signals(dve_step), 1)
                    dve.wait_ge(*me.last)
                    nc.vector.memset(EPS5, 1e-5).then_inc(me.signals(dve_step), 1)
                    dve.wait_ge(*me.last)
                    nc.vector.memset(ONE, 1.0).then_inc(me.signals(dve_step), 1)
                    dve.wait_ge(*me.last)
                    nc.vector.memset(TABLE[32:33, :], NEG).then_inc(me.signals(side_dve), 1)
                    angles()
                    for _ in range(KD):
                        me.emptied_by("act")
                    for c, w in HOT_CUTS:
                        bank = take()
                        dve.wait_ge(*me.last)
                        nc.vector.tensor_copy(VECS_SB[:, c:c + w], bank[0:16, 0:w]) \
                            .then_inc(me.signals(acc_free_dve), 1)
                    dve.wait_ge(*me.last)
                    dve.wait_ge(table_out, 16)
                elif s == "prenorm":
                    dve.wait_ge(*me.last)
                    stt(GA, MOD[:, 8:16], 1.0, GAIN[:, 0, l, :], ALU.add, ALU.mult).then_inc(me.signals(dve_step), 1)
                    dve.wait_ge(*me.last)
                    tt(GB, MOD[:, 16:24], GAIN[:, 1, l, :], ALU.mult).then_inc(me.signals(dve_step), 1)
                    me.emptied_by("act")
                    dve.wait_ge(rstd_ready, me.after(rstd_ready))
                    for k in range(KD):
                        dve.wait_ge(*me.last)
                        stt(H[:, k, :], X[:, k, :], GA[:, k:k + 1], RS, ALU.mult, ALU.mult) \
                            .then_inc(me.signals(normed), 1)
                elif s == "postnorm":
                    me.emptied_by("act")
                    scaled([z(k) for k in range(KD)], [GB[:, k:k + 1] for k in range(KD)])
                    for k in range(KD):
                        dve.wait_ge(*me.last)
                        tt(X[:, k, :], X[:, k, :], z(k), ALU.add).then_inc(me.signals(dve_step), 1)
                elif s == "ln":
                    bank = take()
                    for k in range(KD):
                        dve.wait_ge(*me.last)
                        tt(X[:, k, :], X[:, k, :], bank, ALU.subtract).then_inc(me.signals(normed), 1)
                    dve.wait_ge(*me.last)
                    nc.vector.tensor_copy(TINY[:, 120:121], bank[:, 0:1]).then_inc(me.signals(acc_free_dve), 1)
                    me.emptied_by("act")
                    scaled([X[:, k, :] for k in range(KD)], [LNG[:, 0, l, k:k + 1] for k in range(KD)])
                elif s in ("swa", "even_mix", "odd_mix"):
                    if s != "swa":
                        dve.wait_ge(bias_in, BIAS_IN[0 if s == "even_mix" else 1])
                    attention(steps_of(s, l))
                elif s == "ret":
                    for k in range(4):
                        dve.wait_ge(*me.last)
                        tt(H[:, k, :], H[:, k, :], z(AG + k), ALU.mult).then_inc(me.signals(dve_step), 1)
                    retention()
                    for t in range(2):
                        me.emptied_by("act")
                        scaled([H[:, 4 + t, :]], None, [z(RG + t)])
                elif s == "gla":
                    gla()
                    for t in range(2):
                        me.emptied_by("act")
                        scaled([H[:, 6 + t, :]], [GLAG[:, l:l + 1]], [z(GG + t)])
                elif s == "even_sub":
                    for t in range(4):
                        me.emptied_by("act")
                        scaled([H[:, t, :]], [SUBG])
                elif s == "odd_norms":
                    for t, n, g in ((CQ, 3, QG), (CKV, 2, KVG)):
                        me.emptied_by("act")
                        scaled([z(t + i) for i in range(n)], [g[:, i:i + 1] for i in range(n)])
                elif s == "store":
                    for _ in range(8):
                        me.emptied_by("act")
                else:
                    if s == "up":
                        dve.wait_ge(*me.last)
                        nc.vector.memset(GPAD[:, :, 0:2], 0.0).then_inc(me.signals(dve_step), 1)
                    if s in ("odd_in", "odd_up"):
                        dve.wait_ge(bias_in, BIAS_IN[1])
                    linear(jobs_of(s, l), l)
                if s == "even_in":
                    lp = LAMP.rearrange("p (a b d) -> p a b d", a=2, b=2)
                    prod = RT[:, 0:128].rearrange("p (a d) -> p a d", a=2)
                    dve.wait_ge(*me.last)
                    tt(prod, lp[:, :, 0, :], lp[:, :, 1, :], ALU.mult).then_inc(me.signals(dve_step), 1)
                    dve.wait_ge(*me.last)
                    nc.vector.tensor_reduce(LTMP[:, 0:2], prod, AX.X, ALU.add).then_inc(me.signals(side_dve), 1)
                    dve.wait_ge(side_act, me.after(side_act))
                    dve.wait_ge(*me.last)
                    tt(LAM, LTMP[:, 3:4], LTMP[:, 2:3], ALU.subtract).then_inc(me.signals(dve_step), 1)
                    dve.wait_ge(*me.last)
                    ts(LAM, LAM, LAM_INIT, None, ALU.subtract).then_inc(me.signals(dve_step), 1)
                    dve.wait_ge(*me.last)
                    ts(SUBG, SUBG, 1.0 - LAM_INIT, None, ALU.mult).then_inc(me.signals(dve_step), 1)
                dve.wait_ge(*me.last)
                dve.sem_inc(dve_met, 1)
                dve.wait_ge(pe_met, n_met)
                dve.wait_ge(act_met, n_met)


_INS = ["x", "c", "positions", "w_mod", "b_mod", "pre_norm_gain", "post_norm_gain", "w_in", "attn_sinks", "gla_gate_w",
        "gla_gate_b", "gla_norm_gain", "w_out", "rel_bias_2", "ev_w_in_2", "ev_w_out_2", "ev_lambda_2", "ev_subln_2",
        "od_w_in_2", "od_w_out_2", "od_cmp_pe_2", "od_cmp_w1_2", "od_cmp_w2_2", "od_q_norm_2", "od_kv_norm_2", "od_w_uq_2",
        "od_w_uk_2", "od_w_uv_2", "ffn_w_up_2", "ffn_conv_w_2", "ffn_conv_b_2", "ffn_w_down_2", "ln_g_2", "ln_b_2"]


def kernel(**inputs):
    import concourse.bacc as _bacc
    from concourse.bass_utils import run_bass_kernel_spmd as _run

    nc = _bacc.Bacc("TRN2", target_bir_lowering=False, num_devices=1)
    arrays, io, cst = {}, {}, {}
    for name in _INS:
        a = np.ascontiguousarray(inputs[name])
        arrays["in_" + name] = a
        io[name] = nc.dram_tensor("in_" + name, a.shape, mybir.dt.from_np(a.dtype), kind="ExternalInput").ap()
    for name, a in constants().items():
        arrays["cst_" + name] = a
        cst[name] = nc.dram_tensor("cst_" + name, a.shape, F32, kind="ExternalInput").ap()
    out = nc.dram_tensor("out", [T, D], F32, kind="ExternalOutput").ap()
    build(nc, io, cst, out)
    r = _run(nc, [arrays], core_ids=[0])
    return r.results[0]["out"].reshape(1, T, D)
```

```python
from contextlib import ExitStack

import numpy as np

import concourse.bass as bass
from concourse import mybir

F32 = mybir.dt.float32
I32 = mybir.dt.int32
ACT = mybir.ActivationFunctionType
ALU = mybir.AluOpType
AX = mybir.AxisListType

P = 128
T = 512
B = 128
NB = T // B
D = 1024
KD = D // P
NEG = -1e30
LAYERS = 2
D_IN = 3088
DFF = 2816
NF = DFF // P
ALPHA = (2 * LAYERS) ** 0.25
LAM_INIT = 0.8 - 0.6
SLOTS = 8
HSPAN = 896
BUCKETS = 32
WIDEST = 1280

NTILES = 34


def t5_bucket(dist):
    n = np.maximum(dist, 0)
    nf = np.maximum(n, 1).astype(np.float32)
    large = 16 + (np.log(nf / np.float32(16)) / np.float32(np.log(2048 / 16)) * np.float32(16)).astype(np.int32)
    return np.where(n < 16, n, np.minimum(large, 31))


VECS = [(-511, 511, lambda d: d >= 0), (-127, 255, lambda d: (d >= 0) & (d <= 128)),
        (-127, 511, lambda d: (d >= 0) & (d % 4 == 0)), (-127, 511, lambda d: (d >= 0) & (d % 16 == 0))]
VEC_AT = np.cumsum([0] + [b - a + 1 for a, b, _ in VECS])
VEC_LEN = int(VEC_AT[-1])


def constants():
    f = np.float32
    out = {}
    eye = np.eye(P)
    rot = np.zeros((2, P, P))
    for n, half in enumerate((32, 16)):
        for m in range(P):
            if m % (2 * half) < half:
                rot[n, m + half, m] = -1
            else:
                rot[n, m - half, m] = 1
    ones = np.ones((P, P))
    pair = np.kron(np.eye(2), np.ones((64, 64))) / 64
    out["mats"] = np.stack([eye, rot[0], rot[1], ones / 1024, pair, ones / 128, ones / 384, ones / 256], 1)
    p = np.arange(P)
    freq = np.stack([10000.0 ** (-(p % 32) * 2 / 64), 1 / 10000.0 ** ((p % 32) / 31), np.zeros(P) + (p >= 31)], 1)
    out["freq"] = freq
    inv = (f(10000.0) ** (-np.arange(16, dtype=f) / f(16))).astype(f)[p % 16]
    ang = (np.arange(T, dtype=f)[None] * inv[:, None]).astype(f).astype(np.float64)
    out["mla_rope"] = np.stack([np.cos(ang), np.sin(ang)], 1)
    j, i = np.arange(P)[:, None], np.arange(T)[None]
    gam = 1 - 2.0 ** (-5 - np.arange(4))
    out["decay"] = np.stack([np.where(i >= j, g ** np.maximum(i - j, 0), 0) / 8 for g in gam], 1)
    out["upper"] = (i >= j) / 16.0
    q, c = np.arange(P)[:, None], np.arange(2 * B)[None]
    rel = q + B - c
    out["window"] = np.where((rel >= 0) & (rel < 128), 0, NEG)
    out["causal"] = np.where(q + np.arange(T)[None] - 127 >= 0, 0, NEG)
    j, i = np.arange(P)[:, None], np.arange(P)[None]
    out["sub"] = np.stack([(j // 16 < i // 16), (j // 16 == i // 16) & (i >= j)], 1)
    out["heads"] = (p[:, None] // 32 == np.arange(4)[None])
    hot = []
    for a, b, ok in VECS:
        d = np.arange(a, b + 1)
        h = np.zeros((BUCKETS + 1, len(d)))
        h[np.where(ok(d), t5_bucket(d), BUCKETS), np.arange(len(d))] = 1
        hot.append(h)
    out["onehot"] = np.concatenate(hot, 1)
    return {k: np.ascontiguousarray(v, dtype=f) for k, v in out.items()}


class Side:

    def __init__(self):
        self.given, self.taken, self.last = {}, {}, None
        self.job = self.seg = self.turn = self.group = self.sq = self.step = 0
        self.emptied = {"act": 0, "dve": 0}
        self.first = self.depth = 0

    def signals(self, sem):
        self.given[id(sem)] = self.given.get(id(sem), 0) + 1
        self.last = (sem, self.given[id(sem)])
        return sem

    def after(self, sem, n=1):
        self.taken[id(sem)] = self.taken.get(id(sem), 0) + n
        return self.taken[id(sem)]

    def emptied_by(self, by):
        self.emptied[by] += 1
        self.job += 1

    def begins(self, depth):
        self.first, self.depth = self.job, depth

    def bank(self):
        return (self.job - 1 - self.first) % self.depth


def build(nc, io, cst, out, stop=None):
    ctx = ExitStack()
    with ctx:
        def sb(name, shape):
            return ctx.enter_context(nc.sbuf_tensor(name, [P] + shape, F32))

        X = sb("X", [KD, T])
        H = sb("H", [KD, T])
        Z = sb("Z", [NTILES, T])
        RING = sb("RING", [SLOTS, 8, P])
        BIAS = sb("BIAS", [8 * HSPAN])
        S = sb("S", [2, WIDEST])
        E = sb("E", [2, WIDEST])
        ET = sb("ET", [2, WIDEST // B, B])
        MATS = sb("MATS", [8, P])
        SMALL = sb("SMALL", [1000])
        VECTORS = [[(0, 8, io["c"].rearrange("o (k p) -> (o k) p", p=P)),
                    (8, 48, io["b_mod"].rearrange("l (k p) -> (l k) p", p=P))],
                   [(56, 16, io["pre_norm_gain"].rearrange("l (k p) -> (l k) p", p=P)),
                    (72, 16, io["post_norm_gain"].rearrange("l (k p) -> (l k) p", p=P)),
                    (88, 32, io["ln_g_2"].rearrange("l a (k p) -> (l a k) p", p=P)),
                    (120, 3, io["od_q_norm_2"].rearrange("o (k p) -> (o k) p", p=P)),
                    (123, 2, io["od_kv_norm_2"].rearrange("o (k p) -> (o k) p", p=P)),
                    (125, 1, io["ev_subln_2"])],
                   [(126, 32, io["ln_b_2"].rearrange("l a (k p) -> (l a k) p", p=P)),
                    (158, 44, io["ffn_conv_b_2"].rearrange("l (k p) -> (l k) p", p=P)),
                    (202, 32, io["od_cmp_pe_2"][0].rearrange("kv (l two) d -> (kv l) (two d)", two=2))],
                   [(234, 66, io["ffn_conv_w_2"][0].rearrange("a (k p) -> (a k) p", p=P))],
                   [(300, 66, io["ffn_conv_w_2"][1].rearrange("a (k p) -> (a k) p", p=P))]]
        VEC = sb("VEC", [366])
        TINY = sb("TINY", [160])
        PS = ctx.enter_context(nc.psum_tensor("PS", [P, 8, T], F32))
        SCR = nc.dram_tensor("bias_vectors", [16, VEC_LEN], F32, kind="Internal").ap()

        IDN, ROT64, ROT32, ONES_D, ONES_64, ONES_128, ONES_384, ONES_256 = (MATS[:, i, :] for i in range(8))
        EPS6, EPS5, ONE = TINY[:, 0:1], TINY[:, 1:2], TINY[:, 2:3]
        FREQ, LATE = TINY[:, 4:6], TINY[:, 6:7]
        NMAX, DEN, RDEN = TINY[:, 104:108], TINY[:, 108:112], TINY[:, 112:116]
        GLAG, LAM, LTMP = TINY[:, 14:16], TINY[:, 17:18], TINY[:, 20:24]
        CT, CACT = VEC[:, 0:8], TINY[:, 56:64]
        BMOD, LNG, LNB, CONVB = (VEC[:, c0:c0 + a * n].rearrange("p (a k) -> p a k", a=a)
                                 for c0, a, n in ((8, LAYERS, 24), (88, 4, KD), (126, 4, KD), (158, LAYERS, NF)))
        PREG, POSTG = (VEC[:, c0:c0 + 16].rearrange("p (l k) -> p l k", l=LAYERS) for c0 in (56, 72))
        CONVW = VEC[:, 234:366].rearrange("p (l a k) -> p l a k", l=LAYERS, a=3)
        QG, KVG, SUBG = VEC[:, 120:123], VEC[:, 123:125], VEC[:, 125:126]
        PLACE = VEC[:, 202:234].rearrange("p (a l) -> p a l", a=2)
        VROWS = S.rearrange("p a t -> p (a t)")
        SINKS = TINY[:, 32:48]
        MOD = TINY[:, 64:88], TINY[:, 128:152]
        GA, GB = TINY[:, 88:96], TINY[:, 96:104]

        DECAY = BIAS[:, 0:2048].rearrange("p (h i) -> p h i", h=4)
        UPPER = BIAS[:, 2048:2560]
        WINDOW = BIAS[:, 2560:2816]
        SUBM = BIAS[:, 2816:3072].rearrange("p (a i) -> p a i", a=2)
        HEADS = BIAS[:, 3072:3076]
        BREF = BIAS[:, 3076:3108]
        ROPE = BIAS[:, 3584:5632].rearrange("p (a t) -> p a t", a=4)
        GK1 = BIAS[:, 5632:6400]
        BFULL4 = BIAS[:, 0:2048].rearrange("p (h x) -> p h x", h=4)
        BD4 = BIAS[:, 3072:5120].rearrange("p (h x) -> p h x", h=4)
        BWIN = BIAS[:, 2048:3072].rearrange("p (h x) -> p h x", h=4)
        BD16 = BIAS[:, 5120:7168].rearrange("p (h x) -> p h x", h=4)
        BFULL8 = BIAS[:, :].rearrange("p (h x) -> p h x", h=8)
        TABLE = SMALL[0:33, 0:16]
        GWB = [SMALL[0:17, 32 + 128 * l:160 + 128 * l] for l in range(LAYERS)]
        LAMP = SMALL[:, 600:856]
        CAUSAL = SMALL[:, 0:512]
        KCT = SMALL[:, 512:574]
        VC = SMALL[0:31, 576:704].rearrange("p (g d) -> p g d", g=2)
        H1 = SMALL[:, 704:828].rearrange("p (h c) -> p h c", h=2)
        GATES = SMALL[:, 860:956]
        def rings(depth):
            if depth == 2:
                return S, E, ET
            return (S.rearrange("p a t -> p (a t)").rearrange("p (r t) -> p r t", r=depth),
                    E.rearrange("p a t -> p (a t)").rearrange("p (r t) -> p r t", r=depth),
                    ET.rearrange("p a b q -> p (a b) q").rearrange("p (r b) q -> p r b q", r=depth))
        SQ = S[:, 0, 0:1024].rearrange("p (a t) -> p a t", a=2)
        RS = S[:, 1, 0:512]
        RT = S[:, 1, 512:1024]
        GPAD = E[:, 0, 0:1032].rearrange("p (a t) -> p a t", a=2)
        CONVED = E[:, 1, 0:1024].rearrange("p (a t) -> p a t", a=2)
        GELUED = ET[:, 0, 0:8, :].rearrange("p (a b) q -> p a (b q)", a=2)
        MROPE = ET[:, 1, 0:8, :].rearrange("p (a b) q -> p a (b q)", a=2)
        CMPIN = E[:, :, :].rearrange("p a t -> p (a t)")[:, 0:1984].rearrange("p (a l c) -> p a l c", a=2, l=16)

        def z(i, n=1):
            return Z[:, i, :] if n == 1 else Z[:, i:i + n, :].rearrange("p a t -> p (a t)")

        def ztok(i, tt, c0, n):
            return Z[:, i, tt * P + c0:tt * P + c0 + n]

        XIN = Z[:, 0:8, :].rearrange("p (b a) t -> p b (a t)", b=NB)
        HOT, VECS_SB = z(10, 6)[0:33, 0:VEC_LEN], z(16, 6)[0:16, 0:VEC_LEN]
        HOT_CUTS = [(c, min(T, VEC_LEN - c)) for c in range(0, VEC_LEN, T)]
        GK2 = z(0, 2).rearrange("p (s j) -> p s j", s=8)
        GPROD = z(2, 4).rearrange("p (c j) -> p c j", c=16)
        GQ1, GQ2 = z(10), z(11)
        GS, GTMP = Z[:, 6:10, :], z(33)

        def sem(name):
            return ctx.enter_context(nc.semaphore(name))

        pe_step, act_step, dve_step = sem("pe_step"), sem("act_step"), sem("dve_step")
        pe_met, act_met, dve_met = sem("pe_met"), sem("act_met"), sem("dve_met")
        const_in, x_in, table_out, bias_in, stored = (sem(n) for n in ("const_in", "x_in", "table_out", "bias_in", "stored"))
        mod_dve, mod_pool, pool_step = sem("mod_dve"), sem("mod_pool"), sem("pool_step")
        first_in, rows_in, c_ready, one_set = sem("first_in"), sem("rows_in"), sem("c_ready"), sem("one_set")
        loaded = [sem(f"loaded{i}") for i in range(SLOTS)]
        acc_ready, acc_free_act, acc_free_dve = sem("acc_ready"), sem("acc_free_act"), sem("acc_free_dve")
        scores_ready, scores_free, max_ready = sem("scores_ready"), sem("scores_free"), sem("max_ready")
        exp_ready, probs_ready, turned, turn_free = sem("exp_ready"), sem("probs_ready"), sem("turned"), sem("turn_free")
        values_done, mix_free = sem("values_done"), sem("mix_free")
        sq_ready, sq_used, rstd_ready, normed = sem("sq_ready"), sem("sq_used"), sem("rstd_ready"), sem("normed")
        gla_to_act, gla_to_pe, gla_act = sem("gla_to_act"), sem("gla_to_pe"), sem("gla_act")
        conv_ready, gelu_ready, cmp_ready = sem("conv_ready"), sem("gelu_ready"), sem("cmp_ready")
        side_dve, side_act = sem("side_dve"), sem("side_act")

        def cols(w, c0, n, k0=0, nk=KD):
            return (0, n, nk, w[k0 * P:(k0 + nk) * P, c0:c0 + n].rearrange("(k p) n -> p k n", p=P))

        def at(part, d0):
            return (d0,) + part[1:]

        def job(kind, chunks, src, dst, how="copy", by="act", m=P, **more):
            return dict(kind=kind, chunks=chunks, src=src, dst=dst, how=how, by=by, m=m, **more)

        def feat(w, c0, src, dst, m=P, nk=KD, **more):
            chunks = [[cols(w, c0, m, k0, min(8, nk - k0))] for k0 in range(0, nk, 8)]
            return job("F", chunks, src, dst, m=m, **more)

        def tok(w, c0, src, dst, m=P, nk=KD, **more):
            return job("T", [[cols(w, c0, m, 0, nk)]], src, dst, m=m, **more)

        def twice(w, c0, src, dst, **more):
            part = cols(w, c0, 64)
            return job("F", [[part, at(part, 64)]], src, dst, **more)

        def with_rope(jobs, rot, cos, sin):
            got = []
            for n, j in enumerate(jobs):
                got.append(j)
                if n:
                    got.append(dict(kind="R", chunks=[], of=jobs[n - 1], rot=rot, cos=cos, sin=sin, by="dve"))
            got.append(dict(kind="R", chunks=[], of=jobs[-1], rot=rot, cos=cos, sin=sin, by="dve"))
            for n, g in enumerate(got):
                if g["kind"] == "R":
                    g["back"] = n - max(k for k in range(n) if got[k] is g["of"])
            return got

        def hsrc(k):
            return H[:, k, :]

        def xsrc(k):
            return X[:, k, :]

        PAIRS = RING.rearrange("p s k n -> p (s k n)").rearrange("p (s k n) -> p s k n", s=SLOTS // 2, k=8)

        MACC = E.rearrange("p a t -> p (a t)")[:, 0:1024].rearrange("p (a n) -> p a n", a=4)

        def mod_jobs(l, n):
            w = io["w_mod"][l]
            return [dict(kind="M", by="dve", how="mod", layer=l, n0=g, n=n, wide=(n == 2), turn=g // n % 4,
                         maker="dve" if n == 2 and g // 2 % 2 == 0 else "pool",
                         chunks=[[cols(w, g * P, n * P)]]) for g in range(0, 24, n)]

        def between(jobs, others):
            got, others = [], list(others)
            for j in jobs:
                got.append(j)
                if j["chunks"] and others:
                    got.append(others.pop(0))
            got += others
            for n, g in enumerate(got):
                if g["kind"] == "R":
                    g["back"] = n - max(k for k in range(n) if got[k] is g["of"])
            return got

        AQ, AK, RQ, RK, AG, RG, GG, GQ, GK, AV, RV, GV, GAT, BT, Q1, Q2, LA, TMP = (
            0, 4, 6, 8, 10, 14, 16, 18, 19, 20, 21, 23, 25, 26, 27, 28, 31, 32)

        def first_jobs(l):
            w = io["w_in"][l]
            jobs = with_rope([feat(w, 128 * i, hsrc, z(AQ + i)) for i in range(4)]
                             + [twice(w, 512 + 64 * g, hsrc, z(AK + g)) for g in range(2)],
                             ROT64, ROPE[:, 0, :], ROPE[:, 1, :])
            jobs += with_rope([feat(w, 1280 + 128 * i, hsrc, z(RQ + i)) for i in range(4)],
                              ROT64, ROPE[:, 2, :], ROPE[:, 3, :])
            jobs += [tok(w, 640, hsrc, z(AV))]
            jobs += [tok(w, 1792 + 128 * i, hsrc, z(RV + i)) for i in range(2)]
            jobs += [tok(w, 2560 + 128 * i, hsrc, z(GV + i)) for i in range(2)]
            jobs += [feat(w, 2304, hsrc, z(GQ), scale=32 ** -0.5), feat(w, 2432, hsrc, z(GK))]
            jobs += [feat(w, 3072, hsrc, Z[0:16, GAT, :], m=16)]
            jobs += [feat(w, 768 + 128 * i, hsrc, z(AG + i), how="silu") for i in range(4)]
            jobs += [feat(w, 2048 + 128 * i, hsrc, z(RG + i), how="silu") for i in range(2)]
            jobs += [feat(w, 2816 + 128 * i, hsrc, z(GG + i), how="silu") for i in range(2)]
            return between(jobs, mod_jobs(l + 1, 1)) if l + 1 < LAYERS else jobs

        def out_jobs(w, nk, how):
            if how == "copy":
                return [feat(w, 128 * n, hsrc, z(n), nk=nk) for n in range(KD)]
            return [feat(w, 128 * n, hsrc, X[:, n, :], nk=nk, how="res", by="dve") for n in range(KD)]

        QA, KA, VA, BQ, BK, BV = 0, 4, 8, 12, 18, 24

        def even_jobs():
            w = io["ev_w_in_2"][0]
            jobs = [feat(w, 128 * i, xsrc, z(QA + i)) for i in range(4)]
            jobs += [feat(w, 512 + 128 * i, xsrc, z(KA + i)) for i in range(4)]
            jobs += [tok(w, 1024 + 128 * i, xsrc, z(VA + i)) for i in range(4)]
            for br in range(3):
                jobs += [feat(w, 1536 + 768 * br + 128 * i, xsrc, z(BQ + 2 * br + i)) for i in range(2)]
                jobs += [feat(w, 1792 + 768 * br + 128 * i, xsrc, z(BK + 2 * br + i)) for i in range(2)]
                jobs += [tok(w, 2048 + 768 * br + 128 * i, xsrc, z(BV + 2 * br + i)) for i in range(2)]
            return jobs

        CQT, SK, WK, SV, WV, CQ, CKV, KR, QN, QR, KN, MV, CK, CV = 0, 4, 6, 8, 9, 10, 13, 15, 16, 20, 22, 26, 30, 32

        def odd_jobs():
            w = io["od_w_in_2"][0]
            jobs = []
            for kv, d in ((0, CK), (1, CV)):
                jobs += [twice(w, 512 + kv * 128 + g * 64, xsrc, z(d + g), how="shift") for g in range(2)]
            jobs += [feat(w, 128 * i, xsrc, z(CQT + i)) for i in range(4)]
            for br, d in ((1, SK), (2, WK)):
                jobs += [twice(w, 512 + br * 256 + g * 64, xsrc, z(d + g)) for g in range(2)]
            jobs += [tok(w, 512 + 256 + 128, xsrc, z(SV)), tok(w, 512 + 512 + 128, xsrc, z(WV))]
            jobs += [tok(w, 1280, xsrc, GATES, m=24, how="sigmoid")]
            jobs += [feat(w, 1304 + 128 * i, xsrc, z(CQ + i)) for i in range(3)]
            jobs += [feat(w, 1688 + 128 * i, xsrc, z(CKV + i)) for i in range(2)]
            part = cols(w, 1944, 32)
            return jobs + with_rope([job("F", [[at(part, 32 * i) for i in range(4)]], xsrc, z(KR))], ROT32,
                                    MROPE[:, 0, :], MROPE[:, 1, :])

        def cmp_jobs():
            got = []
            for kv in range(2):
                w1 = io["od_cmp_w1_2"][0, kv]
                for h in range(2):
                    got.append(dict(kind="C", by="act", how="gelu", kv=kv, h=h,
                                    chunks=[[cols(w1, 128 * h, P, 0, 8)], [cols(w1, 128 * h, P, 8, 8)]]))
                part = cols(io["od_cmp_w2_2"][0, kv], 0, 64, 0, 2)
                got.append(dict(kind="C2", by="act", how="kct" if kv == 0 else "vc", kv=kv, back=1,
                                chunks=[[part, at(part, 64)] if kv == 0 else [part]]))
            return got

        def mla_jobs():
            wq, wk, wv = io["od_w_uq_2"][0], io["od_w_uk_2"][0], io["od_w_uv_2"][0]

            def csrc(k):
                return z(CQ + k)

            def ksrc(k):
                return z(CKV + k)
            jobs = with_rope([job("F", [[at(cols(wq, (4 * t + i) * 96 + 64, 32, 0, 3), 32 * i) for i in range(4)]],
                                  csrc, z(QR + t)) for t in range(2)], ROT32, MROPE[:, 0, :], MROPE[:, 1, :])
            jobs += [job("F", [[at(cols(wq, (2 * t + i) * 96, 64, 0, 3), 64 * i) for i in range(2)]], csrc, z(QN + t))
                     for t in range(4)]
            jobs += [feat(wk, 128 * t, ksrc, z(KN + t), nk=2) for t in range(4)]
            jobs += [tok(wv, 128 * t, ksrc, z(MV + t), nk=2) for t in range(4)]
            return jobs

        def up_jobs(l):
            w = io["ffn_w_up_2"][l]
            jobs = []
            for j in range(NF):
                jobs.append(feat(w, DFF + 128 * j, xsrc, None, how="conv", j=j))
                jobs.append(feat(w, 128 * j, xsrc, z(j), how="gate", by="dve", j=j))
            return jobs

        def down_jobs(l):
            w = io["ffn_w_down_2"][l]
            return [feat(w, 128 * n, z, X[:, n, :], nk=NF, how="res", by="dve") for n in range(KD)]

        def half(tile, h, t0, n):
            return Z[64 * (h % 2):64 * (h % 2) + 64, tile, t0:t0 + n]

        def hout(tile, h, b):
            return H[64 * (h % 2):64 * (h % 2) + 64, tile, b * B:b * B + B]

        def step(segs, values, dst, first, last, scale, sink=None, factor=None, late=False):
            return dict(segs=segs, values=values, dst=dst, first=first, last=last, scale=scale, sink=sink,
                        factor=factor, late=late, keys=sum(n for _, n, _ in segs))

        def back(view, x, n, stride=1):
            end = x - stride * n
            return view[:, x:(end if end >= 0 else None):-stride]

        def swa_steps(l):
            got = []
            for h in range(8):
                for b in range(NB):
                    k0 = max(0, b - 1)
                    n = (b + 1 - k0) * B
                    p0 = 64 * (h % 2)
                    seg = ([(half(AQ + h // 2, h, b * B, B), Z[p0:p0 + 64, AK + h // 4, k0 * B:k0 * B + n])], n,
                           WINDOW[:, 2 * B - n:2 * B])
                    vals = [ztok(AV, kb, 64 * (h // 4), 64) for kb in range(k0, b + 1)]
                    got.append(step([seg], vals, hout(h // 2, h, b), True, True, 64 ** -0.5,
                                    sink=SINKS[:, 8 * l + h:8 * l + h + 1]))
            return got

        def even_steps():
            got = []
            for h in range(4):
                for b in range(NB):
                    n = (b + 1) * B
                    for m in range(2):
                        t = 2 * m + h // 2
                        seg = ([(half(QA + t, h, b * B, B), half(KA + t, h, 0, n))], n, back(BFULL4[:, h, :], b * B + 127, n))
                        vals = [ztok(VA + h, kb, 0, P) for kb in range(b + 1)]
                        got.append(step([seg], vals, H[:, h, b * B:b * B + B], m == 0, m == 1, 64 ** -0.5,
                                        factor=LAM if m else None))
            for h in range(4):
                for b in range(NB):
                    segs, vals = [], []
                    for br, view in ((0, BWIN), (1, BD4), (2, BD16)):
                        k0 = max(0, b - 1) if br == 0 else 0
                        n = (b + 1 - k0) * B
                        segs.append(([(half(BQ + 2 * br + h // 2, h, b * B, B), half(BK + 2 * br + h // 2, h, k0 * B, n))],
                                     n, back(view[:, h, :], (b - k0) * B + 127, n)))
                        vals += [ztok(BV + 2 * br + h // 2, kb, 64 * (h % 2), 64) for kb in range(k0, b + 1)]
                    got.append(step(segs, vals, hout(4 + h // 2, h, b), True, True, 64 ** -0.5))
            return got

        def odd_steps():
            got = []
            for h in range(8):
                g, p0 = h // 4, 64 * (h % 2)
                for b in range(NB):
                    n = (b + 1) * B
                    q = half(CQT + h // 2, h, b * B, B)

                    def gate(br):
                        return GATES[:, b * 24 + br * 8 + h:b * 24 + br * 8 + h + 1]
                    seg = ([(q, KCT[p0:p0 + 64, 31 * g:31 * g + 31])], 31, back(BFULL8[:, h, :], B * b + 480, 31, 16))
                    got.append(step([seg], [VC[:, g, :]], None, True, False, 64 ** -0.5, factor=gate(0), late=b == 0))
                    for br, kt, vt in ((1, SK, SV), (2, WK, WV)):
                        seg = ([(q, Z[p0:p0 + 64, kt + g, 0:n])], n, back(BFULL8[:, h, :], B * b + 511, n))
                        vals = [ztok(vt, kb, 64 * g, 64) for kb in range(b + 1)]
                        got.append(step([seg], vals, hout(h // 2, h, b), False, br == 2, 64 ** -0.5, factor=gate(br)))
            for h in range(8):
                r0 = 32 * (h % 4)
                for b in range(NB):
                    n = (b + 1) * B
                    seg = ([(half(QN + h // 2, h, b * B, B), half(KN + h // 2, h, 0, n)),
                            (Z[r0:r0 + 32, QR + h // 4, b * B:b * B + B], Z[r0:r0 + 32, KR, 0:n])],
                           n, back(CAUSAL, b * B + 127, n))
                    vals = [ztok(MV + h // 2, kb, 64 * (h % 2), 64) for kb in range(b + 1)]
                    got.append(step([seg], vals, hout(4 + h // 2, h, b), True, True, 96 ** -0.5))
            return got

        stages = [("mod", 0), ("setup", 0)]
        for l in range(LAYERS):
            stages += [(s, l) for s in ("prenorm", "proj", "swa", "ret", "gla", "out", "postnorm")]
        stages += [("even_in", 0), ("even_mix", 0), ("even_sub", 0), ("even_out", 0), ("ln", 0), ("up", 0), ("down", 0),
                   ("ln", 1), ("odd_in", 0), ("odd_norms", 0), ("odd_up", 0), ("odd_mix", 0), ("odd_out", 0), ("ln", 2),
                   ("up", 1), ("down", 1), ("ln", 3)]
        if stop:
            stages = stages[:stages.index(stop) + 1]
        else:
            stages += [("store", 0)]

        def jobs_of(s, l):
            plans = {"mod": lambda: mod_jobs(l, 2), "proj": lambda: first_jobs(l),
                     "out": lambda: out_jobs(io["w_out"][l], 8, "copy"), "even_in": even_jobs,
                     "even_out": lambda: out_jobs(io["ev_w_out_2"][0], 6, "res"),
                     "odd_in": lambda: odd_jobs() + cmp_jobs(), "odd_up": mla_jobs,
                     "odd_out": lambda: out_jobs(io["od_w_out_2"][0], 8, "res"),
                     "up": lambda: up_jobs(l), "down": lambda: down_jobs(l)}
            return plans[s]() if s in plans else []

        def steps_of(s, l):
            if s == "even_mix":
                steps = even_steps()
                return [(steps[:32], 4), (steps[32:], 2)]
            return [(swa_steps(l) if s == "swa" else odd_steps(), 4)]

        LINEAR = ("mod", "proj", "out", "even_in", "even_out", "up", "down", "odd_in", "odd_up", "odd_out")

        BANKS = {"mod": 1, "setup": len(VECTORS) - 1 + KD + len(HOT_CUTS), "prenorm": 1, "postnorm": 1, "ret": 2, "gla": 4, "even_sub": 4, "ln": 2,
                 "odd_norms": 2, "store": 8}
        def modulation(stage):
            landed, c, n_jobs, got = [0] * SLOTS, 0, 0, []
            for s, l in stages[:stages.index(stage) + 1]:
                n_jobs += BANKS.get(s, 0)
                for j in jobs_of(s, l):
                    for parts in j["chunks"]:
                        landed[c % SLOTS] += 16 * len(parts)
                        if j["kind"] == "M" and (s, l) == stage:
                            got.append((j, c % SLOTS, landed[c % SLOTS], n_jobs))
                        c += 2 if j["kind"] == "M" and j["wide"] else 1
                    n_jobs += 1
            return got

        def weights_of(j, c):
            return PAIRS[:, c // 2] if j["wide"] else RING[:, c]

        N_CONST, BIAS_IN = [0], []
        C_IN, FIRST_IN = 16 * 3, 16 * 8
        ROWS_IN = 16 * sum(len(g) for g in VECTORS[1:])

        block = ctx.enter_context(nc.Block())

        @block.gpsimd
        def _(pool):
            n_const, n_bias = [0], [0]

            def load(dst, src):
                n_const[0] += 1
                pool.dma_start(dst, src).then_inc(const_in, 16)

            def load_later(dst, src):
                n_bias[0] += 1
                pool.dma_start(dst, src).then_inc(bias_in, 16)

            def all_met(stage):
                pool.wait_ge(act_met, stages.index(stage))
                pool.wait_ge(dve_met, stages.index(stage))
                pool.wait_ge(pe_met, stages.index(stage))

            def hankel(view, vec, c0, start):
                load_later(view, bass.AP(tensor=SCR.tensor, offset=c0 * VEC_LEN + int(VEC_AT[vec]) + start,
                                         ap=[[1, P], [VEC_LEN, view.shape[1]], [1, view.shape[2]]]))

            n_steps, n_made = [0], [0]

            def products(stage):
                made = []
                for j, c, count, at_job in modulation(stage):
                    if j["maker"] != "pool":
                        continue
                    w, n, acc = weights_of(j, c), j["n"] * P, MACC[:, j["turn"], 0:j["n"] * P]
                    pool.wait_ge(loaded[c], count)
                    back = 2 if j["wide"] else 4
                    if len(made) >= back:
                        pool.wait_ge(acc_ready, made[-back] + 1)
                    made.append(at_job)
                    nc.gpsimd.tensor_tensor(w, w, CACT.unsqueeze(2).broadcast_to([P, KD, n]), ALU.mult) \
                        .then_inc(pool_step, 1)
                    for k in (4, 2):
                        n_steps[0] += 1
                        pool.wait_ge(pool_step, n_steps[0])
                        nc.gpsimd.tensor_tensor(w[:, 0:k, :], w[:, 0:k, :], w[:, k:2 * k, :], ALU.add) \
                            .then_inc(pool_step, 1)
                    n_steps[0] += 1
                    pool.wait_ge(pool_step, n_steps[0])
                    ins = nc.gpsimd.tensor_tensor(acc, w[:, 0, :], w[:, 1, :], ALU.add)
                    ins.then_inc(mod_pool, 1)
                    n_made[0] += 1
                    pool.wait_ge(mod_pool, n_made[0])

            pool.wait_ge(c_ready, 1)
            products(("mod", 0))
            with nc.allow_non_contiguous_dma(reason="small operands, a feature to a partition"):
                for l in range(LAYERS):
                    load(SINKS[:, 8 * l:8 * l + 8], io["attn_sinks"][l].partition_broadcast(P))
                    load(GWB[l][0:16, :], io["gla_gate_w"][l])
                    load(GWB[l][16:17, :], io["gla_gate_b"][l:l + 1])
                    for a in range(2):
                        load(GLAG[64 * a:64 * a + 64, l:l + 1], io["gla_norm_gain"][l].rearrange("(p o) -> p o", o=1))
                load(DECAY, cst["decay"])
                load(UPPER, cst["upper"])
                load(WINDOW, cst["window"])
                load(SUBM, cst["sub"])
                load(HEADS, cst["heads"])
                load(LAMP, io["ev_lambda_2"][0].rearrange("a b -> (a b)").partition_broadcast(P))
                N_CONST[0] = 16 * n_const[0]
                if ("proj", 0) in stages:
                    products(("proj", 0))
                if ("even_in", 0) in stages:
                    all_met(("even_in", 0))
                    hankel(BFULL4, 0, 0, 511 - 127)
                    hankel(BWIN, 1, 4, 0)
                    hankel(BD4, 2, 8, 0)
                    hankel(BD16, 3, 12, 0)
                BIAS_IN.append(16 * n_bias[0])
                if ("even_sub", 0) in stages:
                    all_met(("even_sub", 0))
                    load_later(MROPE, cst["mla_rope"])
                    load_later(CAUSAL, cst["causal"])
                    hankel(BFULL8, 0, 0, 0)
                BIAS_IN.append(16 * n_bias[0])

        @block.sync
        def _(sp):
            job_of = []
            n_jobs = 0
            for s, l in stages:
                js = jobs_of(s, l)
                n_jobs += BANKS.get(s, 0)
                for j in js:
                    for parts in j["chunks"]:
                        c = len(job_of)
                        if "wide" in j and j["wide"]:
                            if c % 4 == 0:
                                if c >= SLOTS:
                                    sp.wait_ge(acc_ready, job_of[c - SLOTS] + 1)
                                sp.dma_start(PAIRS[:, c // 2 % 4], parts[0][3]).then_inc(loaded[c % SLOTS], 16)
                            if c == 4:
                                for g, group in enumerate(VECTORS[1:], 1):
                                    for c0, n, src in group:
                                        r0 = c0 - group[0][0]
                                        sp.dma_start(VROWS[r0:r0 + n, g * P:g * P + P], src).then_inc(rows_in, 16)
                                sp.dma_start(XIN, io["x"][0].rearrange("(b p) n -> p b n", p=P)).then_inc(x_in, 16)
                            job_of += [n_jobs, n_jobs]
                            continue
                        if c >= SLOTS:
                            sp.wait_ge(acc_ready, job_of[c - SLOTS] + 1)
                        for d0, n, nk, src in parts:
                            sp.dma_start(RING[:, c % SLOTS, 0:nk, d0:d0 + n], src).then_inc(loaded[c % SLOTS], 16)
                        job_of.append(n_jobs)
                    n_jobs += 1
            if not stop:
                sp.wait_ge(act_met, len(stages))
                sp.dma_start(out.rearrange("(b p) n -> p b n", p=P), XIN).then_inc(stored, 16)
                sp.wait_ge(stored, 16)


        @block.tensor
        def _(pe):
            me = Side()
            mm = nc.tensor.matmul
            frees = {"act": acc_free_act, "dve": acc_free_dve}
            freed = []
            at_chunk = [0]
            landed = [0] * SLOTS

            def begin(by):
                if me.job >= me.depth:
                    pe.wait_ge(*freed[me.job - me.depth])
                me.emptied_by(by)
                freed.append((frees[by], me.emptied[by]))
                return PS[:, me.bank(), :]

            def done(ins):
                ins.then_inc(me.signals(acc_ready), 1)

            def slot(parts):
                c = at_chunk[0] % SLOTS
                landed[c] += 16 * len(parts)
                pe.wait_ge(loaded[c], landed[c])
                at_chunk[0] += 1
                return RING[:, c], parts[0][2]

            def linear(jobs):
                for j in jobs:
                    bank = begin(j["by"])
                    m = j.get("m", P)
                    if "back" in j:
                        pe.wait_ge(*freed[me.job - 1 - j["back"]])
                    if j["kind"] == "R":
                        ins = mm(bank, j["rot"], j["of"]["dst"], start=True, stop=True)
                    elif j["kind"] == "F":
                        k, total = 0, sum(parts[0][2] for parts in j["chunks"])
                        for parts in j["chunks"]:
                            w, nk = slot(parts)
                            for i in range(nk):
                                ins = mm(bank[0:m, :], w[:, i, 0:m], j["src"](k), start=(k == 0), stop=(k == total - 1))
                                k += 1
                    elif j["kind"] == "T":
                        w, nk = slot(j["chunks"][0])
                        for tt in range(NB):
                            for i in range(nk):
                                ins = mm(bank[:, tt * m:tt * m + m], j["src"](i)[:, tt * B:tt * B + B], w[:, i, 0:m],
                                         start=(i == 0), stop=(i == nk - 1))
                    elif j["kind"] == "M":
                        c = at_chunk[0] % SLOTS
                        landed[c] += 16
                        at_chunk[0] += 2 if j["wide"] else 1
                        if j["maker"] == "dve":
                            pe.wait_ge(mod_dve, me.after(mod_dve))
                        else:
                            pe.wait_ge(mod_pool, me.after(mod_pool))
                        for n in range(j["n"]):
                            ins = mm(bank[:, n:n + 1], MACC[:, j["turn"], n * P:n * P + P], ONE, start=True, stop=True)
                    elif j["kind"] == "C":
                        if j["kv"] == 0 and j["h"] == 0:
                            pe.wait_ge(cmp_ready, me.after(cmp_ready))
                        for a, parts in enumerate(j["chunks"]):
                            w, nk = slot(parts)
                            for i in range(nk):
                                k = 8 * a + i
                                ins = mm(bank[:, 0:62], w[:, i, :], CMPIN[:, j["kv"], k, :], start=(k == 0), stop=(k == 15))
                    elif j["kv"] == 0:
                        w, nk = slot(j["chunks"][0])
                        for i in range(2):
                            ins = mm(bank[:, 0:62], w[:, i, :], H1[:, i, :], start=(i == 0), stop=(i == 1))
                    else:
                        w, nk = slot(j["chunks"][0])
                        for g in range(2):
                            for i in range(2):
                                ins = mm(bank[0:31, g * 64:g * 64 + 64], H1[:, i, 31 * g:31 * g + 31], w[:, i, 0:64],
                                         start=(i == 0), stop=(i == 1))
                    done(ins)

            def sums(ones, n):
                bank = begin("act")
                for k in range(n):
                    pe.wait_ge(sq_ready, me.sq + 1)
                    ins = mm(bank, ones, SQ[:, me.sq % 2, :], start=(k == 0), stop=(k == n - 1))
                    me.sq += 1
                    if k < n - 1:
                        ins.then_inc(me.signals(sq_used), 1)
                done(ins)

            def score_bank():
                if me.seg - 1 > 0:
                    pe.wait_ge(scores_free, me.seg - 1)
                me.seg += 1
                return PS[:, 2 + (me.seg - 1) % 2, :]

            def wide_score_bank():
                if me.seg - 3 > 0:
                    pe.wait_ge(scores_free, me.seg - 3)
                me.seg += 1
                return PS[:, (me.seg - 1) % 4, :]

            def mix_bank():
                if me.group - 1 > 0:
                    pe.wait_ge(mix_free, me.group - 1)
                return PS[:, 6 + me.group % 2, :]

            def attention(steps, depth):
                n, base, turns = len(steps), me.step, {}
                _, es, ets = rings(depth)

                def scores(i):
                    for pairs, keys, _ in steps[i]["segs"]:
                        bank = wide_score_bank()
                        for a, (q, k) in enumerate(pairs):
                            ins = mm(bank[:, 0:keys], q, k, start=(a == 0), stop=(a == len(pairs) - 1))
                        ins.then_inc(me.signals(scores_ready), 1)

                def turn(i):
                    pe.wait_ge(probs_ready, base + i + 1)
                    keys = steps[i]["keys"]
                    for c0 in range(0, keys, 4 * B):
                        if me.turn - 1 > 0:
                            pe.wait_ge(turn_free, me.turn - 1)
                        bank = PS[:, 4 + me.turn % 2, :]
                        for c in range(c0, min(keys, c0 + 4 * B), B):
                            w = min(B, keys - c)
                            ins = nc.tensor.transpose(bank[0:w, c - c0:c - c0 + B], es[:, i % depth, c:c + w], IDN)
                        ins.then_inc(me.signals(turned), 1)
                        me.turn += 1
                    turns[i] = me.turn

                def values(i):
                    s = steps[i]
                    pe.wait_ge(turn_free, turns[i])
                    bank = mix_bank()
                    for a, v in enumerate(s["values"]):
                        w = min(B, s["keys"] - a * B)
                        ins = mm(bank[0:v.shape[1], 0:B], v, ets[0:w, i % depth, a, :], start=(s["first"] and a == 0),
                                 stop=(s["last"] and a == len(s["values"]) - 1))
                    ins.then_inc(me.signals(values_done), 1)
                    me.group += s["last"]
                for i in range(n + depth):
                    if i < n:
                        scores(i)
                    if 0 <= i - depth + 1 < n:
                        turn(i - depth + 1)
                    if i >= depth:
                        values(i - depth)
                me.step += n

            def retention():
                for h in range(4):
                    t, p0 = h // 2, 64 * (h % 2)
                    o = mix_bank()[0:64, :]

                    def value(jb):
                        pe.wait_ge(scores_free, me.seg - (jb < NB - 1))
                        mm(o[:, jb * B:T], ztok(RV + t, jb, p0, 64), E[:, jb % 2, 0:T - jb * B], start=(jb == 0),
                            stop=(jb == NB - 1), skip_group_check=True) \
                            .then_inc(me.signals(values_done), 1)
                    for jb in range(NB):
                        mm(score_bank()[:, 0:T - jb * B], Z[p0:p0 + 64, RK + t, jb * B:jb * B + B],
                            Z[p0:p0 + 64, RQ + t, jb * B:T], start=True, stop=True) \
                            .then_inc(me.signals(scores_ready), 1)
                        if jb:
                            value(jb - 1)
                    value(NB - 1)
                    me.group += 1

            def gla(l):
                pe.wait_ge(gla_to_pe, me.after(gla_to_pe))
                bank = begin("dve")
                for tt in range(NB):
                    ins = mm(bank[:, tt * B:tt * B + B], Z[0:17, GAT, tt * B:tt * B + B], GWB[l], start=True, stop=True)
                done(ins)
                pe.wait_ge(gla_to_pe, me.after(gla_to_pe))
                bank = begin("act")
                for a in range(NB):
                    ins = mm(bank[:, a * B:T], z(LA)[:, a * B:a * B + B], UPPER[:, 0:T - a * B], start=(a == 0),
                             stop=(a == NB - 1), skip_group_check=True)
                done(ins)
                for qb in range(NB):
                    pe.wait_ge(gla_to_pe, me.after(gla_to_pe))
                    for jb in range(qb):
                        bank = score_bank()
                        k0 = (0, 0, 128, 384)[qb] + jb * B
                        mm(bank, GK1[:, k0:k0 + B], GQ1, start=True, stop=True).then_inc(me.signals(scores_ready), 1)
                    bank = score_bank()
                    for a in range(8):
                        c = slice(16 * a, 16 * a + 16)
                        ins = mm(bank.rearrange("p (h i) -> p h i", h=4)[:, :, c], GK2[:, a, :],
                                 GQ2.rearrange("p (h i) -> p h i", h=4)[:, :, c], start=True, stop=True)
                    ins.then_inc(me.signals(scores_ready), 1)
                    bank = score_bank()
                    for c in range(16):
                        ins = mm(bank[:, 4 * c:4 * c + 4], GPROD[:, c, :], HEADS, start=True, stop=True)
                    ins.then_inc(me.signals(scores_ready), 1)
                    o = mix_bank()[0:64, :]
                    pe.wait_ge(gla_to_pe, me.after(gla_to_pe))
                    for h in range(4):
                        for jb in range(qb + 1):
                            ins = mm(o[:, h * B:h * B + B], ztok(GV + h // 2, jb, 64 * (h % 2), 64),
                                     GS[:, jb, h * B:h * B + B], start=(jb == 0), stop=(jb == qb))
                    ins.then_inc(me.signals(values_done), 1)
                    me.group += 1

            for n_met, (s, l) in enumerate(stages, 1):
                me.begins(4 if s in LINEAR else 2)
                if s == "mod":
                    pe.wait_ge(first_in, C_IN)
                    bank = begin("act")
                    done(nc.tensor.transpose(bank[:, 0:56], VROWS[0:56, 0:P], IDN[0:56, 0:56]))
                    pe.wait_ge(one_set, 1)
                if s == "swa" and l == 0:
                    pe.wait_ge(const_in, N_CONST[0])
                if s == "setup":
                    pe.wait_ge(rows_in, ROWS_IN)
                    for g, group in enumerate(VECTORS[1:], 1):
                        n = sum(n for _, n, _ in group)
                        bank = begin("act")
                        done(nc.tensor.transpose(bank[:, 0:n], VROWS[0:n, g * P:g * P + P], IDN[0:n, 0:n]))
                    pe.wait_ge(first_in, FIRST_IN)
                    pe.wait_ge(x_in, 16)
                    for k in range(KD):
                        bank = begin("act")
                        for b in range(NB):
                            ins = nc.tensor.transpose(bank[:, b * B:b * B + B], XIN[:, b, k * P:k * P + P], IDN)
                        done(ins)
                    pe.wait_ge(side_dve, me.after(side_dve))
                    for c, w in HOT_CUTS:
                        bank = begin("dve")
                        done(mm(bank[0:16, 0:w], TABLE, HOT[:, c:c + w], start=True, stop=True))
                elif s in ("prenorm", "postnorm"):
                    sums(ONES_D, KD)
                elif s == "ln":
                    bank = begin("dve")
                    for k in range(KD):
                        ins = mm(bank, ONES_D, X[:, k, :], start=(k == 0), stop=(k == KD - 1))
                    done(ins)
                    sums(ONES_D, KD)
                elif s in ("swa", "even_mix", "odd_mix"):
                    for steps, depth in steps_of(s, l):
                        attention(steps, depth)
                elif s == "ret":
                    retention()
                    for t in range(2):
                        sums(ONES_64, 1)
                elif s == "gla":
                    gla(l)
                    for t in range(2):
                        sums(ONES_64, 1)
                elif s == "even_sub":
                    for t in range(4):
                        sums(ONES_128, 1)
                elif s == "odd_norms":
                    sums(ONES_384, 3)
                    sums(ONES_256, 2)
                elif s == "store":
                    for n in range(8):
                        bank = begin("act")
                        b, c = n // 2, n % 2
                        for i in range(4):
                            ins = nc.tensor.transpose(bank[:, i * P:i * P + P], X[:, 4 * c + i, b * B:b * B + B], IDN)
                        done(ins)
                else:
                    linear(jobs_of(s, l))
                pe.wait_ge(*me.last)
                pe.sem_inc(pe_met, 1)
                pe.wait_ge(act_met, n_met)
                pe.wait_ge(dve_met, n_met)

        @block.scalar
        def _(act):
            me = Side()
            fn = nc.scalar.activation
            vals = [0]
            squared = []
            inner = [0]

            def take():
                me.emptied_by("act")
                act.wait_ge(acc_ready, me.job)
                return PS[:, me.bank(), :]

            def stat(tiles, eps):
                for k, t in enumerate(tiles):
                    if me.sq >= 2:
                        act.wait_ge(*squared[me.sq - 2])
                    fn(SQ[:, me.sq % 2, :], t, ACT.Square).then_inc(me.signals(sq_ready), 1)
                    me.sq += 1
                    if k < len(tiles) - 1:
                        inner[0] += 1
                        squared.append((sq_used, inner[0]))
                    else:
                        squared.append((acc_ready, me.job + 1))
                bank = take()
                act.wait_ge(*me.last)
                fn(RS, bank, ACT.Ln, bias=eps).then_inc(me.signals(acc_free_act), 1)
                act.wait_ge(*me.last)
                fn(RS, RS, ACT.Exp, scale=-0.5).then_inc(me.signals(rstd_ready), 1)

            def linear(jobs, l):
                n = 0
                for j in jobs:
                    if j["by"] != "act":
                        me.emptied_by(j["by"])
                        continue
                    bank = take()
                    how, m = j["how"], j.get("m", P)
                    if how == "copy" and "scale" in j:
                        fn(j["dst"], bank[0:m, :], ACT.Copy, scale=j["scale"]).then_inc(me.signals(acc_free_act), 1)
                    elif how == "copy":
                        fn(j["dst"], bank[0:m, :], ACT.Copy).then_inc(me.signals(acc_free_act), 1)
                    elif how == "silu":
                        fn(j["dst"], bank, ACT.Silu).then_inc(me.signals(acc_free_act), 1)
                    elif how == "shift":
                        fn(j["dst"][0:64, :], bank[0:64, :], ACT.Copy).then_inc(me.signals(act_step), 1)
                        fn(j["dst"][64:128, 0:T - 1], bank[64:128, 1:T], ACT.Copy).then_inc(me.signals(acc_free_act), 1)
                    elif how == "sigmoid":
                        fn(j["dst"], bank[:, 0:96], ACT.Sigmoid).then_inc(me.signals(acc_free_act), 1)
                    elif how == "gelu":
                        act.wait_ge(*me.last)
                        fn(H1[:, j["h"], :], bank[:, 0:62], ACT.Gelu_apprx_tanh).then_inc(me.signals(acc_free_act), 1)
                    elif how == "kct":
                        fn(KCT, bank[:, 0:62], ACT.Copy).then_inc(me.signals(acc_free_act), 1)
                    elif how == "vc":
                        fn(VC, bank[0:31, 0:128].rearrange("p (g d) -> p g d", g=2), ACT.Copy) \
                            .then_inc(me.signals(acc_free_act), 1)
                    elif how == "conv":
                        if l * NF + n - 1 > 0:
                            act.wait_ge(conv_ready, l * NF + n - 1)
                        act.wait_ge(*me.last)
                        fn(GPAD[:, n % 2, 2:T + 2], bank, ACT.Copy).then_inc(me.signals(acc_free_act), 1)
                        act.wait_ge(conv_ready, l * NF + n + 1)
                        act.wait_ge(*me.last)
                        fn(GELUED[:, n % 2, :], CONVED[:, n % 2, :], ACT.Gelu_apprx_tanh) \
                            .then_inc(me.signals(gelu_ready), 1)
                        n += 1

            def attention(steps, depth):
                n, base, turns, t = len(steps), me.step, [], me.turn
                ss, es, ets = rings(depth)
                for s in steps:
                    t += -(-s["keys"] // (4 * B))
                    turns.append(t)

                def exps(i):
                    s, r = steps[i], i % depth
                    act.wait_ge(max_ready, base + i + 1)
                    if i >= depth:
                        act.wait_ge(turned, turns[i - depth])
                    keys = s["keys"] + (s["sink"] is not None)
                    fn(es[:, r, 0:keys], ss[:, r, 0:keys], ACT.Exp, bias=NMAX[:, r:r + 1], scale=1.0,
                        accum_out=DEN[:, r:r + 1]) \
                        .then_inc(me.signals(exp_ready), 1)

                def collect(i):
                    s, r = steps[i], i % depth
                    if i >= depth:
                        act.wait_ge(values_done, vals[0] + i - depth + 1)
                    w = min(B, s["keys"])
                    for c0 in range(0, s["keys"], 4 * B):
                        me.turn += 1
                        act.wait_ge(turned, me.turn)
                        nb = -(-min(4 * B, s["keys"] - c0) // B)
                        fn(ets[0:w, r, c0 // B:c0 // B + nb, :],
                            PS[0:w, 4 + (me.turn - 1) % 2, 0:nb * B].rearrange("p (a q) -> p a q", a=nb), ACT.Copy) \
                            .then_inc(me.signals(turn_free), 1)

                def mixed(i):
                    s = steps[i]
                    if s["last"]:
                        act.wait_ge(values_done, vals[0] + i + 1)
                        fn(s["dst"], PS[0:s["values"][0].shape[1], 6 + me.group % 2, 0:B], ACT.Copy) \
                            .then_inc(me.signals(mix_free), 1)
                        me.group += 1
                for i in range(n + depth):
                    if i < n:
                        exps(i)
                    if 0 <= i - depth + 1 < n:
                        collect(i - depth + 1)
                    if i >= depth:
                        mixed(i - depth)
                me.step += n
                vals[0] += n

            def retention():
                for h in range(4):
                    vals[0] += NB
                    act.wait_ge(values_done, vals[0])
                    fn(H[64 * (h % 2):64 * (h % 2) + 64, 4 + h // 2, :], PS[0:64, 6 + me.group % 2, :], ACT.Copy) \
                        .then_inc(me.signals(mix_free), 1)
                    me.group += 1

            def gla():
                me.emptied_by("dve")
                act.wait_ge(gla_to_act, me.after(gla_to_act))
                act.wait_ge(*me.last)
                fn(z(TMP), z(TMP), ACT.Exp, scale=-1.0).then_inc(me.signals(act_step), 1)
                act.wait_ge(*me.last)
                fn(z(TMP), z(TMP), ACT.Ln, bias=ONE).then_inc(me.signals(gla_act), 1)
                bank = take()
                act.wait_ge(*me.last)
                fn(z(BT), bank, ACT.Copy).then_inc(me.signals(acc_free_act), 1)
                act.wait_ge(gla_to_act, me.after(gla_to_act))
                fn(z(Q1)[:, B:T], z(Q1)[:, B:T], ACT.Exp).then_inc(me.signals(act_step), 1)
                fn(z(Q2), z(Q2), ACT.Exp).then_inc(me.signals(act_step), 1)
                fn(GK1, GK1, ACT.Exp).then_inc(me.signals(gla_act), 1)
                for qb in range(NB):
                    act.wait_ge(gla_to_act, me.after(gla_to_act))
                    fn(z(0, 2), z(0, 2), ACT.Exp).then_inc(me.signals(act_step), 1)
                    fn(z(2, 4), z(2, 4), ACT.Exp).then_inc(me.signals(gla_act), 1)
                    vals[0] += 1
                    act.wait_ge(values_done, vals[0])
                    o = PS[0:64, 6 + me.group % 2, :].rearrange("p (a b i) -> p a b i", a=2, b=2)
                    fn(H[0:64, 6:8, qb * B:qb * B + B], o[:, :, 0, :], ACT.Copy).then_inc(me.signals(act_step), 1)
                    fn(H[64:128, 6:8, qb * B:qb * B + B], o[:, :, 1, :], ACT.Copy).then_inc(me.signals(mix_free), 1)
                    me.group += 1

            def stats(groups, eps):
                act.wait_ge(*me.last)
                for tiles in groups:
                    stat(tiles, eps)
                    act.wait_ge(normed, me.after(normed, len(tiles)))

            for n_met, (s, l) in enumerate(stages, 1):
                me.begins(4 if s in LINEAR else 2)
                if s == "mod":
                    pairs = [j["chunks"][0][0][3] for j in jobs_of(s, l)]
                    for c0, n, src in VECTORS[0]:
                        act.dma_start(VROWS[c0:c0 + n, 0:P], src).then_inc(first_in, 16)
                    act.dma_start(IDN, cst["mats"][:, 0, :]).then_inc(first_in, 16)
                    for i in (1, 3):
                        act.dma_start(PAIRS[:, i], pairs[i]).then_inc(loaded[2 * i], 16)
                    bank = take()
                    fn(VEC[:, 0:56], bank[:, 0:56], ACT.Copy).then_inc(me.signals(acc_free_act), 1)
                    act.wait_ge(*me.last)
                    fn(CACT, CT, ACT.Silu).then_inc(c_ready, 1)
                    act.dma_start(MATS[:, 1:8, :], cst["mats"][:, 1:8, :]).then_inc(first_in, 16)
                    act.dma_start(z(22).bitcast(I32), io["positions"][0].partition_broadcast(P)).then_inc(first_in, 16)
                    act.dma_start(TINY[:, 4:7], cst["freq"]).then_inc(first_in, 16)
                    act.dma_start(HOT, cst["onehot"]).then_inc(first_in, 16)
                    act.dma_start(TABLE[0:32, :], io["rel_bias_2"]).then_inc(first_in, 16)
                    for i in range(5, len(pairs), 2):
                        act.wait_ge(acc_ready, i - 2)
                        act.dma_start(PAIRS[:, i % 4], pairs[i]).then_inc(loaded[2 * (i % 4)], 16)
                if s == "swa" and l == 0:
                    act.wait_ge(const_in, N_CONST[0])
                if s == "setup":
                    for group in VECTORS[1:]:
                        c0, n = group[0][0], sum(n for _, n, _ in group)
                        bank = take()
                        fn(VEC[:, c0:c0 + n], bank[:, 0:n], ACT.Copy).then_inc(me.signals(acc_free_act), 1)
                    for k in range(KD):
                        bank = take()
                        fn(X[:, k, :], bank, ACT.Copy).then_inc(me.signals(acc_free_act), 1)
                    for _ in HOT_CUTS:
                        me.emptied_by("dve")
                    act.wait_ge(acc_free_dve, me.emptied["dve"])
                    act.dma_start(SCR, VECS_SB).then_inc(table_out, 16)
                    act.wait_ge(side_dve, me.after(side_dve, 2))
                    for n in range(2):
                        fn(ROPE[:, 2 * n, :], z(24 + 3 * n), ACT.Sin).then_inc(me.signals(act_step), 1)
                        fn(ROPE[:, 2 * n + 1, :], z(23 + 3 * n), ACT.Sin).then_inc(me.signals(act_step), 1)
                elif s == "prenorm":
                    stat([X[:, k, :] for k in range(KD)], EPS6)
                    for k in range(KD):
                        act.wait_ge(normed, me.after(normed))
                        fn(H[:, k, :], H[:, k, :], ACT.Identity, bias=MOD[l][:, k:k + 1], scale=1.0) \
                            .then_inc(me.signals(act_step), 1)
                elif s == "postnorm":
                    stat([z(k) for k in range(KD)], EPS6)
                    act.wait_ge(normed, me.after(normed, KD))
                elif s == "ln":
                    me.emptied_by("dve")
                    act.wait_ge(normed, me.after(normed, KD))
                    stat([X[:, k, :] for k in range(KD)], EPS5)
                    for k in range(KD):
                        act.wait_ge(normed, me.after(normed))
                        fn(X[:, k, :], X[:, k, :], ACT.Identity, bias=LNB[:, l, k:k + 1], scale=1.0) \
                            .then_inc(me.signals(act_step), 1)
                elif s in ("swa", "even_mix", "odd_mix"):
                    for steps, depth in steps_of(s, l):
                        attention(steps, depth)
                elif s == "ret":
                    retention()
                    stats([[H[:, 4 + t, :]] for t in range(2)], EPS6)
                elif s == "gla":
                    gla()
                    stats([[H[:, 6 + t, :]] for t in range(2)], EPS6)
                elif s == "even_sub":
                    stats([[H[:, t, :]] for t in range(4)], EPS5)
                elif s == "odd_norms":
                    stats([[z(CQ + i) for i in range(3)], [z(CKV + i) for i in range(2)]], EPS5)
                elif s == "store":
                    for n in range(8):
                        bank = take()
                        fn(z(n), bank, ACT.Copy).then_inc(me.signals(acc_free_act), 1)
                else:
                    linear(jobs_of(s, l), l)
                if s == "even_in":
                    act.wait_ge(side_dve, me.after(side_dve))
                    act.wait_ge(*me.last)
                    fn(LTMP[:, 2:4], LTMP[:, 0:2], ACT.Exp).then_inc(me.signals(side_act), 1)
                act.wait_ge(*me.last)
                act.sem_inc(act_met, 1)
                act.wait_ge(pe_met, n_met)
                act.wait_ge(dve_met, n_met)

        @block.vector
        def _(dve):
            me = Side()
            tt, ts, stt = nc.vector.tensor_tensor, nc.vector.tensor_scalar, nc.vector.scalar_tensor_tensor
            vals = [0]

            def take():
                me.emptied_by("dve")
                dve.wait_ge(acc_ready, me.job)
                return PS[:, me.bank(), :]

            def rope(j):
                bank, d = take(), j["of"]["dst"]
                dve.wait_ge(*me.last)
                tt(RT, bank, j["sin"], ALU.mult).then_inc(me.signals(acc_free_dve), 1)
                dve.wait_ge(*me.last)
                tt(d, d, j["cos"], ALU.mult).then_inc(me.signals(dve_step), 1)
                dve.wait_ge(*me.last)
                tt(d, d, RT, ALU.add).then_inc(me.signals(dve_step), 1)

            def products(j, c, count):
                w, n, acc = weights_of(j, c), j["n"] * P, MACC[:, j["turn"], 0:j["n"] * P]
                dve.wait_ge(loaded[c], count)
                dve.wait_ge(*me.last)
                ts(acc, w[:, 0, 0:n], CACT[:, 0:1], None, ALU.mult).then_inc(me.signals(dve_step), 1)
                for k in range(1, KD):
                    dve.wait_ge(*me.last)
                    stt(acc, w[:, k, 0:n], CACT[:, k:k + 1], acc, ALU.mult, ALU.add) \
                        .then_inc(me.signals(dve_step if k < KD - 1 else mod_dve), 1)

            def modulate(j):
                bank = take()
                dve.wait_ge(*me.last)
                tt(MOD[j["layer"]][:, j["n0"]:j["n0"] + j["n"]], bank[:, 0:j["n"]],
                    BMOD[:, j["layer"], j["n0"]:j["n0"] + j["n"]], ALU.add) \
                    .then_inc(me.signals(acc_free_dve), 1)

            def linear(jobs, l):
                n = 0
                for j in jobs:
                    if j["kind"] == "C" and j["kv"] == 0 and j["h"] == 0:
                        dve.wait_ge(acc_free_act, me.emptied["act"])
                        dve.wait_ge(bias_in, BIAS_IN[1])
                        for kv in range(2):
                            for g in range(2):
                                src = z((CK, CV)[kv] + g)
                                win = bass.AP(tensor=src.tensor, offset=src.offset, ap=[list(src.ap[0]), [2, 16], [16, 31]])
                                dve.wait_ge(*me.last)
                                tt(CMPIN[:, kv, :, 31 * g:31 * g + 31], win,
                                    PLACE[:, kv, :].unsqueeze(2).broadcast_to([P, 16, 31]), ALU.add) \
                                    .then_inc(me.signals(cmp_ready if kv + g == 2 else dve_step), 1)
                    if j["by"] != "dve":
                        me.emptied_by(j["by"])
                        if j["how"] == "conv":
                            dve.wait_ge(acc_free_act, me.emptied["act"])
                            g, c, a = GPAD[:, n % 2, :], CONVED[:, n % 2, :], j["j"]
                            tap = [CONVW[:, l, i, a:a + 1] for i in range(3)] + [CONVB[:, l, a:a + 1]]
                            dve.wait_ge(*me.last)
                            ts(c, g[:, 2:T + 2], tap[2], tap[3], ALU.mult, ALU.add).then_inc(me.signals(dve_step), 1)
                            dve.wait_ge(*me.last)
                            stt(c, g[:, 1:T + 1], tap[1], c, ALU.mult, ALU.add).then_inc(me.signals(dve_step), 1)
                            dve.wait_ge(*me.last)
                            stt(c, g[:, 0:T], tap[0], c, ALU.mult, ALU.add).then_inc(me.signals(conv_ready), 1)
                        continue
                    if j["kind"] == "R":
                        rope(j)
                    elif j["kind"] == "M":
                        modulate(j)
                    elif j["how"] == "gate":
                        bank = take()
                        dve.wait_ge(gelu_ready, me.after(gelu_ready))
                        dve.wait_ge(*me.last)
                        tt(j["dst"], bank, GELUED[:, n % 2, :], ALU.mult).then_inc(me.signals(acc_free_dve), 1)
                        n += 1
                    elif j["how"] == "res":
                        bank = take()
                        dve.wait_ge(*me.last)
                        stt(j["dst"], j["dst"], ALPHA, bank, ALU.mult, ALU.add).then_inc(me.signals(acc_free_dve), 1)

            def attention(steps, depth):
                n, base, lag = len(steps), me.step, depth // 2
                ss, es, _ = rings(depth)

                def scaled(i):
                    s, r, c = steps[i], i % depth, 0
                    for _, keys, bias in s["segs"]:
                        me.seg += 1
                        dve.wait_ge(scores_ready, me.seg)
                        stt(ss[:, r, c:c + keys], PS[:, (me.seg - 1) % 4, 0:keys], s["scale"], bias, ALU.mult,
                            ALU.add) \
                            .then_inc(me.signals(scores_free), 1)
                        c += keys
                    if s["sink"] is not None:
                        nc.vector.tensor_copy(ss[:, r, c:c + 1], s["sink"]).then_inc(me.signals(dve_step), 1)
                    return me.last

                def recips(i):
                    s, r = steps[i], i % depth
                    dve.wait_ge(exp_ready, base + i + 1)
                    nc.vector.reciprocal(RDEN[:, r:r + 1], DEN[:, r:r + 1]).then_inc(me.signals(dve_step), 1)
                    if s["late"]:
                        dve.wait_ge(*me.last)
                        tt(RDEN[:, r:r + 1], RDEN[:, r:r + 1], LATE, ALU.mult).then_inc(me.signals(dve_step), 1)
                    return me.last

                def maximum(i, written):
                    s, r = steps[i], i % depth
                    dve.wait_ge(*written)
                    nc.vector.tensor_reduce(NMAX[:, r:r + 1], ss[:, r, 0:s["keys"] + (s["sink"] is not None)], AX.X,
                                            ALU.max, negate=True) \
                        .then_inc(me.signals(max_ready), 1)

                def normalise(i, written):
                    s, r = steps[i], i % depth
                    e = es[:, r, 0:s["keys"]]
                    dve.wait_ge(*written)
                    if s["factor"] is None:
                        ts(e, e, RDEN[:, r:r + 1], None, ALU.mult).then_inc(me.signals(probs_ready), 1)
                    else:
                        ts(e, e, RDEN[:, r:r + 1], s["factor"], ALU.mult, ALU.mult).then_inc(me.signals(probs_ready), 1)
                for i in range(n + lag):
                    if i < n:
                        written = scaled(i)
                    if i >= lag:
                        inverted = recips(i - lag)
                    if i < n:
                        maximum(i, written)
                    if i >= lag:
                        normalise(i - lag, inverted)
                me.step += n
                vals[0] += n

            def retention():
                for h in range(4):
                    for jb in range(NB):
                        me.seg += 1
                        dve.wait_ge(scores_ready, me.seg)
                        if jb >= 2 or h:
                            if vals[0] - 1 > 0:
                                dve.wait_ge(values_done, vals[0] - 1)
                        vals[0] += 1
                        w = T - jb * B
                        dve.wait_ge(*me.last)
                        tt(E[:, jb % 2, 0:w], PS[:, 2 + (me.seg - 1) % 2, 0:w], DECAY[:, h, 0:w], ALU.mult) \
                            .then_inc(me.signals(scores_free), 1)

            def gla():
                dve.wait_ge(*me.last)
                nc.vector.tensor_copy(GTMP[0:16, :], z(GAT)[0:16, :]).then_inc(me.signals(dve_step), 1)
                dve.wait_ge(*me.last)
                nc.vector.memset(z(GAT)[0:32, :], 1.0).then_inc(me.signals(dve_step), 1)
                dve.wait_ge(*me.last)
                nc.vector.tensor_copy(z(GAT)[0:16, :], GTMP[0:16, :]).then_inc(me.signals(gla_to_pe), 1)
                bank = take()
                dve.wait_ge(*me.last)
                nc.vector.tensor_copy(z(LA), bank).then_inc(me.signals(acc_free_dve), 1)
                dve.wait_ge(*me.last)
                stt(z(TMP), z(LA), -1.0, z(LA), ALU.mult, ALU.max).then_inc(me.signals(gla_to_act), 1)
                dve.wait_ge(*me.last)
                ts(z(LA), z(LA), 0.0, None, ALU.min).then_inc(me.signals(dve_step), 1)
                dve.wait_ge(gla_act, me.after(gla_act))
                dve.wait_ge(*me.last)
                tt(z(LA), z(LA), z(TMP), ALU.subtract).then_inc(me.signals(gla_to_pe), 1)
                me.emptied_by("act")
                dve.wait_ge(acc_free_act, me.emptied["act"])
                b = z(BT)
                dve.wait_ge(*me.last)
                nc.vector.memset(BREF[:, 0:1], 0.0).then_inc(me.signals(dve_step), 1)
                dve.wait_ge(*me.last)
                nc.vector.tensor_copy(BREF[:, 1:32], b[:, 15:511:16]).then_inc(me.signals(dve_step), 1)
                dve.wait_ge(*me.last)
                tt(z(Q2).rearrange("p (a i) -> p a i", a=32), b.rearrange("p (a i) -> p a i", a=32),
                    BREF.unsqueeze(2).broadcast_to([P, 32, 16]), ALU.subtract) \
                    .then_inc(me.signals(dve_step), 1)
                k0 = 0
                for qb in range(1, NB):
                    end = b[:, qb * B - 1:qb * B]
                    dve.wait_ge(*me.last)
                    ts(z(Q1)[:, qb * B:qb * B + B], b[:, qb * B:qb * B + B], end, None, ALU.subtract) \
                        .then_inc(me.signals(dve_step), 1)
                    dve.wait_ge(*me.last)
                    ts(GK1[:, k0:k0 + qb * B], b[:, 0:qb * B], end, -1.0, ALU.subtract, ALU.mult) \
                        .then_inc(me.signals(gla_to_act if qb == NB - 1 else dve_step), 1)
                    k0 += qb * B
                dve.wait_ge(gla_act, me.after(gla_act))
                dve.wait_ge(*me.last)
                tt(z(Q1)[:, B:T], z(Q1)[:, B:T], z(GQ)[:, B:T], ALU.mult).then_inc(me.signals(dve_step), 1)
                dve.wait_ge(*me.last)
                tt(z(Q2), z(Q2), z(GQ), ALU.mult).then_inc(me.signals(dve_step), 1)
                k0 = 0
                for qb in range(1, NB):
                    dve.wait_ge(*me.last)
                    tt(GK1[:, k0:k0 + qb * B], GK1[:, k0:k0 + qb * B], z(GK)[:, 0:qb * B], ALU.mult) \
                        .then_inc(me.signals(dve_step), 1)
                    k0 += qb * B
                for qb in range(NB):
                    bb, qq, kk = (z(t)[:, qb * B:qb * B + B] for t in (BT, GQ, GK))

                    def within(x):
                        return x.rearrange("p (a c) -> p c a", a=8).unsqueeze(3).broadcast_to([P, 16, 8, 16])

                    def over(x, n):
                        return x.unsqueeze(1).broadcast_to([P, n, B])
                    prod4 = GPROD.rearrange("p c (a j) -> p c a j", a=8)
                    dve.wait_ge(*me.last)
                    tt(GK2, BREF[:, 8 * qb:8 * qb + 8].unsqueeze(2).broadcast_to([P, 8, B]), over(bb, 8),
                        ALU.subtract) \
                        .then_inc(me.signals(dve_step), 1)
                    dve.wait_ge(*me.last)
                    ts(GK2, GK2, 0.0, None, ALU.min).then_inc(me.signals(dve_step), 1)
                    dve.wait_ge(*me.last)
                    nc.vector.tensor_copy(prod4, within(bb)).then_inc(me.signals(dve_step), 1)
                    dve.wait_ge(*me.last)
                    tt(GPROD, GPROD, over(bb, 16), ALU.subtract).then_inc(me.signals(dve_step), 1)
                    dve.wait_ge(*me.last)
                    ts(GPROD, GPROD, 0.0, None, ALU.min).then_inc(me.signals(gla_to_act), 1)
                    dve.wait_ge(gla_act, me.after(gla_act))
                    dve.wait_ge(*me.last)
                    tt(GK2, GK2, over(kk, 8), ALU.mult).then_inc(me.signals(dve_step), 1)
                    dve.wait_ge(*me.last)
                    tt(GPROD, GPROD, over(kk, 16), ALU.mult).then_inc(me.signals(dve_step), 1)
                    for t, q in ((GQ1, Q1), (GQ2, Q2)):
                        if qb or q == Q2:
                            dve.wait_ge(*me.last)
                            tt(t.rearrange("p (h i) -> p h i", h=4), over(z(q)[:, qb * B:qb * B + B], 4),
                                HEADS.unsqueeze(2).broadcast_to([P, 4, B]), ALU.mult) \
                                .then_inc(me.signals(dve_step), 1)
                    dve.wait_ge(*me.last)
                    tt(prod4, prod4, within(qq), ALU.mult).then_inc(me.signals(gla_to_pe), 1)
                    for jb in range(qb):
                        me.seg += 1
                        dve.wait_ge(scores_ready, me.seg)
                        dve.wait_ge(*me.last)
                        nc.vector.tensor_copy(GS[:, jb, :], PS[:, 2 + (me.seg - 1) % 2, :]) \
                            .then_inc(me.signals(scores_free), 1)
                    own = GS[:, qb, :].rearrange("p (h i) -> p h i", h=4)
                    me.seg += 1
                    dve.wait_ge(scores_ready, me.seg)
                    dve.wait_ge(*me.last)
                    tt(own, PS[:, 2 + (me.seg - 1) % 2, :].rearrange("p (h i) -> p h i", h=4),
                        SUBM[:, 0, :].unsqueeze(1).broadcast_to([P, 4, B]), ALU.mult) \
                        .then_inc(me.signals(scores_free), 1)
                    me.seg += 1
                    dve.wait_ge(scores_ready, me.seg)
                    near = PS[:, 2 + (me.seg - 1) % 2, 0:64].rearrange("p (c h) -> p h c", h=4)
                    for h in range(4):
                        dve.wait_ge(*me.last)
                        tt(GTMP[:, h * B:h * B + B].rearrange("p (a c) -> p a c", a=8),
                            SUBM[:, 1, :].rearrange("p (a c) -> p a c", a=8), near[:, h, :].unsqueeze(1).broadcast_to([P, 8, 16]), ALU.mult) \
                            .then_inc(me.signals(scores_free if h == 3 else dve_step), 1)
                    dve.wait_ge(*me.last)
                    tt(GS[:, qb, :], GS[:, qb, :], GTMP, ALU.add).then_inc(me.signals(gla_to_pe), 1)
                    vals[0] += 1
                    dve.wait_ge(values_done, vals[0])

            def scaled(tiles, gains, gates=None):
                dve.wait_ge(rstd_ready, me.after(rstd_ready))
                for n, t in enumerate(tiles):
                    if gates:
                        if gains is None:
                            dve.wait_ge(*me.last)
                            tt(t, t, RS, ALU.mult).then_inc(me.signals(dve_step), 1)
                        else:
                            dve.wait_ge(*me.last)
                            stt(t, t, gains[n], RS, ALU.mult, ALU.mult).then_inc(me.signals(dve_step), 1)
                        dve.wait_ge(*me.last)
                        tt(t, t, gates[n], ALU.mult).then_inc(me.signals(normed), 1)
                    else:
                        dve.wait_ge(*me.last)
                        stt(t, t, gains[n], RS, ALU.mult, ALU.mult).then_inc(me.signals(normed), 1)

            def angles():
                whole, parts = 12582912.0, (6.28125, 0.0019350051879882812, 3.01991605e-7)
                dve.wait_ge(*me.last)
                nc.vector.tensor_copy(z(29), z(22).bitcast(I32)).then_inc(me.signals(dve_step), 1)
                for n in range(2):
                    r, c, turns = z(23 + 3 * n), z(24 + 3 * n), z(25 + 3 * n)
                    dve.wait_ge(*me.last)
                    ts(r, z(29), FREQ[:, n:n + 1], None, ALU.mult).then_inc(me.signals(dve_step), 1)
                    dve.wait_ge(*me.last)
                    ts(turns, r, float(1 / (2 * np.pi)), whole, ALU.mult, ALU.add).then_inc(me.signals(dve_step), 1)
                    dve.wait_ge(*me.last)
                    ts(turns, turns, whole, None, ALU.subtract).then_inc(me.signals(dve_step), 1)
                    for part in parts:
                        dve.wait_ge(*me.last)
                        stt(r, turns, -part, r, ALU.mult, ALU.add).then_inc(me.signals(dve_step), 1)
                    dve.wait_ge(*me.last)
                    ts(r, r, 3.1415925, -3.1415925, ALU.min, ALU.max).then_inc(me.signals(dve_step), 1)
                    dve.wait_ge(*me.last)
                    stt(c, r, -1.0, r, ALU.mult, ALU.min) \
                        .then_inc(me.signals(dve_step), 1)
                    dve.wait_ge(*me.last)
                    ts(c, c, float(np.pi / 2), None, ALU.add).then_inc(me.signals(side_dve if n else dve_step), 1)

            for n_met, (s, l) in enumerate(stages, 1):
                me.begins(4 if s in LINEAR else 2)
                if s == "setup":
                    dve.wait_ge(first_in, FIRST_IN)
                    nc.vector.memset(EPS6, 1e-6).then_inc(me.signals(dve_step), 1)
                    dve.wait_ge(*me.last)
                    nc.vector.memset(EPS5, 1e-5).then_inc(me.signals(dve_step), 1)
                    dve.wait_ge(*me.last)
                    nc.vector.memset(TABLE[32:33, :], NEG).then_inc(me.signals(side_dve), 1)
                    angles()
                    for _ in range(len(VECTORS) - 1 + KD):
                        me.emptied_by("act")
                    for c, w in HOT_CUTS:
                        bank = take()
                        dve.wait_ge(*me.last)
                        nc.vector.tensor_copy(VECS_SB[:, c:c + w], bank[0:16, 0:w]) \
                            .then_inc(me.signals(acc_free_dve), 1)
                    dve.wait_ge(*me.last)
                    dve.wait_ge(table_out, 16)
                elif s == "prenorm":
                    dve.wait_ge(*me.last)
                    stt(GA, MOD[l][:, 8:16], 1.0, PREG[:, l, :], ALU.add, ALU.mult).then_inc(me.signals(dve_step), 1)
                    dve.wait_ge(*me.last)
                    tt(GB, MOD[l][:, 16:24], POSTG[:, l, :], ALU.mult).then_inc(me.signals(dve_step), 1)
                    me.emptied_by("act")
                    dve.wait_ge(rstd_ready, me.after(rstd_ready))
                    for k in range(KD):
                        dve.wait_ge(*me.last)
                        stt(H[:, k, :], X[:, k, :], GA[:, k:k + 1], RS, ALU.mult, ALU.mult) \
                            .then_inc(me.signals(normed), 1)
                elif s == "postnorm":
                    me.emptied_by("act")
                    scaled([z(k) for k in range(KD)], [GB[:, k:k + 1] for k in range(KD)])
                    for k in range(KD):
                        dve.wait_ge(*me.last)
                        tt(X[:, k, :], X[:, k, :], z(k), ALU.add).then_inc(me.signals(dve_step), 1)
                elif s == "ln":
                    bank = take()
                    for k in range(KD):
                        dve.wait_ge(*me.last)
                        tt(X[:, k, :], X[:, k, :], bank, ALU.subtract).then_inc(me.signals(normed), 1)
                    dve.wait_ge(*me.last)
                    nc.vector.tensor_copy(TINY[:, 120:121], bank[:, 0:1]).then_inc(me.signals(acc_free_dve), 1)
                    me.emptied_by("act")
                    scaled([X[:, k, :] for k in range(KD)], [LNG[:, l, k:k + 1] for k in range(KD)])
                elif s in ("swa", "even_mix", "odd_mix"):
                    if s == "swa" and l == 0:
                        dve.wait_ge(const_in, N_CONST[0])
                    if s != "swa":
                        dve.wait_ge(bias_in, BIAS_IN[0 if s == "even_mix" else 1])
                    for steps, depth in steps_of(s, l):
                        attention(steps, depth)
                elif s == "ret":
                    for k in range(4):
                        dve.wait_ge(*me.last)
                        tt(H[:, k, :], H[:, k, :], z(AG + k), ALU.mult).then_inc(me.signals(dve_step), 1)
                    retention()
                    for t in range(2):
                        me.emptied_by("act")
                        scaled([H[:, 4 + t, :]], None, [z(RG + t)])
                elif s == "gla":
                    gla()
                    for t in range(2):
                        me.emptied_by("act")
                        scaled([H[:, 6 + t, :]], [GLAG[:, l:l + 1]], [z(GG + t)])
                elif s == "even_sub":
                    for t in range(4):
                        me.emptied_by("act")
                        scaled([H[:, t, :]], [SUBG])
                elif s == "odd_norms":
                    for t, n, g in ((CQ, 3, QG), (CKV, 2, KVG)):
                        me.emptied_by("act")
                        scaled([z(t + i) for i in range(n)], [g[:, i:i + 1] for i in range(n)])
                elif s == "store":
                    for _ in range(8):
                        me.emptied_by("act")
                else:
                    if s == "mod":
                        me.emptied_by("act")
                        nc.vector.memset(ONE, 1.0).then_inc(me.signals(one_set), 1)
                        dve.wait_ge(c_ready, 1)
                        made = modulation(("mod", 0))
                        for i in range(0, len(made), 2):
                            if i >= 4:
                                dve.wait_ge(acc_ready, made[i - 4][3] + 1)
                            products(*made[i][:3])
                            if i:
                                modulate(made[i - 2][0])
                                modulate(made[i - 1][0])
                        modulate(made[-2][0])
                        modulate(made[-1][0])
                    if s == "up":
                        dve.wait_ge(*me.last)
                        nc.vector.memset(GPAD[:, :, 0:2], 0.0).then_inc(me.signals(dve_step), 1)
                    if s in ("odd_in", "odd_up"):
                        dve.wait_ge(bias_in, BIAS_IN[1])
                    if s != "mod":
                        linear(jobs_of(s, l), l)
                if s == "even_in":
                    lp = LAMP.rearrange("p (a b d) -> p a b d", a=2, b=2)
                    prod = RT[:, 0:128].rearrange("p (a d) -> p a d", a=2)
                    dve.wait_ge(*me.last)
                    tt(prod, lp[:, :, 0, :], lp[:, :, 1, :], ALU.mult).then_inc(me.signals(dve_step), 1)
                    dve.wait_ge(*me.last)
                    nc.vector.tensor_reduce(LTMP[:, 0:2], prod, AX.X, ALU.add).then_inc(me.signals(side_dve), 1)
                    dve.wait_ge(side_act, me.after(side_act))
                    dve.wait_ge(*me.last)
                    tt(LAM, LTMP[:, 3:4], LTMP[:, 2:3], ALU.subtract).then_inc(me.signals(dve_step), 1)
                    dve.wait_ge(*me.last)
                    ts(LAM, LAM, LAM_INIT, None, ALU.subtract).then_inc(me.signals(dve_step), 1)
                    dve.wait_ge(*me.last)
                    ts(SUBG, SUBG, 1.0 - LAM_INIT, None, ALU.mult).then_inc(me.signals(dve_step), 1)
                dve.wait_ge(*me.last)
                dve.sem_inc(dve_met, 1)
                dve.wait_ge(pe_met, n_met)
                dve.wait_ge(act_met, n_met)


_INS = ["x", "c", "positions", "w_mod", "b_mod", "pre_norm_gain", "post_norm_gain", "w_in", "attn_sinks", "gla_gate_w",
        "gla_gate_b", "gla_norm_gain", "w_out", "rel_bias_2", "ev_w_in_2", "ev_w_out_2", "ev_lambda_2", "ev_subln_2",
        "od_w_in_2", "od_w_out_2", "od_cmp_pe_2", "od_cmp_w1_2", "od_cmp_w2_2", "od_q_norm_2", "od_kv_norm_2", "od_w_uq_2",
        "od_w_uk_2", "od_w_uv_2", "ffn_w_up_2", "ffn_conv_w_2", "ffn_conv_b_2", "ffn_w_down_2", "ln_g_2", "ln_b_2"]


def kernel(**inputs):
    import concourse.bacc as _bacc
    from concourse.bass_utils import run_bass_kernel_spmd as _run

    nc = _bacc.Bacc("TRN2", target_bir_lowering=False, num_devices=1)
    arrays, io, cst = {}, {}, {}
    for name in _INS:
        a = np.ascontiguousarray(inputs[name])
        arrays["in_" + name] = a
        io[name] = nc.dram_tensor("in_" + name, a.shape, mybir.dt.from_np(a.dtype), kind="ExternalInput").ap()
    for name, a in constants().items():
        arrays["cst_" + name] = a
        cst[name] = nc.dram_tensor("cst_" + name, a.shape, F32, kind="ExternalInput").ap()
    out = nc.dram_tensor("out", [T, D], F32, kind="ExternalOutput").ap()
    build(nc, io, cst, out)
    r = _run(nc, [arrays], core_ids=[0])
    return r.results[0]["out"].reshape(1, T, D)
```

```python
from contextlib import ExitStack

import numpy as np

import concourse.bass as bass
from concourse import mybir

F32 = mybir.dt.float32
F32R = mybir.dt.float32r
I32 = mybir.dt.int32
ACT = mybir.ActivationFunctionType
ALU = mybir.AluOpType
AX = mybir.AxisListType

P = 128
T = 512
B = 128
NB = T // B
D = 1024
KD = D // P
NEG = -1e30
LAYERS = 2
D_IN = 3088
DFF = 2816
NF = DFF // P
ALPHA = (2 * LAYERS) ** 0.25
LAM_INIT = 0.8 - 0.6
SLOTS = 4
TILE = T * 4
HSPAN = 896
BUCKETS = 32
WIDEST = 1280

NTILES = 34


def t5_bucket(dist):
    n = np.maximum(dist, 0)
    nf = np.maximum(n, 1).astype(np.float32)
    large = 16 + (np.log(nf / np.float32(16)) / np.float32(np.log(2048 / 16)) * np.float32(16)).astype(np.int32)
    return np.where(n < 16, n, np.minimum(large, 31))


VECS = [(-511, 511, lambda d: d >= 0), (-127, 255, lambda d: (d >= 0) & (d <= 128)),
        (-127, 511, lambda d: (d >= 0) & (d % 4 == 0)), (-127, 511, lambda d: (d >= 0) & (d % 16 == 0))]
VEC_AT = np.cumsum([0] + [b - a + 1 for a, b, _ in VECS])
VEC_LEN = int(VEC_AT[-1])


def constants():
    f = np.float32
    out = {}
    eye = np.eye(P)
    rot = np.zeros((2, P, P))
    for n, half in enumerate((32, 16)):
        for m in range(P):
            if m % (2 * half) < half:
                rot[n, m + half, m] = -1
            else:
                rot[n, m - half, m] = 1
    ones = np.ones((P, P))
    pair = np.kron(np.eye(2), np.ones((64, 64))) / 64
    out["mats"] = np.stack([eye, rot[0], rot[1], ones / 1024, pair, ones / 128, ones / 384, ones / 256], 1)
    p = np.arange(P)
    freq = np.stack([10000.0 ** (-(p % 32) * 2 / 64), 1 / 10000.0 ** ((p % 32) / 31), np.zeros(P) + (p >= 31)], 1)
    out["freq"] = freq
    inv = (f(10000.0) ** (-np.arange(16, dtype=f) / f(16))).astype(f)[p % 16]
    ang = (np.arange(T, dtype=f)[None] * inv[:, None]).astype(f).astype(np.float64)
    out["mla_rope"] = np.stack([np.cos(ang), np.sin(ang)], 1)
    j, i = np.arange(P)[:, None], np.arange(T)[None]
    gam = 1 - 2.0 ** (-5 - np.arange(4))
    out["decay"] = np.stack([np.where(i >= j, g ** np.maximum(i - j, 0), 0) / 8 for g in gam], 1)
    out["upper"] = (i >= j) / 16.0
    q, c = np.arange(P)[:, None], np.arange(2 * B)[None]
    rel = q + B - c
    out["window"] = np.where((rel >= 0) & (rel < 128), 0, NEG)
    out["causal"] = np.where(q + np.arange(T)[None] - 127 >= 0, 0, NEG)
    j, i = np.arange(P)[:, None], np.arange(P)[None]
    out["sub"] = np.stack([(j // 16 < i // 16), (j // 16 == i // 16) & (i >= j)], 1)
    out["heads"] = (p[:, None] // 32 == np.arange(4)[None])
    hot = []
    for a, b, ok in VECS:
        d = np.arange(a, b + 1)
        h = np.zeros((BUCKETS + 1, len(d)))
        h[np.where(ok(d), t5_bucket(d), BUCKETS), np.arange(len(d))] = 1
        hot.append(h)
    out["onehot"] = np.concatenate(hot, 1)
    return {k: np.ascontiguousarray(v, dtype=f) for k, v in out.items()}


class Side:

    def __init__(self):
        self.given, self.taken, self.last = {}, {}, None
        self.job = self.seg = self.turn = self.group = self.sq = self.step = 0
        self.emptied = {"act": 0, "dve": 0}
        self.first = self.depth = 0

    def signals(self, sem):
        self.given[id(sem)] = self.given.get(id(sem), 0) + 1
        self.last = (sem, self.given[id(sem)])
        return sem

    def after(self, sem, n=1):
        self.taken[id(sem)] = self.taken.get(id(sem), 0) + n
        return self.taken[id(sem)]

    def emptied_by(self, by):
        self.emptied[by] += 1
        self.job += 1

    def begins(self, depth):
        self.first, self.depth = self.job, depth

    def bank(self):
        return (self.job - 1 - self.first) % self.depth


def build(nc, io, cst, out, stop=None):
    ctx = ExitStack()
    with ctx:
        ends = {"end": -(-nc.sbuf_base // 32) * 32}

        def sb(name, shape):
            ends[name], ends["end"] = ends["end"], ends["end"] + -(-4 * int(np.prod(shape)) // 32) * 32
            return nc.alloc_sbuf_tensor_at(name, [P] + shape, F32, offset=ends[name])

        def split(name, tiles, offset):
            return nc.alloc_sbuf_tensor_at(name, [P, tiles, T], F32R, offset=offset)

        X = sb("X", [KD, T])
        H = sb("H", [KD, T])
        Z = sb("Z", [NTILES, T])
        BIAS = sb("BIAS", [8 * HSPAN])
        RING = sb("RING", [2 * SLOTS, 8, P])
        S = sb("S", [2, WIDEST])
        E = sb("E", [2, WIDEST])
        ET = sb("ET", [2, WIDEST // B, B])
        HI = split("HI", 8, ends["E"] + 2 * TILE)
        LO = split("LO", 8, ends["H"])
        HIDDEN = split("HIDDEN", 2 * NF, ends["Z"])
        WHI = [nc.alloc_sbuf_tensor_at(f"WHI{i}", [P, 8, P], F32R, offset=ends["RING"] + (SLOTS + 2 * i) * 2 * TILE)
               for i in range(2)]
        WLO = [nc.alloc_sbuf_tensor_at(f"WLO{i}", [P, 8, P], F32R, offset=ends["RING"] + (SLOTS + 2 * i + 1) * 2 * TILE)
               for i in range(2)]
        MROPE = sb("MROPE", [2, T])
        MATS = sb("MATS", [8, P])
        SMALL = sb("SMALL", [1000])
        VECTORS = [[(0, 8, io["c"].rearrange("o (k p) -> (o k) p", p=P)),
                    (8, 48, io["b_mod"].rearrange("l (k p) -> (l k) p", p=P))],
                   [(56, 16, io["pre_norm_gain"].rearrange("l (k p) -> (l k) p", p=P)),
                    (72, 16, io["post_norm_gain"].rearrange("l (k p) -> (l k) p", p=P)),
                    (88, 32, io["ln_g_2"].rearrange("l a (k p) -> (l a k) p", p=P)),
                    (120, 3, io["od_q_norm_2"].rearrange("o (k p) -> (o k) p", p=P)),
                    (123, 2, io["od_kv_norm_2"].rearrange("o (k p) -> (o k) p", p=P)),
                    (125, 1, io["ev_subln_2"])],
                   [(126, 32, io["ln_b_2"].rearrange("l a (k p) -> (l a k) p", p=P)),
                    (158, 44, io["ffn_conv_b_2"].rearrange("l (k p) -> (l k) p", p=P)),
                    (202, 32, io["od_cmp_pe_2"][0].rearrange("kv (l two) d -> (kv l) (two d)", two=2))],
                   [(234, 66, io["ffn_conv_w_2"][0].rearrange("a (k p) -> (a k) p", p=P))],
                   [(300, 66, io["ffn_conv_w_2"][1].rearrange("a (k p) -> (a k) p", p=P))]]
        VEC = sb("VEC", [366])
        TINY = sb("TINY", [160])
        PS = ctx.enter_context(nc.psum_tensor("PS", [P, 8, T], F32))
        SCR = nc.dram_tensor("bias_vectors", [16, VEC_LEN], F32, kind="Internal").ap()

        IDN, ROT64, ROT32, ONES_D, ONES_64, ONES_128, ONES_384, ONES_256 = (MATS[:, i, :] for i in range(8))
        EPS6, EPS5, ONE = TINY[:, 0:1], TINY[:, 1:2], TINY[:, 2:3]
        FREQ, LATE = TINY[:, 4:6], TINY[:, 6:7]
        NMAX, DEN, RDEN = TINY[:, 152:160], TINY[:, 104:112], TINY[:, 112:120]
        GLAG, LAM, LTMP = TINY[:, 14:16], TINY[:, 17:18], TINY[:, 20:24]
        CT, CACT = VEC[:, 0:8], TINY[:, 56:64]
        BMOD, LNG, LNB, CONVB = (VEC[:, c0:c0 + a * n].rearrange("p (a k) -> p a k", a=a)
                                 for c0, a, n in ((8, LAYERS, 24), (88, 4, KD), (126, 4, KD), (158, LAYERS, NF)))
        PREG, POSTG = (VEC[:, c0:c0 + 16].rearrange("p (l k) -> p l k", l=LAYERS) for c0 in (56, 72))
        CONVW = VEC[:, 234:366].rearrange("p (l a k) -> p l a k", l=LAYERS, a=3)
        QG, KVG, SUBG = VEC[:, 120:123], VEC[:, 123:125], VEC[:, 125:126]
        PLACE = VEC[:, 202:234].rearrange("p (a l) -> p a l", a=2)
        VROWS = S.rearrange("p a t -> p (a t)")
        SINKS = TINY[:, 32:48]
        MOD = TINY[:, 64:88], TINY[:, 128:152]
        GA, GB = TINY[:, 88:96], TINY[:, 96:104]

        DECAY = BIAS[:, 0:2048].rearrange("p (h i) -> p h i", h=4)
        UPPER = BIAS[:, 2048:2560]
        WINDOW = BIAS[:, 2560:2816]
        SUBM = BIAS[:, 2816:3072].rearrange("p (a i) -> p a i", a=2)
        HEADS = BIAS[:, 3072:3076]
        BREF = BIAS[:, 3076:3108]
        ROPE = BIAS[:, 3584:5632].rearrange("p (a t) -> p a t", a=4)
        GK1 = BIAS[:, 5632:6400]
        BFULL4 = BIAS[:, 0:2048].rearrange("p (h x) -> p h x", h=4)
        BD4 = BIAS[:, 3072:5120].rearrange("p (h x) -> p h x", h=4)
        BWIN = BIAS[:, 2048:3072].rearrange("p (h x) -> p h x", h=4)
        BD16 = BIAS[:, 5120:7168].rearrange("p (h x) -> p h x", h=4)
        BFULL8 = BIAS[:, :].rearrange("p (h x) -> p h x", h=8)
        TABLE = SMALL[0:33, 0:16]
        GWB = [SMALL[0:17, 32 + 128 * l:160 + 128 * l] for l in range(LAYERS)]
        LAMP = SMALL[:, 600:856]
        CAUSAL = SMALL[:, 0:512]
        KCT = SMALL[:, 512:574]
        VC = SMALL[0:31, 576:704].rearrange("p (g d) -> p g d", g=2)
        H1 = SMALL[:, 704:828].rearrange("p (h c) -> p h c", h=2)
        GATES = SMALL[:, 860:956]
        def rings(depth):
            if depth == 2:
                return S, E, ET
            t, w = 2 * WIDEST // depth * depth, 2 * WIDEST // B // depth * depth
            return (S.rearrange("p a t -> p (a t)")[:, 0:t].rearrange("p (r t) -> p r t", r=depth),
                    E.rearrange("p a t -> p (a t)")[:, 0:t].rearrange("p (r t) -> p r t", r=depth),
                    ET.rearrange("p a b q -> p (a b) q")[:, 0:w].rearrange("p (r b) q -> p r b q", r=depth))
        XSUM = S[:, 1, 512:1024]
        SQ4 = S.rearrange("p a t -> p (a t)")[:, 0:2048].rearrange("p (a t) -> p a t", a=4)
        RS4 = ET.rearrange("p a b q -> p (a b q)")[:, 0:2048].rearrange("p (a t) -> p a t", a=4)
        SQ = S[:, 0, 0:1024].rearrange("p (a t) -> p a t", a=2)
        RS = S[:, 1, 0:512]
        RT = S[:, 1, 512:1024]
        GPAD = S[:, 0, 0:1032].rearrange("p (a t) -> p a t", a=2)
        GELUED = S[:, 1, 0:1024].rearrange("p (a t) -> p a t", a=2)
        CONVED = E[:, 0, 0:1024].rearrange("p (a t) -> p a t", a=2)
        PRODUCT = BIAS[:, 6144:6656]
        CMPIN = BIAS[:, 0:1984].rearrange("p (a l c) -> p a l c", a=2, l=16)

        def z(i, n=1):
            return Z[:, i, :] if n == 1 else Z[:, i:i + n, :].rearrange("p a t -> p (a t)")

        def ztok(i, tt, c0, n):
            return Z[:, i, tt * P + c0:tt * P + c0 + n]

        XIN = Z[:, 0:8, :].rearrange("p (b a) t -> p b (a t)", b=NB)
        HOT, VECS_SB = z(10, 6)[0:33, 0:VEC_LEN], z(16, 6)[0:16, 0:VEC_LEN]
        HOT_CUTS = [(c, min(T, VEC_LEN - c)) for c in range(0, VEC_LEN, T)]
        GK2 = [z(i, 2).rearrange("p (s j) -> p s j", s=8) for i in (0, 20)]
        GPROD = [z(i, 4).rearrange("p (c j) -> p c j", c=16) for i in (2, 12)]
        GQ1, GQ2 = (z(10), z(22)), (z(11), z(29))
        GS, GTMP = Z[:, 6:10, :], z(33)

        def sem(name):
            return ctx.enter_context(nc.semaphore(name))

        pe_step, act_step, dve_step = sem("pe_step"), sem("act_step"), sem("dve_step")
        pe_met, act_met, dve_met = sem("pe_met"), sem("act_met"), sem("dve_met")
        const_in, x_in, table_out, bias_in, stored = (sem(n) for n in ("const_in", "x_in", "table_out", "bias_in", "stored"))
        post_scaled, post_added = sem("post_scaled"), sem("post_added")
        mod_dve, mod_pool, pool_step = sem("mod_dve"), sem("mod_pool"), sem("pool_step")
        first_in, rows_in, c_ready, one_set = sem("first_in"), sem("rows_in"), sem("c_ready"), sem("one_set")
        loaded = [sem(f"loaded{i}") for i in range(SLOTS)]
        pair_loaded = [sem(f"pair_loaded{i}") for i in range(4)]
        w_hi, w_split, w_used, hi_ready, lo_ready = (sem(n) for n in ("w_hi", "w_split", "w_used", "hi_ready", "lo_ready"))
        acc_ready, acc_free_act, acc_free_dve = sem("acc_ready"), sem("acc_free_act"), sem("acc_free_dve")
        scores_ready, scores_free, max_ready = sem("scores_ready"), sem("scores_free"), sem("max_ready")
        exp_ready, probs_ready, turned, turn_free = sem("exp_ready"), sem("probs_ready"), sem("turned"), sem("turn_free")
        values_done, mix_free = sem("values_done"), sem("mix_free")
        sq_ready, sq_used, rstd_ready, normed = sem("sq_ready"), sem("sq_used"), sem("rstd_ready"), sem("normed")
        gla_to_act, gla_to_pe, gla_act = sem("gla_to_act"), sem("gla_to_pe"), sem("gla_act")
        gla_to_pool, keys_to_exp, keys_exp, keys_ready = (sem(n) for n in ("gla_to_pool", "keys_to_exp", "keys_exp", "keys_ready"))
        conv_ready, gelu_ready, cmp_ready = sem("conv_ready"), sem("gelu_ready"), sem("cmp_ready")
        side_dve, side_act = sem("side_dve"), sem("side_act")

        def cols(w, c0, n, k0=0, nk=KD):
            return (0, n, nk, w[k0 * P:(k0 + nk) * P, c0:c0 + n].rearrange("(k p) n -> p k n", p=P))

        def at(part, d0):
            return (d0,) + part[1:]

        def job(kind, chunks, src, dst, how="copy", by="act", m=P, **more):
            return dict(kind=kind, chunks=chunks, src=src, dst=dst, how=how, by=by, m=m, **more)

        def feat(w, c0, src, dst, m=P, nk=KD, **more):
            chunks = [[cols(w, c0, m, k0, min(8, nk - k0))] for k0 in range(0, nk, 8)]
            return job("F", chunks, src, dst, m=m, **more)

        def followed(jobs, follower):
            got = []
            for n, j in enumerate(jobs):
                got.append(j)
                if n:
                    got.append(follower(jobs[n - 1]))
            got.append(follower(jobs[-1]))
            for n, g in enumerate(got):
                if "of" in g:
                    g["back"] = n - max(k for k in range(n) if got[k] is g["of"])
            return got

        def turned_jobs(jobs):
            return followed(jobs, lambda j: dict(kind="V", chunks=[], of=j, by="act", how="turned",
                                                 to=j.get("to", j["dst"])))

        def twice(w, c0, src, dst, **more):
            part = cols(w, c0, 64)
            return job("F", [[part, at(part, 64)]], src, dst, **more)

        def with_rope(jobs, rot, cos, sin):
            return followed(jobs, lambda j: dict(kind="R", chunks=[], of=j, rot=rot, cos=cos, sin=sin, by="dve"))

        def src(k):
            return HI[:, k, :], LO[:, k, :]

        def hidden(k):
            return HIDDEN[:, k, :], HIDDEN[:, NF + k, :]

        def inputs_of(s):
            if s in ("proj", "out", "odd_out"):
                return [H[:, k, :] for k in range(KD)]
            if s == "even_out":
                return [H[:, k, :] for k in range(6)]
            if s in ("even_in", "odd_in", "up"):
                return [X[:, k, :] for k in range(KD)]
            return [z(CQ + k) for k in range(5)] if s == "odd_up" else []

        PAIRS = RING.rearrange("p s k n -> p (s k n)").rearrange("p (s k n) -> p s k n", s=4, k=8)

        MACC = E.rearrange("p a t -> p (a t)")[:, 0:1024].rearrange("p (a n) -> p a n", a=4)

        def mod_jobs(l, n):
            w = io["w_mod"][l]
            return [dict(kind="M", by="dve", how="mod", layer=l, n0=g, n=n, wide=(n == 2), turn=g // n % 4,
                         maker="dve" if n == 1 or g // n % 4 < 3 else "pool",
                         chunks=[[cols(w, g * P, n * P)]]) for g in range(0, 24, n)]

        def between(jobs, others):
            got, others = [], list(others)
            for j in jobs:
                got.append(j)
                if j["chunks"] and others:
                    got.append(others.pop(0))
            got += others
            for n, g in enumerate(got):
                if g["kind"] == "C2":
                    g["back"] = n - max(k for k in range(n) if got[k]["kind"] == "C")
                if "of" in g:
                    g["back"] = n - max(k for k in range(n) if got[k] is g["of"])
            return got

        AQ, AK, RQ, RK, AG, RG, GG, GQ, GK, AV, RV, GV, GAT, BT, Q1, Q2, LA, TMP = (
            0, 4, 6, 8, 10, 14, 16, 18, 19, 20, 21, 23, 25, 26, 27, 28, 31, 32)

        def first_jobs(l):
            w = io["w_in"][l]
            jobs = with_rope([feat(w, 128 * i, src, z(AQ + i)) for i in range(4)]
                             + [twice(w, 512 + 64 * g, src, z(AK + g)) for g in range(2)],
                             ROT64, ROPE[:, 0, :], ROPE[:, 1, :])
            jobs += with_rope([feat(w, 1280 + 128 * i, src, z(RQ + i)) for i in range(4)],
                              ROT64, ROPE[:, 2, :], ROPE[:, 3, :])
            jobs += turned_jobs([feat(w, 640, src, z(AV))] + [feat(w, 1792 + 128 * i, src, z(RV + i)) for i in range(2)]
                                + [feat(w, 2560 + 128 * i, src, z(GV + i)) for i in range(2)])
            jobs += [feat(w, 2304, src, z(GQ), scale=32 ** -0.5), feat(w, 2432, src, z(GK))]
            jobs += [feat(w, 3072, src, Z[0:16, GAT, :], m=16)]
            jobs += [feat(w, 768 + 128 * i, src, z(AG + i), how="silu") for i in range(4)]
            jobs += [feat(w, 2048 + 128 * i, src, z(RG + i), how="silu") for i in range(2)]
            jobs += [feat(w, 2816 + 128 * i, src, z(GG + i), how="silu") for i in range(2)]
            return between(jobs, mod_jobs(l + 1, 1)) if l + 1 < LAYERS else jobs

        def out_jobs(w, nk, how):
            if how == "copy":
                return [feat(w, 128 * n, src, z(n), nk=nk) for n in range(KD)]
            return [feat(w, 128 * n, src, X[:, n, :], nk=nk, how="res", by="dve", n=n) for n in range(KD)]

        QA, KA, VA, BQ, BK, BV = 0, 4, 8, 12, 18, 24

        def even_jobs():
            w = io["ev_w_in_2"][0]
            jobs = [feat(w, 128 * i, src, z(QA + i)) for i in range(4)]
            jobs += [feat(w, 512 + 128 * i, src, z(KA + i)) for i in range(4)]
            jobs += turned_jobs([feat(w, 1024 + 128 * i, src, z(VA + i)) for i in range(4)])
            for br in range(3):
                jobs += [feat(w, 1536 + 768 * br + 128 * i, src, z(BQ + 2 * br + i)) for i in range(2)]
                jobs += [feat(w, 1792 + 768 * br + 128 * i, src, z(BK + 2 * br + i)) for i in range(2)]
                jobs += turned_jobs([feat(w, 2048 + 768 * br + 128 * i, src, z(BV + 2 * br + i)) for i in range(2)])
            return jobs

        CQT, SK, WK, SV, WV, CQ, CKV, KR, QN, QR, KN, MV, CK, CV = 0, 4, 6, 8, 9, 10, 13, 15, 16, 20, 22, 26, 30, 32

        def odd_jobs():
            w = io["od_w_in_2"][0]
            jobs = []
            for kv, d in ((0, CK), (1, CV)):
                jobs += [twice(w, 512 + kv * 128 + g * 64, src, z(d + g), how="shift") for g in range(2)]
            jobs += [feat(w, 128 * i, src, z(CQT + i)) for i in range(4)]
            for br, d in ((1, SK), (2, WK)):
                jobs += [twice(w, 512 + br * 256 + g * 64, src, z(d + g)) for g in range(2)]
            jobs += turned_jobs([feat(w, 512 + 256 + 128, src, z(SV)), feat(w, 512 + 512 + 128, src, z(WV)),
                                 feat(w, 1280, src, z(QN)[0:24, :], m=24, how="sigmoid", to=GATES)])
            jobs += [feat(w, 1304 + 128 * i, src, z(CQ + i)) for i in range(3)]
            jobs += [feat(w, 1688 + 128 * i, src, z(CKV + i)) for i in range(2)]
            part = cols(w, 1944, 32)
            jobs += with_rope([job("F", [[at(part, 32 * i) for i in range(4)]], src, z(KR))], ROT32,
                              MROPE[:, 0, :], MROPE[:, 1, :])
            return jobs[:6] + between(jobs[6:], cmp_jobs())

        def cmp_jobs():
            got = []
            for kv in range(2):
                w1 = io["od_cmp_w1_2"][0, kv]
                for h in range(2):
                    got.append(dict(kind="C", by="act", how="gelu", kv=kv, h=h,
                                    chunks=[[cols(w1, 128 * h, P, 0, 8)], [cols(w1, 128 * h, P, 8, 8)]]))
                part = cols(io["od_cmp_w2_2"][0, kv], 0, 64, 0, 2)
                got.append(dict(kind="C2", by="act", how="kct" if kv == 0 else "vc", kv=kv, back=1,
                                chunks=[[part, at(part, 64)] if kv == 0 else [part]]))
            return got

        def mla_jobs():
            wq, wk, wv = io["od_w_uq_2"][0], io["od_w_uk_2"][0], io["od_w_uv_2"][0]

            def ksrc(k):
                return src(3 + k)
            jobs = with_rope([job("F", [[at(cols(wq, (4 * t + i) * 96 + 64, 32, 0, 3), 32 * i) for i in range(4)]],
                                  src, z(QR + t)) for t in range(2)], ROT32, MROPE[:, 0, :], MROPE[:, 1, :])
            jobs += [job("F", [[at(cols(wq, (2 * t + i) * 96, 64, 0, 3), 64 * i) for i in range(2)]], src, z(QN + t))
                     for t in range(4)]
            jobs += [feat(wk, 128 * t, ksrc, z(KN + t), nk=2) for t in range(4)]
            jobs += turned_jobs([feat(wv, 128 * t, ksrc, z(MV + t), nk=2) for t in range(4)])
            return jobs

        def up_jobs(l):
            w = io["ffn_w_up_2"][l]
            jobs = []
            for j in range(NF):
                jobs.append(feat(w, DFF + 128 * j, src, None, how="conv", j=j))
                jobs.append(feat(w, 128 * j, src, None, how="gate", by="dve", j=j))
            return jobs

        def down_jobs(l):
            w = io["ffn_w_down_2"][l]
            return [feat(w, 128 * n, hidden, X[:, n, :], nk=NF, how="res", by="dve", n=n) for n in range(KD)]

        def half(tile, h, t0, n):
            return Z[64 * (h % 2):64 * (h % 2) + 64, tile, t0:t0 + n]

        def hout(tile, h, b):
            return H[64 * (h % 2):64 * (h % 2) + 64, tile, b * B:b * B + B]

        def step(segs, values, dst, first, last, scale, sink=None, factor=None, late=False):
            return dict(segs=segs, values=values, dst=dst, first=first, last=last, scale=scale, sink=sink,
                        factor=factor, late=late, keys=sum(n for _, n, _ in segs))

        def back(view, x, n, stride=1):
            end = x - stride * n
            return view[:, x:(end if end >= 0 else None):-stride]

        def swa_steps(l):
            got = []
            for h in range(8):
                for b in range(NB):
                    k0 = max(0, b - 1)
                    n = (b + 1 - k0) * B
                    p0 = 64 * (h % 2)
                    seg = ([(half(AQ + h // 2, h, b * B, B), Z[p0:p0 + 64, AK + h // 4, k0 * B:k0 * B + n])], n,
                           WINDOW[:, 2 * B - n:2 * B])
                    vals = [ztok(AV, kb, 64 * (h // 4), 64) for kb in range(k0, b + 1)]
                    got.append(step([seg], vals, hout(h // 2, h, b), True, True, 64 ** -0.5,
                                    sink=SINKS[:, 8 * l + h:8 * l + h + 1]))
            return got

        def even_steps():
            got = []
            for h in range(4):
                for b in range(NB):
                    n = (b + 1) * B
                    for m in range(2):
                        t = 2 * m + h // 2
                        seg = ([(half(QA + t, h, b * B, B), half(KA + t, h, 0, n))], n, back(BFULL4[:, h, :], b * B + 127, n))
                        vals = [ztok(VA + h, kb, 0, P) for kb in range(b + 1)]
                        got.append(step([seg], vals, H[:, h, b * B:b * B + B], m == 0, m == 1, 64 ** -0.5,
                                        factor=LAM if m else None))
            for h in range(4):
                for b in range(NB):
                    segs, vals = [], []
                    for br, view in ((0, BWIN), (1, BD4), (2, BD16)):
                        k0 = max(0, b - 1) if br == 0 else 0
                        n = (b + 1 - k0) * B
                        segs.append(([(half(BQ + 2 * br + h // 2, h, b * B, B), half(BK + 2 * br + h // 2, h, k0 * B, n))],
                                     n, back(view[:, h, :], (b - k0) * B + 127, n)))
                        vals += [ztok(BV + 2 * br + h // 2, kb, 64 * (h % 2), 64) for kb in range(k0, b + 1)]
                    got.append(step(segs, vals, hout(4 + h // 2, h, b), True, True, 64 ** -0.5))
            return got

        def odd_steps():
            got = []
            for h in range(8):
                g, p0 = h // 4, 64 * (h % 2)
                for b in range(NB):
                    n = (b + 1) * B
                    q = half(CQT + h // 2, h, b * B, B)

                    def gate(br):
                        return GATES[:, b * 24 + br * 8 + h:b * 24 + br * 8 + h + 1]
                    seg = ([(q, KCT[p0:p0 + 64, 31 * g:31 * g + 31])], 31, back(BFULL8[:, h, :], B * b + 480, 31, 16))
                    got.append(step([seg], [VC[:, g, :]], None, True, False, 64 ** -0.5, factor=gate(0), late=b == 0))
                    for br, kt, vt in ((1, SK, SV), (2, WK, WV)):
                        seg = ([(q, Z[p0:p0 + 64, kt + g, 0:n])], n, back(BFULL8[:, h, :], B * b + 511, n))
                        vals = [ztok(vt, kb, 64 * g, 64) for kb in range(b + 1)]
                        got.append(step([seg], vals, hout(h // 2, h, b), False, br == 2, 64 ** -0.5, factor=gate(br)))
            for h in range(8):
                r0 = 32 * (h % 4)
                for b in range(NB):
                    n = (b + 1) * B
                    seg = ([(half(QN + h // 2, h, b * B, B), half(KN + h // 2, h, 0, n)),
                            (Z[r0:r0 + 32, QR + h // 4, b * B:b * B + B], Z[r0:r0 + 32, KR, 0:n])],
                           n, back(CAUSAL, b * B + 127, n))
                    vals = [ztok(MV + h // 2, kb, 64 * (h % 2), 64) for kb in range(b + 1)]
                    got.append(step([seg], vals, hout(4 + h // 2, h, b), True, True, 96 ** -0.5))
            return got

        stages = [("mod", 0), ("setup", 0)]
        for l in range(LAYERS):
            stages += [(s, l) for s in ("prenorm", "proj", "swa", "ret", "gla", "out", "postnorm")]
        stages += [("even_in", 0), ("even_mix", 0), ("even_sub", 0), ("even_out", 0), ("ln", 0), ("up", 0), ("down", 0),
                   ("ln", 1), ("odd_in", 0), ("odd_norms", 0), ("odd_up", 0), ("odd_mix", 0), ("odd_out", 0), ("ln", 2),
                   ("up", 1), ("down", 1), ("ln", 3)]
        if stop:
            stages = stages[:stages.index(stop) + 1]
        else:
            stages += [("store", 0)]

        def jobs_of(s, l):
            plans = {"mod": lambda: mod_jobs(l, 2), "proj": lambda: first_jobs(l),
                     "out": lambda: out_jobs(io["w_out"][l], 8, "copy"), "even_in": even_jobs,
                     "even_out": lambda: out_jobs(io["ev_w_out_2"][0], 6, "res"),
                     "odd_in": odd_jobs, "odd_up": mla_jobs,
                     "odd_out": lambda: out_jobs(io["od_w_out_2"][0], 8, "res"),
                     "up": lambda: up_jobs(l), "down": lambda: down_jobs(l)}
            return plans[s]() if s in plans else []

        def steps_of(s, l):
            if s == "even_mix":
                steps = even_steps()
                short = [s for s in steps[32:] if s["keys"] <= 768]
                return [(steps[:32], 5), (short, 3), ([s for s in steps[32:] if s["keys"] > 768], 2)]
            return [(swa_steps(l), 6)] if s == "swa" else [(odd_steps(), 5)]

        LINEAR = ("mod", "proj", "out", "even_in", "even_out", "up", "down", "odd_in", "odd_up", "odd_out")

        BANKS = {"mod": 1, "setup": len(VECTORS) - 1 + KD + len(HOT_CUTS), "prenorm": 1, "postnorm": 1, "ret": 4, "gla": 2, "even_sub": 4, "ln": 2,
                 "odd_norms": 2, "store": 8}
        def modulation(stage):
            landed, c, n_jobs, got = [0] * SLOTS, 0, 0, []
            for s, l in stages[:stages.index(stage) + 1]:
                n_jobs += BANKS.get(s, 0)
                for j in jobs_of(s, l):
                    for parts in j["chunks"]:
                        if j["kind"] == "M" and j["wide"]:
                            if (s, l) == stage:
                                got.append((j, j["turn"], 16 * (j["n0"] // 8 + 1), n_jobs))
                            continue
                        landed[c % SLOTS] += 16 * len(parts)
                        if (s, l) == stage and j["kind"] == "M":
                            got.append((j, c % SLOTS, landed[c % SLOTS], n_jobs))
                        c += 1
                    n_jobs += 1
            return got

        def split_chunks():
            c, landed, n_jobs, n_used, got = 0, [0] * SLOTS, 0, 0, []
            for s, l in stages:
                n_jobs += BANKS.get(s, 0)
                for j in jobs_of(s, l):
                    for i, parts in enumerate(j["chunks"]):
                        if j["kind"] == "M" and j["wide"]:
                            continue
                        landed[c % SLOTS] += 16 * len(parts)
                        if j["kind"] == "F":
                            last = i == len(j["chunks"]) - 1
                            n_used += not last
                            got.append((RING[:, c % SLOTS, 0:parts[0][2], :], (loaded[c % SLOTS], landed[c % SLOTS]), c,
                                        (acc_ready, n_jobs + 1) if last else (w_used, n_used)))
                        c += 1
                    n_jobs += 1
            return got

        def weights_of(j, c):
            return PAIRS[:, c] if j["wide"] else RING[:, c]

        N_CONST = [0]
        BIAS_IN = {"even_mix": 16 * 4, "odd_in": 16 * 6, "odd_up": 16 * 6, "odd_mix": 16 * 7}
        C_IN, FIRST_IN = 16 * 3, 16 * 8
        AHEAD, N_TURNS = 8, len(VECTORS) - 1 + KD
        ROWS_IN = 16 * sum(len(g) for g in VECTORS[1:])

        block = ctx.enter_context(nc.Block())

        @block.gpsimd
        def _(pool):
            n_const = [0]

            def all_met(stage):
                pool.wait_ge(act_met, stages.index(stage))
                pool.wait_ge(dve_met, stages.index(stage))
                pool.wait_ge(pe_met, stages.index(stage))

            def load(dst, src):
                n_const[0] += 1
                pool.dma_start(dst, src).then_inc(const_in, 16)

            n_steps, n_made = [0], [0]

            def products(stage):
                made = []
                for j, c, count, at_job in modulation(stage):
                    if j["maker"] != "pool":
                        continue
                    w, n, acc = weights_of(j, c), j["n"] * P, MACC[:, j["turn"], 0:j["n"] * P]
                    pool.wait_ge(pair_loaded[c], count)
                    if made:
                        pool.wait_ge(acc_ready, made[-1] + 1)
                    made.append(at_job)
                    nc.gpsimd.tensor_tensor(w, w, CACT.unsqueeze(2).broadcast_to([P, KD, n]), ALU.mult) \
                        .then_inc(pool_step, 1)
                    for k in (4, 2):
                        n_steps[0] += 1
                        pool.wait_ge(pool_step, n_steps[0])
                        nc.gpsimd.tensor_tensor(w[:, 0:k, :], w[:, 0:k, :], w[:, k:2 * k, :], ALU.add) \
                            .then_inc(pool_step, 1)
                    n_steps[0] += 1
                    pool.wait_ge(pool_step, n_steps[0])
                    ins = nc.gpsimd.tensor_tensor(acc, w[:, 0, :], w[:, 1, :], ALU.add)
                    ins.then_inc(mod_pool, 1)
                    n_made[0] += 1
                    pool.wait_ge(mod_pool, n_made[0])

            pool.wait_ge(c_ready, 1)
            products(("mod", 0))
            with nc.allow_non_contiguous_dma(reason="small operands, a feature to a partition"):
                for l in range(LAYERS):
                    load(SINKS[:, 8 * l:8 * l + 8], io["attn_sinks"][l].partition_broadcast(P))
                    load(GWB[l][0:16, :], io["gla_gate_w"][l])
                    load(GWB[l][16:17, :], io["gla_gate_b"][l:l + 1])
                    for a in range(2):
                        load(GLAG[64 * a:64 * a + 64, l:l + 1], io["gla_norm_gain"][l].rearrange("(p o) -> p o", o=1))
                load(DECAY, cst["decay"])
                load(UPPER, cst["upper"])
                load(WINDOW, cst["window"])
                load(SUBM, cst["sub"])
                load(HEADS, cst["heads"])
                load(LAMP, io["ev_lambda_2"][0].rearrange("a b -> (a b)").partition_broadcast(P))
                N_CONST[0] = 16 * n_const[0]

            def gla(l):
                def over(x, n):
                    return x.unsqueeze(1).broadcast_to([P, n, B])

                def exponents(qb):
                    keys = GK2[qb % 2]
                    if qb >= 2:
                        pool.wait_ge(gla_to_pe, 10 * l + 2 * qb)
                    nc.gpsimd.tensor_tensor(keys, BREF[:, 8 * qb:8 * qb + 8].unsqueeze(2).broadcast_to([P, 8, B]),
                                            over(z(BT)[:, qb * B:qb * B + B], 8), ALU.subtract).then_inc(pool_step, 1)
                    n_steps[0] += 1
                    pool.wait_ge(pool_step, n_steps[0])
                    nc.gpsimd.tensor_scalar(keys, keys, 0.0, None, ALU.min).then_inc(keys_to_exp, 1)

                def operands(qb):
                    for t, q in ((GQ1, Q1), (GQ2, Q2)):
                        if qb or q == Q2:
                            nc.gpsimd.tensor_tensor(t[qb % 2].rearrange("p (h i) -> p h i", h=4),
                                                    over(z(q)[:, qb * B:qb * B + B], 4),
                                                    HEADS.unsqueeze(2).broadcast_to([P, 4, B]), ALU.mult) \
                                .then_inc(pool_step, 1)
                            n_steps[0] += 1
                    n_exp[0] += 1
                    pool.wait_ge(keys_exp, n_exp[0])
                    nc.gpsimd.tensor_tensor(GK2[qb % 2], GK2[qb % 2], over(z(GK)[:, qb * B:qb * B + B], 8), ALU.mult) \
                        .then_inc(keys_ready, 1)
                pool.wait_ge(gla_to_pool, 2 * l + 1)
                exponents(0)
                pool.wait_ge(gla_to_pool, 2 * l + 2)
                operands(0)
                all_met(("gla", l))
                for qb in range(1, NB):
                    exponents(qb)
                    operands(qb)

            n_exp, chunk, chunks = [0], 0, split_chunks()
            for s, l in stages:
                if s == "gla":
                    gla(l)
                if s == "postnorm":
                    for k in range(KD):
                        pool.wait_ge(post_scaled, KD * l + k + 1)
                        nc.gpsimd.tensor_tensor(X[:, k, :], X[:, k, :], z(k), ALU.add).then_inc(post_added, 1)
                for j in jobs_of(s, l):
                    for parts in j["chunks"] if j["kind"] == "F" else []:
                        raw = chunks[chunk][0]
                        chunk += 1
                        pool.wait_ge(w_hi, chunk)
                        nk, i2 = raw.shape[1], (chunk - 1) % 2
                        nc.gpsimd.tensor_tensor(WLO[i2][:, 0:nk, :], raw, WHI[i2][:, 0:nk, :], ALU.subtract) \
                            .then_inc(w_split, 1)

        @block.sync
        def _(sp):
            freed = []
            n_jobs, n_split = 0, 0
            for s, l in stages:
                js = jobs_of(s, l)
                n_jobs += BANKS.get(s, 0)
                for n, j in enumerate(js):
                    for parts in j["chunks"]:
                        if j["kind"] == "M" and j["wide"]:
                            if n % 2 == 0:
                                if n >= 4:
                                    sp.wait_ge(acc_ready, n_jobs - 4 + 1)
                                sp.dma_start(PAIRS[:, n % 4], parts[0][3]).then_inc(pair_loaded[n % 4], 16)
                            if n == 2:
                                for g, group in enumerate(VECTORS[1:], 1):
                                    for c0, m, rows in group:
                                        r0 = c0 - group[0][0]
                                        sp.dma_start(VROWS[r0:r0 + m, g * P:g * P + P], rows).then_inc(rows_in, 16)
                                sp.dma_start(XIN, io["x"][0].rearrange("(b p) n -> p b n", p=P)).then_inc(x_in, 16)
                            continue
                        c = len(freed)
                        if c >= SLOTS:
                            sp.wait_ge(*freed[c - SLOTS])
                        elif c == 0:
                            sp.wait_ge(acc_ready, n_wide)
                        for d0, m, nk, part in parts:
                            sp.dma_start(RING[:, c % SLOTS, 0:nk, d0:d0 + m], part).then_inc(loaded[c % SLOTS], 16)
                        if j["kind"] == "F":
                            n_split += 1
                            freed.append((w_split, n_split))
                        else:
                            freed.append((acc_ready, n_jobs + 1))
                    n_jobs += 1
                if s == "mod":
                    n_wide = n_jobs + N_TURNS
            if not stop:
                sp.wait_ge(act_met, len(stages))
                sp.dma_start(out.rearrange("(b p) n -> p b n", p=P), XIN).then_inc(stored, 16)
                sp.wait_ge(stored, 16)


        @block.tensor
        def _(pe):
            me = Side()
            mm = nc.tensor.matmul
            frees = {"act": acc_free_act, "dve": acc_free_dve}
            freed = []
            at_chunk, at_split = [0], [0]
            landed = [0] * SLOTS

            def begin(by):
                if me.job >= me.depth:
                    pe.wait_ge(*freed[me.job - me.depth])
                me.emptied_by(by)
                freed.append((frees[by], me.emptied[by]))
                return PS[:, me.bank(), :]

            def done(ins):
                ins.then_inc(me.signals(acc_ready), 1)

            def slot(parts):
                c = at_chunk[0] % SLOTS
                landed[c] += 16 * len(parts)
                pe.wait_ge(loaded[c], landed[c])
                at_chunk[0] += 1
                return RING[:, c], parts[0][2]

            def linear(jobs, n_inputs):
                n_taken = 0
                for j in jobs:
                    bank = begin(j["by"])
                    m = j.get("m", P)
                    if "back" in j:
                        pe.wait_ge(*freed[me.job - 1 - j["back"]])
                    if j["kind"] == "R":
                        ins = mm(bank, j["rot"], j["of"]["dst"], start=True, stop=True)
                    elif j["kind"] == "V":
                        tile, m = j["of"]["dst"], j["of"].get("m", P)
                        for b in range(NB):
                            ins = nc.tensor.transpose(bank[:, b * m:b * m + m], tile[:, b * B:b * B + B], IDN[0:m, 0:m])
                    elif j["kind"] == "F":
                        k, total = 0, sum(parts[0][2] for parts in j["chunks"])
                        for parts in j["chunks"]:
                            nk, i2 = parts[0][2], at_split[0] % 2
                            landed[at_chunk[0] % SLOTS] += 16 * len(parts)
                            at_chunk[0] += 1
                            at_split[0] += 1
                            pe.wait_ge(w_split, at_split[0])
                            for i in range(nk):
                                hi, lo = j["src"](k)
                                if n_taken < n_inputs and (k >= n_taken or j["src"] is not src):
                                    n = 1 if j["src"] is src else n_inputs - n_taken
                                    pe.wait_ge(lo_ready, me.after(lo_ready, n))
                                    n_taken += n
                                mm(bank, WHI[i2][:, i, :], hi, start=(k == 0), stop=False)
                                mm(bank, WHI[i2][:, i, :], lo, start=False, stop=False)
                                ins = mm(bank, WLO[i2][:, i, :], hi, start=False, stop=(k == total - 1))
                                k += 1
                            if k < total:
                                ins.then_inc(me.signals(w_used), 1)
                    elif j["kind"] == "M":
                        if not j["wide"]:
                            landed[at_chunk[0] % SLOTS] += 16
                            at_chunk[0] += 1
                        if j["maker"] == "dve":
                            pe.wait_ge(mod_dve, me.after(mod_dve))
                        else:
                            pe.wait_ge(mod_pool, me.after(mod_pool))
                        for n in range(j["n"]):
                            ins = mm(bank[:, n:n + 1], MACC[:, j["turn"], n * P:n * P + P], ONE, start=True, stop=True)
                    elif j["kind"] == "C":
                        if j["kv"] == 0 and j["h"] == 0:
                            pe.wait_ge(cmp_ready, me.after(cmp_ready))
                        for a, parts in enumerate(j["chunks"]):
                            w, nk = slot(parts)
                            for i in range(nk):
                                k = 8 * a + i
                                ins = mm(bank[:, 0:62], w[:, i, :], CMPIN[:, j["kv"], k, :], start=(k == 0), stop=(k == 15))
                    elif j["kv"] == 0:
                        w, nk = slot(j["chunks"][0])
                        for i in range(2):
                            ins = mm(bank[:, 0:62], w[:, i, :], H1[:, i, :], start=(i == 0), stop=(i == 1))
                    else:
                        w, nk = slot(j["chunks"][0])
                        for g in range(2):
                            for i in range(2):
                                ins = mm(bank[0:31, g * 64:g * 64 + 64], H1[:, i, 31 * g:31 * g + 31], w[:, i, 0:64],
                                         start=(i == 0), stop=(i == 1))
                    done(ins)

            def sums(ones, n):
                bank = begin("act")
                for k in range(n):
                    pe.wait_ge(sq_ready, me.sq + 1)
                    ins = mm(bank, ones, SQ[:, me.sq % 2, :], start=(k == 0), stop=(k == n - 1))
                    me.sq += 1
                    if k < n - 1:
                        ins.then_inc(me.signals(sq_used), 1)
                done(ins)

            def head_sums(ones, n):
                for i in range(n):
                    bank = begin("act")
                    pe.wait_ge(sq_ready, me.sq + 1)
                    done(mm(bank, ones, SQ4[:, i, :], start=True, stop=True))
                    me.sq += 1

            def score_bank():
                if me.seg - 1 > 0:
                    pe.wait_ge(scores_free, me.seg - 1)
                me.seg += 1
                return PS[:, 2 + (me.seg - 1) % 2, :]

            def wide_score_bank():
                if me.seg - 3 > 0:
                    pe.wait_ge(scores_free, me.seg - 3)
                me.seg += 1
                return PS[:, (me.seg - 1) % 4, :]

            def mix_bank():
                if me.group - 1 > 0:
                    pe.wait_ge(mix_free, me.group - 1)
                return PS[:, 6 + me.group % 2, :]

            def attention(steps, depth):
                n, base, turns = len(steps), me.step, {}
                _, es, ets = rings(depth)

                def scores(i):
                    for pairs, keys, _ in steps[i]["segs"]:
                        bank = wide_score_bank()
                        for a, (q, k) in enumerate(pairs):
                            ins = mm(bank[:, 0:keys], q, k, start=(a == 0), stop=(a == len(pairs) - 1))
                        ins.then_inc(me.signals(scores_ready), 1)

                def turn(i):
                    pe.wait_ge(probs_ready, base + i + 1)
                    keys = steps[i]["keys"]
                    for c0 in range(0, keys, 4 * B):
                        if me.turn - 1 > 0:
                            pe.wait_ge(turn_free, me.turn - 1)
                        bank = PS[:, 4 + me.turn % 2, :]
                        for c in range(c0, min(keys, c0 + 4 * B), B):
                            w = min(B, keys - c)
                            ins = nc.tensor.transpose(bank[0:w, c - c0:c - c0 + B], es[:, i % depth, c:c + w], IDN)
                        ins.then_inc(me.signals(turned), 1)
                        me.turn += 1
                    turns[i] = me.turn

                def values(i):
                    s = steps[i]
                    pe.wait_ge(turn_free, turns[i])
                    bank = mix_bank()
                    for a, v in enumerate(s["values"]):
                        w = min(B, s["keys"] - a * B)
                        ins = mm(bank[0:v.shape[1], 0:B], v, ets[0:w, i % depth, a, :], start=(s["first"] and a == 0),
                                 stop=(s["last"] and a == len(s["values"]) - 1))
                    ins.then_inc(me.signals(values_done), 1)
                    me.group += s["last"]
                for i in range(n + depth):
                    if i < n:
                        scores(i)
                    if 0 <= i - depth + 1 < n:
                        turn(i - depth + 1)
                    if i >= depth:
                        values(i - depth)
                me.step += n

            def retention(heads):
                for h in heads:
                    t, p0 = h // 2, 64 * (h % 2)
                    o = mix_bank()[0:64, :]

                    def value(jb):
                        pe.wait_ge(scores_free, me.seg - (jb < NB - 1))
                        mm(o[:, jb * B:T], ztok(RV + t, jb, p0, 64), E[:, jb % 2, 0:T - jb * B], start=(jb == 0),
                            stop=(jb == NB - 1), skip_group_check=True) \
                            .then_inc(me.signals(values_done), 1)
                    for jb in range(NB):
                        mm(score_bank()[:, 0:T - jb * B], Z[p0:p0 + 64, RK + t, jb * B:jb * B + B],
                            Z[p0:p0 + 64, RQ + t, jb * B:T], start=True, stop=True) \
                            .then_inc(me.signals(scores_ready), 1)
                        if jb:
                            value(jb - 1)
                    value(NB - 1)
                    me.group += 1

            def gate_logits(l):
                pe.wait_ge(gla_to_pe, me.after(gla_to_pe))
                bank = begin("dve")
                for tt in range(NB):
                    ins = mm(bank[:, tt * B:tt * B + B], Z[0:17, GAT, tt * B:tt * B + B], GWB[l], start=True, stop=True)
                done(ins)

            def running_sums():
                pe.wait_ge(gla_to_pe, me.after(gla_to_pe))
                bank = begin("act")
                for a in range(NB):
                    ins = mm(bank[:, a * B:T], z(LA)[:, a * B:a * B + B], UPPER[:, 0:T - a * B], start=(a == 0),
                             stop=(a == NB - 1), skip_group_check=True)
                done(ins)

            def gla():
                for qb in range(NB):
                    pe.wait_ge(keys_ready, me.after(keys_ready))
                    pe.wait_ge(gla_to_pe, me.after(gla_to_pe))
                    for jb in range(qb):
                        bank = score_bank()
                        k0 = (0, 0, 128, 384)[qb] + jb * B
                        mm(bank, GK1[:, k0:k0 + B], GQ1[qb % 2], start=True, stop=True).then_inc(me.signals(scores_ready), 1)
                    bank = score_bank()
                    for a in range(8):
                        c = slice(16 * a, 16 * a + 16)
                        ins = mm(bank.rearrange("p (h i) -> p h i", h=4)[:, :, c], GK2[qb % 2][:, a, :],
                                 GQ2[qb % 2].rearrange("p (h i) -> p h i", h=4)[:, :, c], start=True, stop=True)
                    ins.then_inc(me.signals(scores_ready), 1)
                    bank = score_bank()
                    for c in range(16):
                        ins = mm(bank[:, 4 * c:4 * c + 4], GPROD[qb % 2][:, c, :], HEADS, start=True, stop=True)
                    ins.then_inc(me.signals(scores_ready), 1)
                    o = mix_bank()[0:64, :]
                    pe.wait_ge(gla_to_pe, me.after(gla_to_pe))
                    for h in range(4):
                        for jb in range(qb + 1):
                            ins = mm(o[:, h * B:h * B + B], ztok(GV + h // 2, jb, 64 * (h % 2), 64),
                                     GS[:, jb, h * B:h * B + B], start=(jb == 0), stop=(jb == qb))
                    ins.then_inc(me.signals(values_done), 1)
                    me.group += 1

            for n_met, (s, l) in enumerate(stages, 1):
                me.begins(4 if s in LINEAR or s == "even_sub" else 2)
                if s == "swa" and l == 0:
                    pe.wait_ge(const_in, N_CONST[0])
                if s == "mod":
                    pe.wait_ge(first_in, C_IN)
                    bank = begin("act")
                    done(nc.tensor.transpose(bank[:, 0:56], VROWS[0:56, 0:P], IDN[0:56, 0:56]))
                    pe.wait_ge(one_set, 1)
                    linear(jobs_of(s, l)[:AHEAD], 0)
                    pe.wait_ge(rows_in, ROWS_IN)
                    for g, group in enumerate(VECTORS[1:], 1):
                        n = sum(n for _, n, _ in group)
                        bank = begin("act")
                        done(nc.tensor.transpose(bank[:, 0:n], VROWS[0:n, g * P:g * P + P], IDN[0:n, 0:n]))
                    pe.wait_ge(first_in, FIRST_IN)
                    pe.wait_ge(x_in, 16)
                    for k in range(KD):
                        bank = begin("act")
                        for b in range(NB):
                            ins = nc.tensor.transpose(bank[:, b * B:b * B + B], XIN[:, b, k * P:k * P + P], IDN)
                        done(ins)
                    linear(jobs_of(s, l)[AHEAD:], 0)
                elif s == "setup":
                    pe.wait_ge(side_dve, me.after(side_dve))
                    for c, w in HOT_CUTS:
                        bank = begin("dve")
                        done(mm(bank[0:16, 0:w], TABLE, HOT[:, c:c + w], start=True, stop=True))
                elif s in ("prenorm", "postnorm"):
                    sums(ONES_D, KD)
                elif s == "ln":
                    bank = begin("dve")
                    done(mm(bank, ONES_D, XSUM, start=True, stop=True))
                    sums(ONES_D, KD)
                elif s in ("swa", "even_mix", "odd_mix"):
                    for steps, depth in steps_of(s, l):
                        attention(steps, depth)
                elif s == "ret":
                    gate_logits(l)
                    retention([0])
                    running_sums()
                    retention([1, 2, 3])
                    head_sums(ONES_64, 2)
                elif s == "gla":
                    gla()
                    head_sums(ONES_64, 2)
                elif s == "even_sub":
                    head_sums(ONES_128, 4)
                elif s == "odd_norms":
                    sums(ONES_384, 3)
                    sums(ONES_256, 2)
                elif s == "store":
                    for n in range(8):
                        bank = begin("act")
                        b, c = n // 2, n % 2
                        for i in range(4):
                            ins = nc.tensor.transpose(bank[:, i * P:i * P + P], X[:, 4 * c + i, b * B:b * B + B], IDN)
                        done(ins)
                else:
                    linear(jobs_of(s, l), len(inputs_of(s)))
                pe.wait_ge(*me.last)
                pe.sem_inc(pe_met, 1)
                pe.wait_ge(act_met, n_met)
                pe.wait_ge(dve_met, n_met)

        @block.scalar
        def _(act):
            me = Side()
            fn = nc.scalar.activation
            vals = [0]
            squared = []
            inner = [0]

            def take():
                me.emptied_by("act")
                act.wait_ge(acc_ready, me.job)
                return PS[:, me.bank(), :]

            def stat(tiles, eps):
                for k, t in enumerate(tiles):
                    if me.sq >= 2:
                        act.wait_ge(*squared[me.sq - 2])
                    fn(SQ[:, me.sq % 2, :], t, ACT.Square).then_inc(me.signals(sq_ready), 1)
                    me.sq += 1
                    if k < len(tiles) - 1:
                        inner[0] += 1
                        squared.append((sq_used, inner[0]))
                    else:
                        squared.append((acc_ready, me.job + 1))
                bank = take()
                act.wait_ge(*me.last)
                fn(RS, bank, ACT.Ln, bias=eps).then_inc(me.signals(acc_free_act), 1)
                act.wait_ge(*me.last)
                fn(RS, RS, ACT.Exp, scale=-0.5).then_inc(me.signals(rstd_ready), 1)

            def inputs(tiles):
                for k, t in enumerate(tiles):
                    fn(HI[:, k, :], t, ACT.Copy).then_inc(me.signals(hi_ready), 1)

            def hankel(view, vec, c0, start):
                n_bias[0] += 1
                act.dma_start(view, bass.AP(tensor=SCR.tensor, offset=c0 * VEC_LEN + int(VEC_AT[vec]) + start,
                                            ap=[[1, P], [VEC_LEN, view.shape[1]], [1, view.shape[2]]])) \
                    .then_inc(bias_in, 16)

            n_bias, n_hi, at_split, chunks = [0], [0], [0], split_chunks()

            def weights(upto):
                while n_hi[0] < min(upto, len(chunks)):
                    raw, landed, _, _ = chunks[n_hi[0]]
                    act.wait_ge(*landed)
                    if n_hi[0] >= 2:
                        act.wait_ge(*chunks[n_hi[0] - 2][3])
                    fn(WHI[n_hi[0] % 2][:, 0:raw.shape[1], :], raw, ACT.Copy).then_inc(w_hi, 1)
                    n_hi[0] += 1

            def gelu(n):
                act.wait_ge(conv_ready, n_gelu[0] + 1)
                n_gelu[0] += 1
                fn(GELUED[:, n % 2, :], CONVED[:, n % 2, :], ACT.Gelu_apprx_tanh).then_inc(me.signals(gelu_ready), 1)

            n_gelu = [0]

            def linear(jobs, l):
                n = 0
                weights(at_split[0] + 1)
                for j in jobs:
                    for _ in j["chunks"] if j["kind"] == "F" else []:
                        at_split[0] += 1
                        m = at_split[0]
                        if m < len(chunks) and chunks[m][2] - chunks[m - 1][2] <= SLOTS:
                            weights(m + 1)
                    if j["by"] != "act":
                        if j["how"] == "gate" if j["kind"] == "F" else False:
                            gelu(n - 1)
                        me.emptied_by(j["by"])
                        continue
                    bank = take()
                    how, m = j["how"], j.get("m", P)
                    if how == "copy" and "scale" in j:
                        fn(j["dst"], bank[0:m, :], ACT.Copy, scale=j["scale"]).then_inc(me.signals(acc_free_act), 1)
                    elif how == "copy":
                        fn(j["dst"], bank[0:m, :], ACT.Copy).then_inc(me.signals(acc_free_act), 1)
                    elif how == "silu":
                        fn(j["dst"], bank, ACT.Silu).then_inc(me.signals(acc_free_act), 1)
                    elif how == "shift":
                        fn(j["dst"][0:64, :], bank[0:64, :], ACT.Copy).then_inc(me.signals(act_step), 1)
                        fn(j["dst"][64:128, 0:T - 1], bank[64:128, 1:T], ACT.Copy).then_inc(me.signals(acc_free_act), 1)
                    elif how == "sigmoid":
                        fn(j["dst"], bank[0:m, :], ACT.Sigmoid).then_inc(me.signals(acc_free_act), 1)
                    elif how == "turned":
                        fn(j["to"], bank[:, 0:j["to"].shape[1]], ACT.Copy).then_inc(me.signals(acc_free_act), 1)
                    elif how == "gelu":
                        act.wait_ge(*me.last)
                        fn(H1[:, j["h"], :], bank[:, 0:62], ACT.Gelu_apprx_tanh).then_inc(me.signals(acc_free_act), 1)
                    elif how == "kct":
                        fn(KCT, bank[:, 0:62], ACT.Copy).then_inc(me.signals(acc_free_act), 1)
                    elif how == "vc":
                        fn(VC, bank[0:31, 0:128].rearrange("p (g d) -> p g d", g=2), ACT.Copy) \
                            .then_inc(me.signals(acc_free_act), 1)
                    elif how == "conv":
                        fn(GPAD[:, n % 2, 2:T + 2], bank, ACT.Copy).then_inc(me.signals(acc_free_act), 1)
                        n += 1
                weights(at_split[0] + 1)

            def attention(steps, depth):
                n, base, turns, t = len(steps), me.step, [], me.turn
                ss, es, ets = rings(depth)
                for s in steps:
                    t += -(-s["keys"] // (4 * B))
                    turns.append(t)

                def exps(i):
                    s, r = steps[i], i % depth
                    act.wait_ge(max_ready, base + i + 1)
                    if i >= depth:
                        act.wait_ge(turned, turns[i - depth])
                    keys = s["keys"] + (s["sink"] is not None)
                    fn(es[:, r, 0:keys], ss[:, r, 0:keys], ACT.Exp, bias=NMAX[:, r:r + 1], scale=1.0,
                        accum_out=DEN[:, r:r + 1]) \
                        .then_inc(me.signals(exp_ready), 1)

                def collect(i):
                    s, r = steps[i], i % depth
                    if i >= depth:
                        act.wait_ge(values_done, vals[0] + i - depth + 1)
                    w = min(B, s["keys"])
                    for c0 in range(0, s["keys"], 4 * B):
                        me.turn += 1
                        act.wait_ge(turned, me.turn)
                        nb = -(-min(4 * B, s["keys"] - c0) // B)
                        fn(ets[0:w, r, c0 // B:c0 // B + nb, :],
                            PS[0:w, 4 + (me.turn - 1) % 2, 0:nb * B].rearrange("p (a q) -> p a q", a=nb), ACT.Copy) \
                            .then_inc(me.signals(turn_free), 1)

                def mixed(i):
                    s = steps[i]
                    if s["last"]:
                        act.wait_ge(values_done, vals[0] + i + 1)
                        fn(s["dst"], PS[0:s["values"][0].shape[1], 6 + me.group % 2, 0:B], ACT.Copy) \
                            .then_inc(me.signals(mix_free), 1)
                        me.group += 1
                for i in range(n + depth):
                    if 0 <= i - depth + 1 < n:
                        collect(i - depth + 1)
                    if i < n:
                        exps(i)
                    if i >= depth:
                        mixed(i - depth)
                me.step += n
                vals[0] += n

            def retention(heads):
                for h in heads:
                    vals[0] += NB
                    act.wait_ge(values_done, vals[0])
                    fn(H[64 * (h % 2):64 * (h % 2) + 64, 4 + h // 2, :], PS[0:64, 6 + me.group % 2, :], ACT.Copy) \
                        .then_inc(me.signals(mix_free), 1)
                    me.group += 1

            def log_decays():
                me.emptied_by("dve")
                act.wait_ge(gla_to_act, me.after(gla_to_act))
                act.wait_ge(*me.last)
                fn(z(TMP), z(TMP), ACT.Exp, scale=-1.0).then_inc(me.signals(act_step), 1)
                act.wait_ge(*me.last)
                fn(z(TMP), z(TMP), ACT.Ln, bias=ONE).then_inc(me.signals(gla_act), 1)

            def running_sums():
                bank = take()
                act.wait_ge(*me.last)
                fn(z(BT), bank, ACT.Copy).then_inc(me.signals(acc_free_act), 1)

            def decays():
                act.wait_ge(gla_to_act, me.after(gla_to_act))
                fn(z(Q1)[:, B:T], z(Q1)[:, B:T], ACT.Exp).then_inc(me.signals(act_step), 1)
                fn(z(Q2), z(Q2), ACT.Exp).then_inc(me.signals(act_step), 1)
                fn(GK1, GK1, ACT.Exp).then_inc(me.signals(gla_act), 1)

            def within(qb):
                act.wait_ge(keys_to_exp, me.after(keys_to_exp))
                fn(GK2[qb % 2], GK2[qb % 2], ACT.Exp).then_inc(me.signals(keys_exp), 1)
                act.wait_ge(gla_to_act, me.after(gla_to_act))
                fn(GPROD[qb % 2], GPROD[qb % 2], ACT.Exp).then_inc(me.signals(gla_act), 1)

            def gla():
                for qb in range(NB):
                    if qb + 1 < NB:
                        within(qb + 1)
                    vals[0] += 1
                    act.wait_ge(values_done, vals[0])
                    o = PS[0:64, 6 + me.group % 2, :].rearrange("p (a b i) -> p a b i", a=2, b=2)
                    fn(H[0:64, 6:8, qb * B:qb * B + B], o[:, :, 0, :], ACT.Copy).then_inc(me.signals(act_step), 1)
                    fn(H[64:128, 6:8, qb * B:qb * B + B], o[:, :, 1, :], ACT.Copy).then_inc(me.signals(mix_free), 1)
                    me.group += 1

            def head_stats(tiles, eps):
                n = len(tiles)
                for i, t in enumerate(tiles):
                    if i < 2:
                        act.wait_ge(*me.last)
                    fn(SQ4[:, i, :], t, ACT.Square).then_inc(me.signals(sq_ready), 1)
                for i in range(n):
                    squared.append((acc_ready, me.job + 1))
                    me.sq += 1
                    bank = take()
                    fn(RS4[:, i, :], bank, ACT.Ln, bias=eps).then_inc(me.signals(acc_free_act), 1)
                act.wait_ge(*me.last)
                fn(RS4[:, 0:n, :], RS4[:, 0:n, :], ACT.Exp, scale=-0.5).then_inc(me.signals(rstd_ready), 1)
                act.wait_ge(normed, me.after(normed, n))

            def stats(groups, eps):
                act.wait_ge(*me.last)
                for tiles in groups:
                    stat(tiles, eps)
                    act.wait_ge(normed, me.after(normed, len(tiles)))

            for n_met, (s, l) in enumerate(stages, 1):
                me.begins(4 if s in LINEAR or s == "even_sub" else 2)
                if s == "even_in":
                    hankel(BFULL4, 0, 0, 511 - 127)
                    hankel(BWIN, 1, 4, 0)
                    hankel(BD4, 2, 8, 0)
                    hankel(BD16, 3, 12, 0)
                if s == "even_sub":
                    act.dma_start(MROPE[:, :, :], cst["mla_rope"]).then_inc(bias_in, 16)
                    act.dma_start(CAUSAL, cst["causal"]).then_inc(bias_in, 16)
                if s == "odd_norms":
                    hankel(BFULL8, 0, 0, 0)
                if s == "mod":
                    pairs = [j["chunks"][0][0][3] for j in jobs_of(s, l)]
                    for c0, n, src in VECTORS[0]:
                        act.dma_start(VROWS[c0:c0 + n, 0:P], src).then_inc(first_in, 16)
                    act.dma_start(IDN, cst["mats"][:, 0, :]).then_inc(first_in, 16)
                    for i in (1, 3):
                        act.dma_start(PAIRS[:, i], pairs[i]).then_inc(pair_loaded[i], 16)
                    bank = take()
                    fn(VEC[:, 0:56], bank[:, 0:56], ACT.Copy).then_inc(me.signals(acc_free_act), 1)
                    act.wait_ge(*me.last)
                    fn(CACT, CT, ACT.Silu).then_inc(c_ready, 1)
                    act.dma_start(MATS[:, 1:8, :], cst["mats"][:, 1:8, :]).then_inc(first_in, 16)
                    act.dma_start(z(22).bitcast(I32), io["positions"][0].partition_broadcast(P)).then_inc(first_in, 16)
                    act.dma_start(TINY[:, 4:7], cst["freq"]).then_inc(first_in, 16)
                    act.dma_start(HOT, cst["onehot"]).then_inc(first_in, 16)
                    act.dma_start(TABLE[0:32, :], io["rel_bias_2"]).then_inc(first_in, 16)
                    for i in range(5, len(pairs), 2):
                        act.wait_ge(acc_ready, i - 2)
                        act.dma_start(PAIRS[:, i % 4], pairs[i]).then_inc(pair_loaded[i % 4], 16)
                    for _ in range(AHEAD):
                        me.emptied_by("dve")
                    for group in VECTORS[1:]:
                        c0, n = group[0][0], sum(n for _, n, _ in group)
                        bank = take()
                        fn(VEC[:, c0:c0 + n], bank[:, 0:n], ACT.Copy).then_inc(me.signals(acc_free_act), 1)
                    for k in range(KD):
                        bank = take()
                        fn(X[:, k, :], bank, ACT.Copy).then_inc(me.signals(acc_free_act), 1)
                    for _ in range(len(pairs) - AHEAD):
                        me.emptied_by("dve")
                if s == "swa" and l == 0:
                    act.wait_ge(const_in, N_CONST[0])
                if s == "setup":
                    for _ in HOT_CUTS:
                        me.emptied_by("dve")
                    act.wait_ge(acc_free_dve, me.emptied["dve"])
                    act.dma_start(SCR, VECS_SB).then_inc(table_out, 16)
                    weights(1)
                elif s == "prenorm":
                    stat([X[:, k, :] for k in range(KD)], EPS6)
                    for k in range(KD):
                        act.wait_ge(normed, me.after(normed))
                        fn(H[:, k, :], H[:, k, :], ACT.Identity, bias=MOD[l][:, k:k + 1], scale=1.0) \
                            .then_inc(me.signals(act_step), 1)
                    if l == 0:
                        act.wait_ge(side_dve, me.after(side_dve, 2))
                        for n in range(2):
                            fn(ROPE[:, 2 * n, :], z(24 + 3 * n), ACT.Sin).then_inc(me.signals(act_step), 1)
                            fn(ROPE[:, 2 * n + 1, :], z(23 + 3 * n), ACT.Sin).then_inc(me.signals(act_step), 1)
                elif s == "postnorm":
                    stat([z(k) for k in range(KD)], EPS6)
                    act.wait_ge(post_scaled, KD * (l + 1))
                elif s == "ln":
                    me.emptied_by("dve")
                    act.wait_ge(normed, me.after(normed, KD))
                    stat([X[:, k, :] for k in range(KD)], EPS5)
                    for k in range(KD):
                        act.wait_ge(normed, me.after(normed))
                        fn(X[:, k, :], X[:, k, :], ACT.Identity, bias=LNB[:, l, k:k + 1], scale=1.0) \
                            .then_inc(me.signals(act_step), 1)
                elif s in ("swa", "even_mix", "odd_mix"):
                    for steps, depth in steps_of(s, l):
                        attention(steps, depth)
                elif s == "ret":
                    log_decays()
                    retention([0])
                    running_sums()
                    retention([1])
                    decays()
                    retention([2])
                    within(0)
                    retention([3])
                    head_stats([H[:, 4 + t, :] for t in range(2)], EPS6)
                elif s == "gla":
                    gla()
                    head_stats([H[:, 6 + t, :] for t in range(2)], EPS6)
                elif s == "even_sub":
                    head_stats([H[:, t, :] for t in range(4)], EPS5)
                elif s == "odd_norms":
                    stats([[z(CQ + i) for i in range(3)], [z(CKV + i) for i in range(2)]], EPS5)
                elif s == "store":
                    for n in range(8):
                        bank = take()
                        fn(z(n), bank, ACT.Copy).then_inc(me.signals(acc_free_act), 1)
                elif s != "mod":
                    inputs(inputs_of(s))
                    linear(jobs_of(s, l), l)
                if s == "even_in":
                    act.wait_ge(side_dve, me.after(side_dve))
                    act.wait_ge(*me.last)
                    fn(LTMP[:, 2:4], LTMP[:, 0:2], ACT.Exp).then_inc(me.signals(side_act), 1)
                act.wait_ge(*me.last)
                act.sem_inc(act_met, 1)
                act.wait_ge(pe_met, n_met)
                act.wait_ge(dve_met, n_met)

        @block.vector
        def _(dve):
            me = Side()
            tt, ts, stt = nc.vector.tensor_tensor, nc.vector.tensor_scalar, nc.vector.scalar_tensor_tensor
            vals = [0]

            def take():
                me.emptied_by("dve")
                dve.wait_ge(acc_ready, me.job)
                return PS[:, me.bank(), :]

            def rope(j):
                bank, d = take(), j["of"]["dst"]
                dve.wait_ge(*me.last)
                tt(RT, bank, j["sin"], ALU.mult).then_inc(me.signals(acc_free_dve), 1)
                dve.wait_ge(*me.last)
                tt(d, d, j["cos"], ALU.mult).then_inc(me.signals(dve_step), 1)
                dve.wait_ge(*me.last)
                tt(d, d, RT, ALU.add).then_inc(me.signals(dve_step), 1)

            def products(j, c, count):
                w, n, acc = weights_of(j, c), j["n"] * P, MACC[:, j["turn"], 0:j["n"] * P]
                dve.wait_ge((pair_loaded if j["wide"] else loaded)[c], count)
                dve.wait_ge(*me.last)
                ts(acc, w[:, 0, 0:n], CACT[:, 0:1], None, ALU.mult).then_inc(me.signals(dve_step), 1)
                for k in range(1, KD):
                    dve.wait_ge(*me.last)
                    stt(acc, w[:, k, 0:n], CACT[:, k:k + 1], acc, ALU.mult, ALU.add) \
                        .then_inc(me.signals(dve_step if k < KD - 1 else mod_dve), 1)

            def modulate(j):
                bank = take()
                dve.wait_ge(*me.last)
                tt(MOD[j["layer"]][:, j["n0"]:j["n0"] + j["n"]], bank[:, 0:j["n"]],
                    BMOD[:, j["layer"], j["n0"]:j["n0"] + j["n"]], ALU.add) \
                    .then_inc(me.signals(acc_free_dve), 1)

            def linear(jobs, l):
                n = 0
                made = [m[:3] for m in modulation(("proj", l))] if any(j["kind"] == "M" for j in jobs) else []
                for m in made[0:1]:
                    products(*m)
                for j in jobs:
                    if j["kind"] == "C" and j["kv"] == 0 and j["h"] == 0:
                        dve.wait_ge(acc_free_act, me.emptied["act"])
                        dve.wait_ge(bias_in, BIAS_IN["odd_in"])
                        for kv in range(2):
                            for g in range(2):
                                src = z((CK, CV)[kv] + g)
                                win = bass.AP(tensor=src.tensor, offset=src.offset, ap=[list(src.ap[0]), [2, 16], [16, 31]])
                                dve.wait_ge(*me.last)
                                tt(CMPIN[:, kv, :, 31 * g:31 * g + 31], win,
                                    PLACE[:, kv, :].unsqueeze(2).broadcast_to([P, 16, 31]), ALU.add) \
                                    .then_inc(me.signals(cmp_ready if kv + g == 2 else dve_step), 1)
                    if j["by"] != "dve":
                        me.emptied_by(j["by"])
                        if j["how"] == "conv":
                            dve.wait_ge(acc_free_act, me.emptied["act"])
                            g, c, a = GPAD[:, n % 2, :], CONVED[:, n % 2, :], j["j"]
                            tap = [CONVW[:, l, i, a:a + 1] for i in range(3)] + [CONVB[:, l, a:a + 1]]
                            dve.wait_ge(*me.last)
                            ts(c, g[:, 2:T + 2], tap[2], tap[3], ALU.mult, ALU.add).then_inc(me.signals(dve_step), 1)
                            dve.wait_ge(*me.last)
                            stt(c, g[:, 1:T + 1], tap[1], c, ALU.mult, ALU.add).then_inc(me.signals(dve_step), 1)
                            dve.wait_ge(*me.last)
                            stt(c, g[:, 0:T], tap[0], c, ALU.mult, ALU.add).then_inc(me.signals(conv_ready), 1)
                        continue
                    if j["kind"] == "R":
                        rope(j)
                    elif j["kind"] == "M":
                        modulate(j)
                        made.pop(0)
                        for m in made[0:1]:
                            products(*m)
                    elif j["how"] == "gate":
                        bank = take()
                        dve.wait_ge(gelu_ready, me.after(gelu_ready))
                        dve.wait_ge(*me.last)
                        tt(HIDDEN[:, n, :], bank, GELUED[:, n % 2, :], ALU.mult).then_inc(me.signals(dve_step), 1)
                        tt(PRODUCT, bank, GELUED[:, n % 2, :], ALU.mult).then_inc(me.signals(acc_free_dve), 1)
                        dve.wait_ge(*me.last)
                        tt(HIDDEN[:, NF + n, :], PRODUCT, HIDDEN[:, n, :], ALU.subtract).then_inc(me.signals(dve_step), 1)
                        n += 1
                    elif j["how"] == "res":
                        bank = take()
                        dve.wait_ge(*me.last)
                        stt(j["dst"], j["dst"], ALPHA, bank, ALU.mult, ALU.add).then_inc(me.signals(acc_free_dve), 1)
                        if j["n"] == 1:
                            dve.wait_ge(*me.last)
                            tt(XSUM, X[:, 0, :], X[:, 1, :], ALU.add).then_inc(me.signals(dve_step), 1)
                        elif j["n"]:
                            dve.wait_ge(*me.last)
                            tt(XSUM, XSUM, j["dst"], ALU.add).then_inc(me.signals(dve_step), 1)

            def attention(steps, depth):
                n, base, lag = len(steps), me.step, 2 if depth > 3 else 1
                ss, es, _ = rings(depth)

                def scaled(i):
                    s, r, c = steps[i], i % depth, 0
                    for _, keys, bias in s["segs"]:
                        me.seg += 1
                        dve.wait_ge(scores_ready, me.seg)
                        stt(ss[:, r, c:c + keys], PS[:, (me.seg - 1) % 4, 0:keys], s["scale"], bias, ALU.mult,
                            ALU.add) \
                            .then_inc(me.signals(scores_free), 1)
                        c += keys
                    if s["sink"] is not None:
                        nc.vector.tensor_copy(ss[:, r, c:c + 1], s["sink"]).then_inc(me.signals(dve_step), 1)
                    return me.last

                def recips(i):
                    s, r = steps[i], i % depth
                    dve.wait_ge(exp_ready, base + i + 1)
                    nc.vector.reciprocal(RDEN[:, r:r + 1], DEN[:, r:r + 1]).then_inc(me.signals(dve_step), 1)
                    if s["late"]:
                        dve.wait_ge(*me.last)
                        tt(RDEN[:, r:r + 1], RDEN[:, r:r + 1], LATE, ALU.mult).then_inc(me.signals(dve_step), 1)
                    return me.last

                def maximum(i, written):
                    s, r = steps[i], i % depth
                    dve.wait_ge(*written)
                    nc.vector.tensor_reduce(NMAX[:, r:r + 1], ss[:, r, 0:s["keys"] + (s["sink"] is not None)], AX.X,
                                            ALU.max, negate=True) \
                        .then_inc(me.signals(max_ready), 1)

                def normalise(i, written):
                    s, r = steps[i], i % depth
                    e = es[:, r, 0:s["keys"]]
                    dve.wait_ge(*written)
                    if s["factor"] is None:
                        ts(e, e, RDEN[:, r:r + 1], None, ALU.mult).then_inc(me.signals(probs_ready), 1)
                    else:
                        ts(e, e, RDEN[:, r:r + 1], s["factor"], ALU.mult, ALU.mult).then_inc(me.signals(probs_ready), 1)
                for i in range(n + lag):
                    if i < n:
                        written = scaled(i)
                    if i >= lag:
                        inverted = recips(i - lag)
                    if i < n:
                        maximum(i, written)
                    if i >= lag:
                        normalise(i - lag, inverted)
                me.step += n
                vals[0] += n

            def retention(heads):
                for h in heads:
                    for jb in range(NB):
                        me.seg += 1
                        dve.wait_ge(scores_ready, me.seg)
                        if jb >= 2 or h:
                            if vals[0] - 1 > 0:
                                dve.wait_ge(values_done, vals[0] - 1)
                        vals[0] += 1
                        w = T - jb * B
                        dve.wait_ge(*me.last)
                        tt(E[:, jb % 2, 0:w], PS[:, 2 + (me.seg - 1) % 2, 0:w], DECAY[:, h, 0:w], ALU.mult) \
                            .then_inc(me.signals(scores_free), 1)

            def gate_input():
                dve.wait_ge(*me.last)
                nc.vector.tensor_copy(GTMP[0:16, :], z(GAT)[0:16, :]).then_inc(me.signals(dve_step), 1)
                dve.wait_ge(*me.last)
                nc.vector.memset(z(GAT)[0:32, :], 1.0).then_inc(me.signals(dve_step), 1)
                dve.wait_ge(*me.last)
                nc.vector.tensor_copy(z(GAT)[0:16, :], GTMP[0:16, :]).then_inc(me.signals(gla_to_pe), 1)

            def gate_logits():
                bank = take()
                dve.wait_ge(*me.last)
                nc.vector.tensor_copy(z(LA), bank).then_inc(me.signals(acc_free_dve), 1)
                dve.wait_ge(*me.last)
                stt(z(TMP), z(LA), -1.0, z(LA), ALU.mult, ALU.max).then_inc(me.signals(gla_to_act), 1)
                dve.wait_ge(*me.last)
                ts(z(LA), z(LA), 0.0, None, ALU.min).then_inc(me.signals(dve_step), 1)

            def log_decays():
                dve.wait_ge(gla_act, me.after(gla_act))
                dve.wait_ge(*me.last)
                tt(z(LA), z(LA), z(TMP), ALU.subtract).then_inc(me.signals(gla_to_pe), 1)
                me.emptied_by("act")

            def decays():
                dve.wait_ge(acc_free_act, me.emptied["act"])
                b = z(BT)
                dve.wait_ge(*me.last)
                nc.vector.memset(BREF[:, 0:1], 0.0).then_inc(me.signals(dve_step), 1)
                dve.wait_ge(*me.last)
                nc.vector.tensor_copy(BREF[:, 1:32], b[:, 15:511:16]).then_inc(me.signals(dve_step), 1)
                dve.wait_ge(*me.last)
                tt(z(Q2).rearrange("p (a i) -> p a i", a=32), b.rearrange("p (a i) -> p a i", a=32),
                    BREF.unsqueeze(2).broadcast_to([P, 32, 16]), ALU.subtract) \
                    .then_inc(me.signals(gla_to_pool), 1)
                k0 = 0
                for qb in range(1, NB):
                    end = b[:, qb * B - 1:qb * B]
                    dve.wait_ge(*me.last)
                    ts(z(Q1)[:, qb * B:qb * B + B], b[:, qb * B:qb * B + B], end, None, ALU.subtract) \
                        .then_inc(me.signals(dve_step), 1)
                    dve.wait_ge(*me.last)
                    ts(GK1[:, k0:k0 + qb * B], b[:, 0:qb * B], end, -1.0, ALU.subtract, ALU.mult) \
                        .then_inc(me.signals(gla_to_act if qb == NB - 1 else dve_step), 1)
                    k0 += qb * B

            def decayed():
                dve.wait_ge(gla_act, me.after(gla_act))
                dve.wait_ge(*me.last)
                tt(z(Q1)[:, B:T], z(Q1)[:, B:T], z(GQ)[:, B:T], ALU.mult).then_inc(me.signals(dve_step), 1)
                dve.wait_ge(*me.last)
                tt(z(Q2), z(Q2), z(GQ), ALU.mult).then_inc(me.signals(dve_step), 1)
                k0 = 0
                for qb in range(1, NB):
                    dve.wait_ge(*me.last)
                    tt(GK1[:, k0:k0 + qb * B], GK1[:, k0:k0 + qb * B], z(GK)[:, 0:qb * B], ALU.mult) \
                        .then_inc(me.signals(gla_to_pool if qb == NB - 1 else dve_step), 1)
                    k0 += qb * B

            def within(x):
                return x.rearrange("p (a c) -> p c a", a=8).unsqueeze(3).broadcast_to([P, 16, 8, 16])

            def over(x):
                return x.rearrange("p (a j) -> p a j", a=8).unsqueeze(1).broadcast_to([P, 16, 8, 16])

            def exponents(qb):
                prod, bb = GPROD[qb % 2].rearrange("p c (a j) -> p c a j", a=8), z(BT)[:, qb * B:qb * B + B]
                dve.wait_ge(*me.last)
                tt(prod, within(bb), over(bb), ALU.subtract).then_inc(me.signals(dve_step), 1)
                dve.wait_ge(*me.last)
                ts(GPROD[qb % 2], GPROD[qb % 2], 0.0, None, ALU.min).then_inc(me.signals(gla_to_act), 1)

            def products_within(qb):
                prod = GPROD[qb % 2].rearrange("p c (a j) -> p c a j", a=8)
                qq, kk = (z(t)[:, qb * B:qb * B + B] for t in (GQ, GK))
                dve.wait_ge(gla_act, me.after(gla_act))
                tt(prod, prod, over(kk), ALU.mult).then_inc(me.signals(dve_step), 1)
                dve.wait_ge(*me.last)
                tt(prod, prod, within(qq), ALU.mult).then_inc(me.signals(gla_to_pe), 1)

            def weights(qb):
                for jb in range(qb):
                    me.seg += 1
                    dve.wait_ge(scores_ready, me.seg)
                    nc.vector.tensor_copy(GS[:, jb, :], PS[:, 2 + (me.seg - 1) % 2, :]) \
                        .then_inc(me.signals(scores_free), 1)
                own = GS[:, qb, :].rearrange("p (h i) -> p h i", h=4)
                me.seg += 1
                dve.wait_ge(scores_ready, me.seg)
                tt(own, PS[:, 2 + (me.seg - 1) % 2, :].rearrange("p (h i) -> p h i", h=4),
                    SUBM[:, 0, :].unsqueeze(1).broadcast_to([P, 4, B]), ALU.mult) \
                    .then_inc(me.signals(scores_free), 1)
                me.seg += 1
                dve.wait_ge(scores_ready, me.seg)
                near = PS[:, 2 + (me.seg - 1) % 2, 0:64].rearrange("p (c h) -> p h c", h=4)
                dve.wait_ge(*me.last)
                for h in range(4):
                    tt(GTMP[:, h * B:h * B + B].rearrange("p (a c) -> p a c", a=8),
                        SUBM[:, 1, :].rearrange("p (a c) -> p a c", a=8), near[:, h, :].unsqueeze(1).broadcast_to([P, 8, 16]), ALU.mult) \
                        .then_inc(me.signals(scores_free if h == 3 else dve_step), 1)
                dve.wait_ge(*me.last)
                tt(GS[:, qb, :], GS[:, qb, :], GTMP, ALU.add).then_inc(me.signals(gla_to_pe), 1)

            def gla():
                for qb in range(NB):
                    if qb + 1 < NB:
                        exponents(qb + 1)
                    if qb:
                        dve.wait_ge(values_done, vals[0])
                    weights(qb)
                    vals[0] += 1
                    if qb + 1 < NB:
                        products_within(qb + 1)
                dve.wait_ge(values_done, vals[0])

            def scaled(tiles, gains, signal=normed):
                dve.wait_ge(rstd_ready, me.after(rstd_ready))
                for n, t in enumerate(tiles):
                    dve.wait_ge(*me.last)
                    stt(t, t, gains[n], RS, ALU.mult, ALU.mult).then_inc(me.signals(signal), 1)

            def head_scaled(tiles, gain, gates=None):
                for _ in tiles:
                    me.emptied_by("act")
                dve.wait_ge(rstd_ready, me.after(rstd_ready))
                for n, t in enumerate(tiles):
                    if gain is None:
                        tt(t, t, RS4[:, n, :], ALU.mult).then_inc(me.signals(dve_step), 1)
                    else:
                        stt(t, t, gain, RS4[:, n, :], ALU.mult, ALU.mult) \
                            .then_inc(me.signals(dve_step if gates else normed), 1)
                if gates:
                    dve.wait_ge(*me.last)
                    for t, g in zip(tiles, gates):
                        tt(t, t, g, ALU.mult).then_inc(me.signals(normed), 1)

            def angles():
                whole, parts = 12582912.0, (6.28125, 0.0019350051879882812, 3.01991605e-7)
                dve.wait_ge(*me.last)
                nc.vector.tensor_copy(z(29), z(22).bitcast(I32)).then_inc(me.signals(dve_step), 1)
                for n in range(2):
                    r, c, turns = z(23 + 3 * n), z(24 + 3 * n), z(25 + 3 * n)
                    dve.wait_ge(*me.last)
                    ts(r, z(29), FREQ[:, n:n + 1], None, ALU.mult).then_inc(me.signals(dve_step), 1)
                    dve.wait_ge(*me.last)
                    ts(turns, r, float(1 / (2 * np.pi)), whole, ALU.mult, ALU.add).then_inc(me.signals(dve_step), 1)
                    dve.wait_ge(*me.last)
                    ts(turns, turns, whole, None, ALU.subtract).then_inc(me.signals(dve_step), 1)
                    for part in parts:
                        dve.wait_ge(*me.last)
                        stt(r, turns, -part, r, ALU.mult, ALU.add).then_inc(me.signals(dve_step), 1)
                    dve.wait_ge(*me.last)
                    ts(r, r, 3.1415925, -3.1415925, ALU.min, ALU.max).then_inc(me.signals(dve_step), 1)
                    dve.wait_ge(*me.last)
                    stt(c, r, -1.0, r, ALU.mult, ALU.min) \
                        .then_inc(me.signals(dve_step), 1)
                    dve.wait_ge(*me.last)
                    ts(c, c, float(np.pi / 2), None, ALU.add).then_inc(me.signals(side_dve if n else dve_step), 1)

            for n_met, (s, l) in enumerate(stages, 1):
                me.begins(4 if s in LINEAR or s == "even_sub" else 2)
                if s == "setup":
                    dve.wait_ge(first_in, FIRST_IN)
                    nc.vector.memset(EPS6, 1e-6).then_inc(me.signals(dve_step), 1)
                    dve.wait_ge(*me.last)
                    nc.vector.memset(EPS5, 1e-5).then_inc(me.signals(dve_step), 1)
                    dve.wait_ge(*me.last)
                    nc.vector.memset(TABLE[32:33, :], NEG).then_inc(me.signals(side_dve), 1)
                    for c, w in HOT_CUTS:
                        bank = take()
                        dve.wait_ge(*me.last)
                        nc.vector.tensor_copy(VECS_SB[:, c:c + w], bank[0:16, 0:w]) \
                            .then_inc(me.signals(acc_free_dve), 1)
                elif s == "prenorm":
                    dve.wait_ge(*me.last)
                    stt(GA, MOD[l][:, 8:16], 1.0, PREG[:, l, :], ALU.add, ALU.mult).then_inc(me.signals(dve_step), 1)
                    dve.wait_ge(*me.last)
                    tt(GB, MOD[l][:, 16:24], POSTG[:, l, :], ALU.mult).then_inc(me.signals(dve_step), 1)
                    if l == 0:
                        angles()
                    me.emptied_by("act")
                    dve.wait_ge(rstd_ready, me.after(rstd_ready))
                    for k in range(KD):
                        dve.wait_ge(*me.last)
                        stt(H[:, k, :], X[:, k, :], GA[:, k:k + 1], RS, ALU.mult, ALU.mult) \
                            .then_inc(me.signals(normed), 1)
                    if l == 0:
                        dve.wait_ge(table_out, 16)
                elif s == "postnorm":
                    me.emptied_by("act")
                    scaled([z(k) for k in range(KD)], [GB[:, k:k + 1] for k in range(KD)], post_scaled)
                    dve.wait_ge(post_added, KD * (l + 1))
                elif s == "ln":
                    bank = take()
                    for k in range(KD):
                        dve.wait_ge(*me.last)
                        tt(X[:, k, :], X[:, k, :], bank, ALU.subtract).then_inc(me.signals(normed), 1)
                    dve.wait_ge(*me.last)
                    nc.vector.tensor_copy(TINY[:, 121:122], bank[:, 0:1]).then_inc(me.signals(acc_free_dve), 1)
                    me.emptied_by("act")
                    scaled([X[:, k, :] for k in range(KD)], [LNG[:, l, k:k + 1] for k in range(KD)])
                elif s in ("swa", "even_mix", "odd_mix"):
                    if s == "swa" and l == 0:
                        dve.wait_ge(const_in, N_CONST[0])
                    if s != "swa":
                        dve.wait_ge(bias_in, BIAS_IN[s])
                    for steps, depth in steps_of(s, l):
                        attention(steps, depth)
                elif s == "ret":
                    gate_input()
                    for k in range(4):
                        tt(H[:, k, :], H[:, k, :], z(AG + k), ALU.mult).then_inc(me.signals(dve_step), 1)
                    gate_logits()
                    retention([0])
                    log_decays()
                    retention([1])
                    decays()
                    retention([2])
                    exponents(0)
                    retention([3])
                    decayed()
                    products_within(0)
                    head_scaled([H[:, 4 + t, :] for t in range(2)], None, [z(RG + t) for t in range(2)])
                elif s == "gla":
                    gla()
                    head_scaled([H[:, 6 + t, :] for t in range(2)], GLAG[:, l:l + 1], [z(GG + t) for t in range(2)])
                elif s == "even_sub":
                    head_scaled([H[:, t, :] for t in range(4)], SUBG)
                elif s == "odd_norms":
                    for t, n, g in ((CQ, 3, QG), (CKV, 2, KVG)):
                        me.emptied_by("act")
                        scaled([z(t + i) for i in range(n)], [g[:, i:i + 1] for i in range(n)])
                elif s == "store":
                    for _ in range(8):
                        me.emptied_by("act")
                else:
                    if s == "mod":
                        me.emptied_by("act")
                        nc.vector.memset(ONE, 1.0).then_inc(me.signals(one_set), 1)
                        dve.wait_ge(c_ready, 1)
                        made = modulation(("mod", 0))
                        for i, m in enumerate(made):
                            if i >= 3:
                                if i - 3 == AHEAD:
                                    for _ in range(N_TURNS):
                                        me.emptied_by("act")
                                modulate(made[i - 3][0])
                            if m[0]["maker"] == "dve":
                                products(*m[:3])
                        for m in made[-3:]:
                            modulate(m[0])
                    if s == "up":
                        dve.wait_ge(*me.last)
                        nc.vector.memset(GPAD[:, :, 0:2], 0.0).then_inc(me.signals(dve_step), 1)
                    if s in ("odd_in", "odd_up"):
                        dve.wait_ge(bias_in, BIAS_IN[s])
                    for k, t in enumerate(inputs_of(s)):
                        dve.wait_ge(hi_ready, me.after(hi_ready))
                        tt(LO[:, k, :], t, HI[:, k, :], ALU.subtract).then_inc(me.signals(lo_ready), 1)
                    if s != "mod":
                        linear(jobs_of(s, l), l)
                if s == "even_in":
                    lp = LAMP.rearrange("p (a b d) -> p a b d", a=2, b=2)
                    prod = RT[:, 0:128].rearrange("p (a d) -> p a d", a=2)
                    dve.wait_ge(*me.last)
                    tt(prod, lp[:, :, 0, :], lp[:, :, 1, :], ALU.mult).then_inc(me.signals(dve_step), 1)
                    dve.wait_ge(*me.last)
                    nc.vector.tensor_reduce(LTMP[:, 0:2], prod, AX.X, ALU.add).then_inc(me.signals(side_dve), 1)
                    dve.wait_ge(side_act, me.after(side_act))
                    dve.wait_ge(*me.last)
                    tt(LAM, LTMP[:, 3:4], LTMP[:, 2:3], ALU.subtract).then_inc(me.signals(dve_step), 1)
                    dve.wait_ge(*me.last)
                    ts(LAM, LAM, LAM_INIT, None, ALU.subtract).then_inc(me.signals(dve_step), 1)
                    dve.wait_ge(*me.last)
                    ts(SUBG, SUBG, 1.0 - LAM_INIT, None, ALU.mult).then_inc(me.signals(dve_step), 1)
                dve.wait_ge(*me.last)
                dve.sem_inc(dve_met, 1)
                dve.wait_ge(pe_met, n_met)
                dve.wait_ge(act_met, n_met)


_INS = ["x", "c", "positions", "w_mod", "b_mod", "pre_norm_gain", "post_norm_gain", "w_in", "attn_sinks", "gla_gate_w",
        "gla_gate_b", "gla_norm_gain", "w_out", "rel_bias_2", "ev_w_in_2", "ev_w_out_2", "ev_lambda_2", "ev_subln_2",
        "od_w_in_2", "od_w_out_2", "od_cmp_pe_2", "od_cmp_w1_2", "od_cmp_w2_2", "od_q_norm_2", "od_kv_norm_2", "od_w_uq_2",
        "od_w_uk_2", "od_w_uv_2", "ffn_w_up_2", "ffn_conv_w_2", "ffn_conv_b_2", "ffn_w_down_2", "ln_g_2", "ln_b_2"]


def kernel(**inputs):
    import concourse.bacc as _bacc
    from concourse.bass_utils import run_bass_kernel_spmd as _run

    nc = _bacc.Bacc("TRN2", target_bir_lowering=False, num_devices=1)
    arrays, io, cst = {}, {}, {}
    for name in _INS:
        a = np.ascontiguousarray(inputs[name])
        arrays["in_" + name] = a
        io[name] = nc.dram_tensor("in_" + name, a.shape, mybir.dt.from_np(a.dtype), kind="ExternalInput").ap()
    for name, a in constants().items():
        arrays["cst_" + name] = a
        cst[name] = nc.dram_tensor("cst_" + name, a.shape, F32, kind="ExternalInput").ap()
    out = nc.dram_tensor("out", [T, D], F32, kind="ExternalOutput").ap()
    build(nc, io, cst, out)
    r = _run(nc, [arrays], core_ids=[0])
    return r.results[0]["out"].reshape(1, T, D)
```
